# Optimizing a Trainium2 kernel written in Bass

```python
import math
import jax, jax.numpy as jnp
from jax import lax
import numpy as np

D_MODEL = 1024
BATCH = 1
SEQ = 512
DEPTH = 2

N_META = 16
D_FF = 2816
NORM_EPS = 1e-6
NEG_INF = -1e30
SWA_Q_HEADS = 8
SWA_KV_HEADS = 2
SWA_HEAD_DIM = 64
SWA_WINDOW = 128
SWA_BLOCK = 128
REL_BUCKETS = 32
REL_MAX_DIST = 128
SWA_Q_DIM = SWA_Q_HEADS * SWA_HEAD_DIM
SWA_KV_DIM = SWA_KV_HEADS * SWA_HEAD_DIM
DN_HEADS = 4
DN_HEAD_DIM = 128
DN_DIM = DN_HEADS * DN_HEAD_DIM
DN_CONV = 4
DN_CHUNK = 64
GLA_HEADS = 4
GLA_KEY_DIM = D_MODEL // 2
GLA_VAL_DIM = D_MODEL
GLA_GATE_RANK = 16
GLA_GATE_NORM = 16.0
GLA_CHUNK = 64
N_EVEN = (DEPTH + 1) // 2
N_ODD = DEPTH // 2
EVEN_IN_SIZES = (SWA_Q_DIM, SWA_KV_DIM, SWA_KV_DIM, DN_DIM, DN_DIM, DN_DIM, DN_DIM, DN_HEADS, DN_HEADS)
EVEN_IN_DIM = sum(EVEN_IN_SIZES)
EVEN_MIX_DIM = SWA_Q_DIM + DN_DIM
ODD_IN_SIZES = (GLA_KEY_DIM, GLA_KEY_DIM, GLA_VAL_DIM, GLA_VAL_DIM, GLA_GATE_RANK)
ODD_IN_DIM = sum(ODD_IN_SIZES)

kernel_name = "hybrid_swa_deltanet_gla_macaron"

def _split(t, sizes):
    idx = np.cumsum(sizes)[:-1].tolist()
    return jnp.split(t, idx, axis=-1)

def rms_norm(x, w):
    x32 = x.astype(jnp.float32)
    y = x32 * lax.rsqrt(jnp.mean(x32 * x32, axis=-1, keepdims=True) + NORM_EPS)
    return (y * w.astype(jnp.float32)).astype(x.dtype)

def l2_norm(x):
    return x * lax.rsqrt(jnp.sum(x * x, axis=-1, keepdims=True) + 1e-6)

def swiglu(x, w_gate, w_up, w_down):
    return (jax.nn.silu(x @ w_gate) * (x @ w_up)) @ w_down

def causal_depthwise_conv(x, w):
    k = w.shape[0]
    return lax.conv_general_dilated(x, w[:, None, :].astype(x.dtype), window_strides=(1,),
                                    padding=[(k - 1, 0)], dimension_numbers=('NWC', 'WIO', 'NWC'),
                                    feature_group_count=x.shape[-1])

def t5_bucket(rel):
    n = jnp.maximum(rel, 0)
    max_exact = REL_BUCKETS // 2
    n_f = jnp.maximum(n, 1).astype(jnp.float32)
    large = max_exact + (jnp.log(n_f / max_exact) / math.log(REL_MAX_DIST / max_exact)
                         * (REL_BUCKETS - max_exact)).astype(jnp.int32)
    large = jnp.minimum(large, REL_BUCKETS - 1)
    return jnp.where(n < max_exact, n, large)

def to_chunks(t, chunk):
    pad = chunk - N_META
    t = jnp.pad(t, [(0, 0), (pad, 0)] + [(0, 0)] * (t.ndim - 2))
    b, lp = t.shape[:2]
    t = t.reshape(b, lp // chunk, chunk, *t.shape[2:])
    return jnp.moveaxis(t, 3, 1)

def from_chunks(t, chunk):
    t = jnp.moveaxis(t, 1, 3)
    b, n, c = t.shape[:3]
    return t.reshape(b, n * c, *t.shape[3:])[:, chunk - N_META:]

def _chunk_first(t):
    return jnp.moveaxis(t, 2, 0)

def sliding_window_attention(q, k, v, sinks, rel_table):
    f32 = jnp.float32
    b, l = q.shape[:2]
    g = SWA_Q_HEADS // SWA_KV_HEADS
    dh = SWA_HEAD_DIM
    pad = SWA_BLOCK - N_META
    lp = l + pad
    nb = lp // SWA_BLOCK
    padw = ((0, 0), (pad, 0), (0, 0), (0, 0))
    qb = jnp.pad(q.astype(f32), padw).reshape(b, nb, SWA_BLOCK, SWA_KV_HEADS, g, dh)
    kb = jnp.pad(k.astype(f32), padw).reshape(b, nb, SWA_BLOCK, SWA_KV_HEADS, dh)
    vb = jnp.pad(v.astype(f32), padw).reshape(b, nb, SWA_BLOCK, SWA_KV_HEADS, dh)
    prev = ((0, 0), (1, 0), (0, 0), (0, 0), (0, 0))
    k_band = jnp.concatenate([jnp.pad(kb[:, :-1], prev), kb], axis=2)
    v_band = jnp.concatenate([jnp.pad(vb[:, :-1], prev), vb], axis=2)
    k_meta = k[:, :N_META].astype(f32)
    v_meta = v[:, :N_META].astype(f32)
    scale = dh ** -0.5
    s_band = jnp.einsum('bnqhgd,bnkhd->bhgnqk', qb, k_band) * scale
    s_meta = jnp.einsum('bnqhgd,bmhd->bhgnqm', qb, k_meta) * scale
    blk = jnp.arange(nb)[:, None]
    pos_q = blk * SWA_BLOCK + jnp.arange(SWA_BLOCK)[None, :] - pad
    pos_kb = blk * SWA_BLOCK + jnp.arange(2 * SWA_BLOCK)[None, :] - SWA_BLOCK - pad
    rel_b = pos_q[:, :, None] - pos_kb[:, None, :]
    mask_b = (pos_kb[:, None, :] >= N_META) & (rel_b >= 0) & (rel_b < SWA_WINDOW)
    rel_m = pos_q[:, :, None] - jnp.arange(N_META)[None, None, :]
    mask_m = rel_m >= 0
    table = rel_table.astype(f32)

    def rel_bias(rel):
        bias = table[t5_bucket(rel)]
        return jnp.moveaxis(bias, -1, 0).reshape(SWA_KV_HEADS, g, *rel.shape)

    s_band = jnp.where(mask_b, s_band + rel_bias(rel_b), NEG_INF)
    s_meta = jnp.where(mask_m, s_meta + rel_bias(rel_m), NEG_INF)
    sink = jnp.broadcast_to(sinks.astype(f32).reshape(SWA_KV_HEADS, g, 1, 1, 1),
                            (b, SWA_KV_HEADS, g, nb, SWA_BLOCK, 1))
    p = jax.nn.softmax(jnp.concatenate([s_band, s_meta, sink], axis=-1), axis=-1)
    nk = 2 * SWA_BLOCK
    o = (jnp.einsum('bhgnqk,bnkhd->bnqhgd', p[..., :nk], v_band)
         + jnp.einsum('bhgnqm,bmhd->bnqhgd', p[..., nk:nk + N_META], v_meta))
    return o.reshape(b, lp, SWA_Q_DIM)[:, pad:]

def chunk_gated_delta_rule(q, k, v, g, beta):
    c = q.shape[-2]
    tri_incl = jnp.tril(jnp.ones((c, c), bool))
    tri_strict = jnp.tril(jnp.ones((c, c), bool), -1)
    gc = jnp.cumsum(g, axis=-1)
    diff = gc[..., :, None] - gc[..., None, :]
    gamma = jnp.where(tri_incl, jnp.exp(jnp.where(tri_incl, diff, 0.0)), 0.0)
    k_beta = k * beta[..., None]
    v_beta = v * beta[..., None]
    a_strict = jnp.where(tri_strict, jnp.einsum('bhnid,bhnjd->bhnij', k_beta, k) * gamma, 0.0)
    m = a_strict + jnp.eye(c, dtype=jnp.float32)
    u = lax.linalg.triangular_solve(m, v_beta, left_side=True, lower=True, unit_diagonal=True)
    w = lax.linalg.triangular_solve(m, k_beta * jnp.exp(gc)[..., None], left_side=True,
                                    lower=True, unit_diagonal=True)
    attn = jnp.einsum('bhnid,bhnjd->bhnij', q, k) * gamma
    q_dec = q * jnp.exp(gc)[..., None]
    k_dec = k * jnp.exp(gc[..., -1:] - gc)[..., None]
    g_last = jnp.exp(gc[..., -1])

    def step(s, xs):
        attn_n, u_n, w_n, qd_n, kd_n, gl_n = xs
        v_new = u_n - jnp.einsum('bhik,bhkv->bhiv', w_n, s)
        o = jnp.einsum('bhik,bhkv->bhiv', qd_n, s) + jnp.einsum('bhij,bhjv->bhiv', attn_n, v_new)
        s = s * gl_n[..., None, None] + jnp.einsum('bhik,bhiv->bhkv', kd_n, v_new)
        return s, o

    bsz, h, _, _, dk = q.shape
    s0 = jnp.zeros((bsz, h, dk, v.shape[-1]), jnp.float32)
    xs = tuple(_chunk_first(t) for t in (attn, u, w, q_dec, k_dec, g_last))
    _, o = lax.scan(step, s0, xs)
    return jnp.moveaxis(o, 0, 2)

def chunk_gla(q, k, v, glog):
    c = q.shape[-2]
    tri = jnp.tril(jnp.ones((c, c), bool))
    bcum = jnp.cumsum(glog, axis=-2)
    q_dec = q * jnp.exp(bcum)
    attn = jnp.where(tri, jnp.einsum('bhnik,bhnjk->bhnij', q_dec, k * jnp.exp(-bcum)), 0.0)
    o_intra = jnp.einsum('bhnij,bhnjv->bhniv', attn, v)
    b_last = bcum[..., -1:, :]
    k_dec = k * jnp.exp(b_last - bcum)
    decay = jnp.exp(b_last[..., 0, :])

    def step(s, xs):
        qd, kd, vv, dl = xs
        o = jnp.einsum('bhik,bhkv->bhiv', qd, s)
        s = s * dl[..., :, None] + jnp.einsum('bhik,bhiv->bhkv', kd, vv)
        return s, o

    bsz, h, _, _, dk = q.shape
    s0 = jnp.zeros((bsz, h, dk, v.shape[-1]), jnp.float32)
    _, o_inter = lax.scan(step, s0, tuple(_chunk_first(t) for t in (q_dec, k_dec, v, decay)))
    return o_intra + jnp.moveaxis(o_inter, 0, 2)

def gated_deltanet(q, k, v, a, bgate, z, conv_w, a_log, dt_bias, norm_w):
    f32 = jnp.float32
    bsz, l, _ = q.shape
    hd = (bsz, l, DN_HEADS, DN_HEAD_DIM)
    qkv = jax.nn.silu(causal_depthwise_conv(jnp.concatenate([q, k, v], axis=-1), conv_w))
    q, k, v = _split(qkv, (DN_DIM, DN_DIM, DN_DIM))
    q = l2_norm(q.reshape(hd).astype(f32)) * DN_HEAD_DIM ** -0.5
    k = l2_norm(k.reshape(hd).astype(f32))
    v = v.reshape(hd).astype(f32)
    beta = jax.nn.sigmoid(bgate.astype(f32))
    g = -jnp.exp(a_log.astype(f32)) * jax.nn.softplus(a.astype(f32) + dt_bias.astype(f32))
    o = chunk_gated_delta_rule(to_chunks(q, DN_CHUNK), to_chunks(k, DN_CHUNK), to_chunks(v, DN_CHUNK),
                               to_chunks(g, DN_CHUNK), to_chunks(beta, DN_CHUNK))
    o = from_chunks(o, DN_CHUNK)
    o = rms_norm(o, norm_w) * jax.nn.silu(z.reshape(hd).astype(f32))
    return o.reshape(bsz, l, DN_DIM).astype(z.dtype)

def even_mixer(h, w_in, conv_w, sinks, a_log, dt_bias, dn_norm_w, w_out, rel_table):
    bsz, l, _ = h.shape
    qa, ka, va, qb, kb, vb, zb, bb, ab = _split(h @ w_in, EVEN_IN_SIZES)
    o_a = sliding_window_attention(qa.reshape(bsz, l, SWA_Q_HEADS, SWA_HEAD_DIM),
                                   ka.reshape(bsz, l, SWA_KV_HEADS, SWA_HEAD_DIM),
                                   va.reshape(bsz, l, SWA_KV_HEADS, SWA_HEAD_DIM), sinks, rel_table)
    o_b = gated_deltanet(qb, kb, vb, ab, bb, zb, conv_w, a_log, dt_bias, dn_norm_w)
    return jnp.concatenate([o_a.astype(h.dtype), o_b.astype(h.dtype)], axis=-1) @ w_out

def odd_mixer(h, w_in, w_gate_up, b_gate, norm_w, w_out):
    f32 = jnp.float32
    bsz, l, _ = h.shape
    dk = GLA_KEY_DIM // GLA_HEADS
    dv = GLA_VAL_DIM // GLA_HEADS
    q, k, v, g, gk_low = _split(h @ w_in, ODD_IN_SIZES)
    glog = jax.nn.log_sigmoid((gk_low @ w_gate_up + b_gate).astype(f32)) / GLA_GATE_NORM
    q = q.reshape(bsz, l, GLA_HEADS, dk).astype(f32) * dk ** -0.5
    k = k.reshape(bsz, l, GLA_HEADS, dk).astype(f32)
    v = v.reshape(bsz, l, GLA_HEADS, dv).astype(f32)
    glog = glog.reshape(bsz, l, GLA_HEADS, dk)
    o = chunk_gla(to_chunks(q, GLA_CHUNK), to_chunks(k, GLA_CHUNK), to_chunks(v, GLA_CHUNK),
                  to_chunks(glog, GLA_CHUNK))
    o = from_chunks(o, GLA_CHUNK)
    o = rms_norm(o, norm_w) * jax.nn.silu(g.reshape(bsz, l, GLA_HEADS, dv).astype(f32))
    return o.reshape(bsz, l, GLA_VAL_DIM).astype(h.dtype) @ w_out

def setup_inputs(seed: int = 0) -> dict:
    key = jax.random.key(seed)
    ks = jax.random.split(key, 24)
    f32 = jnp.float32

    def nrm(k, shape, fan_in):
        return jax.random.normal(k, shape, f32) * fan_in ** -0.5

    dt = jnp.exp(jax.random.uniform(ks[10], (N_EVEN, DN_HEADS), f32) * (math.log(0.1) - math.log(0.001))
                 + math.log(0.001))
    return {
        "x": jax.random.normal(ks[0], (BATCH, SEQ, D_MODEL), f32),
        "meta_tokens": jax.random.normal(ks[1], (N_META, D_MODEL), f32),
        "norm_w": 1.0 + 0.02 * jax.random.normal(ks[2], (DEPTH, 6, D_MODEL), f32),
        "ffn_w_gate": nrm(ks[3], (DEPTH, 2, D_MODEL, D_FF), D_MODEL),
        "ffn_w_up": nrm(ks[4], (DEPTH, 2, D_MODEL, D_FF), D_MODEL),
        "ffn_w_down": nrm(ks[5], (DEPTH, 2, D_FF, D_MODEL), D_FF),
        "rel_bias_table": 0.5 * jax.random.normal(ks[6], (REL_BUCKETS, SWA_Q_HEADS), f32),
        "even_w_in": nrm(ks[7], (N_EVEN, D_MODEL, EVEN_IN_DIM), D_MODEL),
        "even_conv_w": nrm(ks[8], (N_EVEN, DN_CONV, 3 * DN_DIM), DN_CONV),
        "swa_sinks": jax.random.normal(ks[9], (N_EVEN, SWA_Q_HEADS), f32),
        "dn_a_log": jnp.log(jax.random.uniform(ks[11], (N_EVEN, DN_HEADS), f32, 1.0, 16.0)),
        "dn_dt_bias": dt + jnp.log(-jnp.expm1(-dt)),
        "dn_norm_w": 1.0 + 0.02 * jax.random.normal(ks[12], (N_EVEN, DN_HEAD_DIM), f32),
        "even_w_out": nrm(ks[13], (N_EVEN, EVEN_MIX_DIM, D_MODEL), EVEN_MIX_DIM),
        "odd_w_in": nrm(ks[14], (N_ODD, D_MODEL, ODD_IN_DIM), D_MODEL),
        "gla_w_gate_up": nrm(ks[15], (N_ODD, GLA_GATE_RANK, GLA_KEY_DIM), GLA_GATE_RANK),
        "gla_b_gate": 0.1 * jax.random.normal(ks[16], (N_ODD, GLA_KEY_DIM), f32),
        "gla_norm_w": 1.0 + 0.02 * jax.random.normal(ks[17], (N_ODD, GLA_VAL_DIM // GLA_HEADS), f32),
        "odd_w_out": nrm(ks[18], (N_ODD, GLA_VAL_DIM, D_MODEL), GLA_VAL_DIM),
    }

def reference(x, meta_tokens, norm_w, ffn_w_gate, ffn_w_up, ffn_w_down, rel_bias_table,
              even_w_in, even_conv_w, swa_sinks, dn_a_log, dn_dt_bias, dn_norm_w, even_w_out,
              odd_w_in, gla_w_gate_up, gla_b_gate, gla_norm_w, odd_w_out):
    bsz = x.shape[0]
    meta = jnp.broadcast_to(meta_tokens[None].astype(x.dtype), (bsz, N_META, x.shape[-1]))
    h = jnp.concatenate([meta, x], axis=1)
    for layer in range(DEPTH):
        nw = norm_w[layer]
        f = swiglu(rms_norm(h, nw[0]), ffn_w_gate[layer, 0], ffn_w_up[layer, 0], ffn_w_down[layer, 0])
        h = h + 0.5 * rms_norm(f, nw[1])
        hn = rms_norm(h, nw[2])
        if layer % 2 == 0:
            i = layer // 2
            mix = even_mixer(hn, even_w_in[i], even_conv_w[i], swa_sinks[i], dn_a_log[i], dn_dt_bias[i],
                             dn_norm_w[i], even_w_out[i], rel_bias_table)
        else:
            i = layer // 2
            mix = odd_mixer(hn, odd_w_in[i], gla_w_gate_up[i], gla_b_gate[i], gla_norm_w[i], odd_w_out[i])
        h = h + rms_norm(mix, nw[3])
        f = swiglu(rms_norm(h, nw[4]), ffn_w_gate[layer, 1], ffn_w_up[layer, 1], ffn_w_down[layer, 1])
        h = h + 0.5 * rms_norm(f, nw[5])
    return h[:, N_META:]


_drawn_inputs = setup_inputs


def setup_inputs(seed=0):
    import zlib

    import numpy as np

    out = dict(_drawn_inputs(seed))
    spreads = {}
    factors = {'swa_sinks': 4.274, 'dn_norm_w': 3.105, 'gla_norm_w': 5.699}
    for name, (base, spread) in spreads.items():
        noise = np.random.default_rng([zlib.crc32(name.encode()), seed]).standard_normal(out[name].shape)
        drawn = base * np.exp(spread * noise) if base else spread * noise
        out[name] = __import__('jax').numpy.asarray(drawn.astype(out[name].dtype))
    for name, factor in factors.items():
        out[name] = (out[name] * factor).astype(out[name].dtype)
    return out
```

```python
from contextlib import ExitStack

import numpy as np

import concourse.bass as bass
from concourse import mybir

ACT = mybir.ActivationFunctionType
ALU = mybir.AluOpType
AX = mybir.AxisListType
F32 = mybir.dt.float32
F32R = mybir.dt.float32r

P = 128
META = 16
SEQ = 512
TOK = META + SEQ
D = 1024
DT = D // P
FF = 2816
FT = FF // P
FH = FT // 2
EPS = 1e-6
MASKED = -1e30
BUCKETS = 32
MAX_DIST = 128
QH, KVH, HD = 8, 2, 64
GRP = QH // KVH
NBLK = SEQ // P
DH = 4
CONV = 4
GH = 4
CH = 64
RING = 4
AHEAD = 3
EVEN_TILES = 22
EVEN_GATES = 2 * DH
ODD_TILES = 24
RANK = 16
DN_DIM = 128
CONST_LOADS = 11
VEC_ROWS = CONV * 3 * DH + 4 + 2 + 1
HALF = TOK // 2
FULL = "full"
TAIL = "tail"

BAND_N = 3 * P - 1
META_N = P + META - 1
SELF_N = 2 * META - 1
V_BAND, V_NEAR, V_FAR, V_SELF = 0, BAND_N, BAND_N + META_N, BAND_N + 2 * META_N
V_ALL = V_SELF + SELF_N

LEVELS = 7
C_ID, C_FLIP, C_UP, C_ADD, C_LVL = 0, P, 2 * P, 3 * P, 4 * P
C_GLA = C_LVL + LEVELS * P
C_ALL = C_GLA + P


def shape_constants():
    j = np.arange(P)[:, None]
    i = np.arange(P)[None, :]
    masks = np.zeros((P, C_ALL), np.float32)
    masks[:, C_ID:C_ID + P] = i == j
    masks[:, C_FLIP:C_FLIP + P] = i + j == P - 1
    masks[:, C_UP:C_UP + P] = j <= i
    masks[:, C_ADD:C_ADD + P] = np.where(j <= i, 0.0, MASKED)
    for n in range(LEVELS):
        s = 1 << n
        level = (i // (2 * s) == j // (2 * s)) & ((i // s) % 2 == 1) & ((j // s) % 2 == 0)
        masks[:, C_LVL + n * P:C_LVL + (n + 1) * P] = level
    masks[:, C_GLA:C_GLA + P] = (j <= i) & (i // CH == j // CH)

    def bucket(n):
        exact = BUCKETS // 2
        far = np.log(np.maximum(n, 1).astype(np.float32) / np.float32(exact)) / np.float32(np.log(MAX_DIST / exact))
        far = np.minimum(exact + (far * np.float32(BUCKETS - exact)).astype(np.int32), BUCKETS - 1)
        return np.where(n < exact, n, far)

    hot = np.zeros((BUCKETS + 1, V_ALL), np.float32)

    def put(first, rel, valid):
        cols = first + np.arange(len(rel))
        hot[np.where(valid, bucket(np.maximum(rel, 0)), BUCKETS), cols] = 1.0

    rel = 2 * P - 1 - np.arange(BAND_N)
    put(V_BAND, rel, (rel >= 0) & (rel < P))
    rel = P + META - 1 - np.arange(META_N)
    put(V_NEAR, rel, rel >= 0)
    put(V_FAR, rel + P, rel >= 0)
    hot[:, V_FAR:V_FAR + META_N] = 0.0
    hot[BUCKETS - 1, V_FAR:V_FAR + META_N] = 1.0
    rel = META - 1 - np.arange(SELF_N)
    put(V_SELF, rel, rel >= 0)
    scan = np.ones((P, TOK), np.float32)
    scan[:, 0] = 0.0
    scan[:, META::CH] = 0.0
    return masks, hot, scan


class Phase:

    def __init__(self, kind, layer, slots, cols, before, ffn=None):
        self.kind, self.layer, self.slots, self.cols, self.ffn = kind, layer, slots, cols, ffn
        self.slot0 = before["slots"]
        self.evac0 = before["evac"]
        self.f0 = before["f"]
        self.x0 = before["x"]
        self.a0 = before["a"]
        before["slots"] += slots
        if kind in ("gu", "in"):
            before["evac"] += slots
        if kind == "gu":
            before["a"] += slots // 2
        if kind in ("down", "out"):
            before["f"] += DT


class Norm:

    def __init__(self, layer, post, pre, half, cols, h0, x0, sum0, pair, last):
        self.post_col = None if post is None else (6 * layer + post) * DT
        self.pre_col = None if pre is None else (6 * layer + pre) * DT
        self.half, self.cols, self.h0, self.x0, self.pair, self.last = half, cols, h0, x0, pair, last
        self.f0 = h0 - DT
        self.post_sum = None if post is None else sum0
        self.pre_sum = None if pre is None else sum0 + (post is not None)
        self.t0 = META if cols == TAIL else 0


class Mix:

    def __init__(self, layer, x0, evac0, slots):
        self.layer, self.x0, self.evac0, self.slots = layer, x0, evac0, slots


def plan(stop=None):
    n = {"slots": 0, "evac": 0, "f": 0, "x": 0, "a": 0}
    steps = []
    norms = 0
    sums = 0

    def norm(layer, post, pre, half, cols, last=False):
        nonlocal norms, sums
        steps.append(("norm", Norm(layer, post, pre, half, cols, h0=norms * DT, x0=n["x"], sum0=sums,
                                   pair=(n["slots"] + RING - 1) % RING, last=last)))
        norms += 1
        sums += (post is not None) + (pre is not None)
        if pre is not None:
            n["x"] += DT

    norm(0, None, 0, False, FULL)
    for layer in range(2):
        cols = FULL
        for ffn in range(2):
            if ffn:
                cols = TAIL if layer else FULL
            steps.append(("dense", Phase("gu", layer, 2 * FT, cols, n, ffn=ffn)))
            steps.append(("dense", Phase("down", layer, 2 * DT, cols, n, ffn=ffn)))
            if stop == (layer, ffn):
                norm(layer, 1 if ffn == 0 else 5, None, True, cols, last=True)
                return steps
            if ffn:
                norm(layer, 5, None if layer else 6, True, cols, last=bool(layer))
                continue
            norm(layer, 1, 2, True, cols)
            steps.append(("dense", Phase("in", layer, (ODD_TILES if layer else EVEN_TILES) + 1, FULL, n)))
            steps.append(("mix", Mix(layer, n["x"], n["evac"], n["slots"])))
            n["x"] += DT
            steps.append(("dense", Phase("out", layer, DT, TAIL if layer else FULL, n)))
            if stop == (layer, "mix"):
                norm(layer, 3, None, False, TAIL if layer else FULL, last=True)
                return steps
            norm(layer, 3, 4, False, TAIL if layer else FULL)
    return steps


def halves(cols):
    if cols == TAIL:
        return [(META, SEQ)]
    return [(0, HALF), (HALF, HALF)]


def token_cols(tile, cols):
    if cols == TAIL:
        return tile[:, META:TOK]
    return tile.rearrange("p (a b) -> p a b", a=2)


def linked(steps):
    queries = [s.slot0 for k, s in steps if k == "dense" and s.kind == "in" and s.layer == 0]
    twice = [first + t for first in queries for t in range(QH // KVH)]
    for at, (kind, step) in enumerate(steps):
        if kind == "dense":
            step.before = next((s for k, s in reversed(steps[:at]) if k == "norm"), None)
            step.twice = twice
            step.after = next((s for k, s in steps[at:] if k == "norm"), None)
    return steps


class Core:

    def __init__(self, nc, ctx, steps):
        self.nc, self.steps = nc, steps
        self.phases = [s for kind, s in steps if kind == "dense"]
        last = [s for kind, s in steps if kind == "norm"][-1]
        self.h_total = last.h0 + DT

        def sb(name, shape, dt=F32):
            return ctx.enter_context(nc.sbuf_tensor(name, shape, dt))

        def sem(name):
            return ctx.enter_context(nc.semaphore(name))

        self.h = sb("h", [P, DT, TOK])
        self.w_hl = sb("w_hl", [P, RING, 2, FH * P], F32R)
        self.stage = sb("stage", [P, 2, FH * P])
        self.rinv = sb("rinv", [P, TOK])
        self.sq_sum = sb("sq_sum", [P, TOK])
        self.t_gate = sb("t_gate", [P, TOK])
        self.t_up = sb("t_up", [P, TOK])
        self.ident = sb("ident", [P, P])
        self.ones = sb("ones", [P, P])
        self.norm_cols = sb("norm_cols", [P, 12 * DT])
        self.vec_cols = sb("vec_cols", [P, 64])
        self.heads = sb("heads", [P, QH + 2 * DH])
        self.eps = sb("eps", [P, 4])
        self.x_at = (nc.sbuf_base + 31) // 32 * 32
        self.x_hl = sb("x_hl", [P, 2, DT, TOK], F32R)
        self.arena = (nc.sbuf_base + 31) // 32 * 32
        self.acts = sb("acts", [P, 2, FT, TOK], F32R)
        self.psum = ctx.enter_context(nc.psum_tensor("psum", [P, 8, 512], F32))
        self.f_down = self.at("f_down", [P, DT, TOK], self.x_at)
        self.f_mix = self.at("f_mix", [P, DT, TOK], self.arena)
        at = self.arena
        def rows_at(name, rows, width):
            nonlocal at
            buf = self.at(name, [rows, width], at)
            at += (4 * width + 31) // 32 * 32
            return buf

        self.rows_x = rows_at("rows_x", P, NBLK * D)
        self.rows_meta = rows_at("rows_meta", META, D)
        self.rows_norm = rows_at("rows_norm", 12 * DT, P)
        self.rows_vec = rows_at("rows_vec", VEC_ROWS, P)
        self.table = rows_at("table", BUCKETS + 1, QH)
        self.bucket_hot = rows_at("bucket_hot", BUCKETS + 1, V_ALL)
        self.bias_row = rows_at("bias_row", QH, V_ALL)
        self.rows_x = self.rows_x[:].rearrange("p (b d) -> p b d", b=NBLK)
        self.rows_out = self.at("rows_out", [P, NBLK, D], self.arena)

        self.w_hi = sem("w_hi")
        self.w_lo = sem("w_lo")
        self.slot_used = sem("slot_used")
        self.scaled = sem("scaled")
        self.gate_silu = sem("gate_silu")
        self.act_full = sem("act_full")
        self.act_hi = sem("act_hi")
        self.act_lo = sem("act_lo")
        self.f_out = sem("f_out")
        self.sq_made = sem("sq_made")
        self.sq_added = sem("sq_added")
        self.sum_ready = sem("sum_ready")
        self.root_ready = sem("root_ready")
        self.rinv_ready = sem("rinv_ready")
        self.f_scaled = sem("f_scaled")
        self.h_new = sem("h_new")
        self.x_hi = sem("x_hi")
        self.x_lo = sem("x_lo")
        self.consts_in = sem("consts_in")
        self.consts_set = sem("consts_set")
        self.cols_ready = sem("cols_ready")
        self.cols_flip = sem("cols_flip")
        self.tok_in = sem("tok_in")
        self.tok_flip = sem("tok_flip")
        self.bias_stored = sem("bias_stored")
        self.out_flip = sem("out_flip")
        self.out_left = sem("out_left")
        self.out_right = sem("out_right")
        self.out_stored = sem("out_stored")
        self.w_landed = [sem("w_landed_0"), sem("w_landed_1")]
        self.sem = sem
        self.even = Even(self)
        self.odd = Odd(self)
        self.proj = [self.even.proj, self.odd.proj]

    def at(self, name, shape, offset, dt=F32):
        return self.nc.alloc_sbuf_tensor_at(name, shape, dt, offset=offset)

    def slot_kind(self, g):
        for p in self.phases:
            if p.slot0 <= g < p.slot0 + p.slots:
                if p.kind == "in" and g == p.slot0 + p.slots - 1:
                    return DT, RANK if p.layer else EVEN_GATES
                return (FH if p.kind == "down" else DT), P
        return None


class Slot:

    def __init__(self, phase, i, u, off=0):
        self.i, self.u, self.off = i, u, off
        self.base = phase.slot0 + u + off
        self.local = i * RING + (u + off)
        self.ring = self.base % RING
        self.stage = self.base % 2
        self.pair = self.ring
        self.peeled = isinstance(i, int)
        self.twice = phase.twice

    def count(self, lag=0):
        return self.i * RING + (self.base + 1 - lag)

    def landed(self):
        first = self.base + RING * (self.i if self.peeled else 1)
        twice = [g for g in self.twice if g <= first and g % 2 == self.stage]
        return self.i * (16 * RING // 2) + 16 * (self.base // 2 + 1 + len(twice))


def walk(core, phase, engine, step, ahead=0):
    whole = phase.slots - (1 if phase.kind == "in" else 0)
    bodies = (whole - ahead) // RING
    for u in range(RING):
        step(0, u)
    if bodies > 2:
        with engine.Fori(1, bodies) as i:
            for u in range(RING):
                step(i, u)
    else:
        bodies = 1
    for s in range(bodies * RING, phase.slots):
        step(s // RING, s % RING)


def weights(buf, tiles, cols):
    view = buf.rearrange("p (k n) -> p k n", n=P)[:, 0:tiles, :]
    return view if cols == P else view[:, :, 0:cols]


def split_hi(core, act, slot, kind):
    act.wait_ge(core.w_landed[slot.stage], slot.landed())
    if not slot.peeled or slot.count() > RING:
        act.wait_ge(core.slot_used, slot.count(RING))
    act.activation(weights(core.w_hl[:, slot.ring, 0, :], *kind), weights(core.stage[:, slot.stage, :], *kind),
                   ACT.Copy).then_inc(core.w_hi, 1)


def split_lo(core, dve, slot, kind):
    dve.wait_ge(core.w_hi, slot.count())
    dve.tensor_tensor(weights(core.w_hl[:, slot.ring, 1, :], *kind), weights(core.stage[:, slot.stage, :], *kind),
                      weights(core.w_hl[:, slot.ring, 0, :].bitcast(F32), *kind), ALU.subtract).then_inc(core.w_lo, 1)


def split_ahead(core, engine, half, phase, i, u):
    slot = Slot(phase, i, u, AHEAD)
    g = phase.slot0 + (i * RING if isinstance(i, int) else RING) + u + AHEAD
    kind = core.slot_kind(g)
    if kind:
        half(core, engine, slot, kind)



def sync_program(core, sp, a):
    sp.dma_start(core.rows_x, a["x"][0].rearrange("(b p) d -> p b d", p=P)).then_inc(core.tok_in, 16)
    sp.dma_start(core.rows_meta[:, :], a["meta_tokens"]).then_inc(core.tok_in, 16)
    for kind, phase in core.steps:
        if kind == "dense":
            walk(core, phase, sp, lambda i, u, ph=phase: load_slot(core, sp, a, ph, i, u))
    for b in range(NBLK):
        sp.wait_ge(core.out_left, b + 1)
        sp.wait_ge(core.out_right, b + 1)
        sp.dma_start(a["out"][0, b * P:(b + 1) * P, :], core.rows_out[:, b, :]).then_inc(core.out_stored, 16)
    sp.wait_ge(core.out_stored, 16 * NBLK)


def load_slot(core, sp, a, phase, i, u):
    slot = Slot(phase, i, u)
    if not slot.peeled or slot.count() > 2:
        sp.wait_ge(core.w_lo, slot.count(2))
    dst = core.stage[:, slot.stage, :]
    if phase.kind == "gu":
        w = (a["ffn_w_up"] if u % 2 else a["ffn_w_gate"])[phase.layer, phase.ffn]
        col, n, rows = (i * 2 + u // 2) * P, P, w
    elif phase.kind == "down":
        w = a["ffn_w_down"][phase.layer, phase.ffn]
        half = u % 2
        col, n, rows = (i * 2 + u // 2) * P, P, w[half * FH * P:(half + 1) * FH * P]
    else:
        rows = {("in", 0): a["even_w_in"], ("in", 1): a["odd_w_in"],
                ("out", 0): a["even_w_out"], ("out", 1): a["odd_w_out"]}[phase.kind, phase.layer][0]
        col, n = slot.local * P, P
        if phase.kind == "in" and slot.peeled and slot.local == phase.slots - 1:
            n = RANK if phase.layer else EVEN_GATES
    tiles = FH if phase.kind == "down" else DT
    dst = weights(dst, tiles, n)
    if phase.kind == "in" and phase.layer == 0 and slot.peeled and slot.local < QH // KVH:
        src = rows[:, 0:QH * HD].rearrange("(k p) (g h d) -> h p k g d", p=P, g=KVH, d=HD)[slot.local]
        dst = dst.rearrange("p k (g d) -> p k g d", g=KVH)
        for g in range(KVH):
            sp.dma_start(dst[:, :, g, :], src[:, :, g, :]).then_inc(core.w_landed[slot.stage], 16)
        return
    src = rows[:, bass.ds(col, n)].rearrange("(k p) n -> p k n", p=P)
    sp.dma_start(dst, src).then_inc(core.w_landed[slot.stage], 16)



def products(core, pe, phase, slot, kt, w_tile, moving, first, last):
    for part, moved in ((0, 0), (0, 1), (1, 0)):
        lhs = core.w_hl[:, slot.ring, part, w_tile * P:(w_tile + 1) * P]
        for b, (t0, n) in enumerate(halves(phase.cols)):
            out = core.psum[:, 2 * slot.out_pair + b, 0:n]
            op = pe.matmul(out, lhs, moving[:, moved, kt, t0:t0 + n], start=first and part + moved == 0,
                           stop=last and part == 1)
    return op


def tensor_dense(core, pe, phase):
    k = core

    def weights_ready(slot):
        pe.wait_ge(k.w_lo, slot.count())

    if phase.kind == "down":
        def step(i, u):
            slot = Slot(phase, i, u)
            slot.out_pair = (phase.slot0 + u - u % 2) % RING
            m = i * 2 + u // 2
            weights_ready(slot)
            if u % 2 == 0:
                if isinstance(i, int) and i == 0:
                    pe.wait_ge(k.scaled, phase.evac0 - RING + 1 + u)
                else:
                    pe.wait_ge(k.f_out, m + (phase.f0 - 1))
            for kk in range(FH):
                kt = (u % 2) * FH + kk
                if isinstance(i, int) and i == 0 and u < 2:
                    pe.wait_ge(k.act_lo, phase.a0 - FT + kt + 1)
                op = products(k, pe, phase, slot, kt, kk, k.acts, kt == 0, kt == FT - 1)
            op.then_inc(k.slot_used, 1)

        walk(k, phase, pe, step)
        return

    early = phase.kind != "out"
    if early:
        group = [Slot(phase, 0, u) for u in range(RING - 1)]
        for slot in group:
            weights_ready(slot)
            slot.out_pair = slot.pair
        for kt in range(DT):
            pe.wait_ge(k.x_lo, phase.x0 - DT + kt + 1)
            for slot in group:
                op = products(k, pe, phase, slot, kt, kt, k.x_hl, kt == 0, kt == DT - 1)
                if kt == DT - 1:
                    op.then_inc(k.slot_used, 1)
        token_sum(k, pe, phase.before, phase.before.pre_sum)
    else:
        pe.wait_ge(k.x_lo, phase.x0)

    def step(i, u):
        if early and isinstance(i, int) and i == 0 and u < RING - 1:
            return
        slot = Slot(phase, i, u)
        slot.out_pair = slot.pair
        weights_ready(slot)
        if not (isinstance(i, int) and i == 0):
            if phase.kind == "out":
                pe.wait_ge(k.f_out, i * RING + (u + phase.f0 - RING + 1))
            else:
                pe.wait_ge(k.scaled, i * RING + (u + phase.evac0 - RING + 1))
        for kt in range(DT):
            op = products(k, pe, phase, slot, kt, kt, k.x_hl, kt == 0, kt == DT - 1)
        op.then_inc(k.slot_used, 1)

    walk(k, phase, pe, step)


def token_sum(core, pe, norm, n):
    pe.wait_ge(core.sq_added, DT * (n + 1))
    for b, (t0, w) in enumerate(halves(norm.cols)):
        op = pe.matmul(core.psum[:, 2 * norm.pair + b, 0:w], core.ones[:], core.sq_sum[:, t0:t0 + w],
                       start=True, stop=True)
    op.then_inc(core.sum_ready, 1)


def tensor_program(core, pe):
    k = core
    pe.wait_ge(k.consts_set, 5)
    pe.wait_ge(k.consts_in, 16 * CONST_LOADS)
    pe.transpose(k.psum[:, 0, 0:12 * DT], k.rows_norm[0:12 * DT, :], k.ident[0:12 * DT, 0:12 * DT])
    pe.transpose(k.psum[:, 1, 0:VEC_ROWS], k.rows_vec[0:VEC_ROWS, :], k.ident[0:VEC_ROWS, 0:VEC_ROWS])
    pe.matmul(k.psum[0:QH, 2, 0:512], k.table[:], k.bucket_hot[:, 0:512], start=True, stop=True)
    pe.matmul(k.psum[0:QH, 3, 0:V_ALL - 512], k.table[:], k.bucket_hot[:, 512:V_ALL], start=True,
              stop=True).then_inc(k.cols_flip, 1)
    pe.wait_ge(k.tok_in, 32)
    for kt in range(DT):
        pair = (kt + 2) % RING
        if kt >= 2:
            pe.wait_ge(k.h_new, max(kt - RING + 1, 1))
            pe.wait_ge(k.cols_ready, 4)
        pe.transpose(k.psum[:, 2 * pair, 0:META], k.rows_meta[0:META, kt * P:(kt + 1) * P], k.ident[0:META, 0:META])
        for b in range(NBLK):
            at = META + b * P if b < 2 else (b - 2) * P
            op = pe.transpose(k.psum[:, 2 * pair + b // 2, at:at + P], k.rows_x[:, b, kt * P:(kt + 1) * P], k.ident[:])
        op.then_inc(k.tok_flip, 1)
    pe.wait_ge(k.h_new, DT)
    for kind, step in k.steps:
        if kind == "dense":
            tensor_dense(k, pe, step)
        elif kind == "norm":
            if step.post_sum is not None:
                pe.wait_ge(k.f_out, step.f0 + DT)
                token_sum(k, pe, step, step.post_sum)
        elif step.layer == 0:
            even_tensor(k, pe, step)
        else:
            odd_tensor(k, pe, step)
    for b in range(NBLK):
        if b >= 2:
            pe.wait_ge(k.out_left, b - 1)
            pe.wait_ge(k.out_right, b - 1)
        for kt in range(DT):
            if b == 0:
                pe.wait_ge(k.h_new, k.h_total - DT + kt + 1)
            bank = 4 * (b % 2) + kt // 4
            op = pe.transpose(k.psum[:, bank, (kt % 4) * P:(kt % 4 + 1) * P],
                              k.h[:, kt, META + b * P:META + (b + 1) * P], k.ident[:])
            if kt % 4 == 3:
                op.then_inc(k.out_flip, 1)



def bank_cols(core, pair, cols):
    if cols == TAIL:
        return core.psum[:, 2 * pair, 0:SEQ]
    return core.psum[:, 2 * pair:2 * pair + 2, 0:HALF]


def root(core, act, norm, n, half):
    k = core
    act.wait_ge(k.sum_ready, n + 1)
    act.activation(token_cols(k.rinv[:, :], norm.cols), bank_cols(k, norm.pair, norm.cols), ACT.Sqrt,
                   bias=k.eps[:, 1:2] if half else k.eps[:, 0:1],
                   scale=(4.0 if half else 1.0) / D).then_inc(k.root_ready, 1)


def scalar_norm(core, act, norm):
    k = core
    if norm.post_sum is not None:
        root(k, act, norm, norm.post_sum, norm.half)
    if norm.pre_sum is None:
        return
    for kt in range(DT):
        act.wait_ge(k.h_new, norm.h0 + kt + 1)
        tile = k.h[:, kt, norm.t0:TOK]
        col = norm.pre_col + kt
        act.activation(k.x_hl[:, 0, kt, norm.t0:TOK], tile, ACT.Copy,
                       scale=k.norm_cols[:, col:col + 1]).then_inc(k.x_hi, 1)
        if kt >= 2:
            act.wait_ge(k.sq_added, DT * norm.pre_sum + kt - 1)
        buf = k.t_up if kt % 2 else k.t_gate
        act.activation(buf[:, norm.t0:TOK], tile, ACT.Square).then_inc(k.sq_made, 1)
    root(k, act, norm, norm.pre_sum, False)


def scalar_dense(core, act, phase):
    k = core

    def step(i, u):
        split_ahead(k, act, split_hi, phase, i, u)
        slot = Slot(phase, i, u)
        if phase.kind == "gu":
            t = i * 2 + u // 2
            if u % 2 == 0:
                act.wait_ge(k.scaled, slot.local + (phase.evac0 + 1))
                act.activation(token_cols(k.t_gate[:, :], phase.cols), token_cols(k.t_gate[:, :], phase.cols),
                               ACT.Silu).then_inc(k.gate_silu, 1)
            else:
                act.wait_ge(k.act_full, t + (phase.a0 + 1))
                act.activation(token_cols(tile_at(k.acts[:, 0], t), phase.cols), token_cols(k.t_up[:, :], phase.cols),
                               ACT.Copy).then_inc(k.act_hi, 1)
        elif phase.kind == "down" and u % 2:
            pair = (phase.slot0 + u - 1) % RING
            result_tile(k, act, phase, slot, pair, i * 2 + u // 2, u // 2, k.f_down)
        elif phase.kind == "out":
            result_tile(k, act, phase, slot, slot.pair, slot.local, u % 2, k.f_mix)

    walk(k, phase, act, step, AHEAD)


def tile_at(buf, t):
    if isinstance(t, int):
        return buf[:, t, :]
    return buf[:, bass.ds(t, 1), :].rearrange("p a t -> p (a t)")


def result_tile(core, act, phase, slot, pair, m, odd, buf):
    k, norm = core, phase.after
    src = bank_cols(k, pair, phase.cols)
    act.wait_ge(k.slot_used, slot.count())
    if not (isinstance(m, int) and m < 2):
        act.wait_ge(k.sq_added, m + (DT * norm.post_sum - 1))
    squares = k.t_up if odd else k.t_gate
    act.activation(token_cols(squares[:, :], phase.cols), src, ACT.Square).then_inc(k.sq_made, 1)
    col = norm.post_col + m
    scale = k.norm_cols[:, col:col + 1] if isinstance(m, int) else k.norm_cols[:, bass.ds(col, 1)]
    act.activation(token_cols(tile_at(buf, m), phase.cols), src, ACT.Copy, scale=scale).then_inc(k.f_out, 1)


def scalar_program(core, act):
    k = core
    act.wait_ge(k.cols_flip, 1)
    act.activation(k.norm_cols[:, :], k.psum[:, 0, 0:12 * DT], ACT.Copy).then_inc(k.cols_ready, 1)
    act.activation(k.vec_cols[:, 0:VEC_ROWS], k.psum[:, 1, 0:VEC_ROWS], ACT.Copy).then_inc(k.cols_ready, 1)
    act.activation(k.bias_row[0:QH, 0:512], k.psum[0:QH, 2, 0:512], ACT.Copy).then_inc(k.cols_ready, 1)
    act.activation(k.bias_row[0:QH, 512:V_ALL], k.psum[0:QH, 3, 0:V_ALL - 512], ACT.Copy).then_inc(k.cols_ready, 1)
    act.wait_ge(k.consts_set, 5)
    act.wait_ge(k.bias_stored, 16)
    for u in range(AHEAD):
        split_hi(k, act, Slot(k.phases[0], 0, u), (DT, P))
    for kind, step in k.steps:
        if kind == "dense":
            scalar_dense(k, act, step)
        elif kind == "norm":
            scalar_norm(k, act, step)
        elif step.layer == 0:
            even_scalar(k, act, step)
        else:
            odd_scalar(k, act, step)
    for b in range(NBLK):
        act.wait_ge(k.out_flip, 2 * b + 1)
        act.activation(k.rows_out[:, b, 0:512], k.psum[:, 4 * (b % 2), :], ACT.Copy).then_inc(k.out_left, 1)



def vector_norm(core, dve, norm):
    k, t0 = core, norm.t0
    if norm.post_sum is not None:
        f = k.f_down if norm.half else k.f_mix
        dve.wait_ge(k.root_ready, norm.post_sum + 1)
        dve.reciprocal(k.rinv[:, t0:TOK], k.rinv[:, t0:TOK]).then_inc(k.rinv_ready, 1)
        dve.wait_ge(k.rinv_ready, norm.post_sum + 1)

    def scale_f(kt):
        dve.tensor_tensor(f[:, kt, t0:TOK], f[:, kt, t0:TOK], k.rinv[:, t0:TOK], ALU.mult).then_inc(k.f_scaled, 1)

    def lo(kt):
        dve.wait_ge(k.x_hi, norm.x0 + kt + 1)
        col = norm.pre_col + kt
        dve.scalar_tensor_tensor(k.x_hl[:, 1, kt, t0:TOK], k.h[:, kt, t0:TOK], k.norm_cols[:, col:col + 1],
                                 k.x_hl[:, 0, kt, t0:TOK].bitcast(F32), ALU.mult, ALU.subtract).then_inc(k.x_lo, 1)

    for kt in range(DT):
        if norm.post_sum is not None:
            if kt == 0:
                scale_f(0)
            if kt + 1 < DT:
                scale_f(kt + 1)
            dve.wait_ge(k.f_scaled, norm.f0 + kt + 1)
            dve.tensor_tensor(k.h[:, kt, t0:TOK], k.h[:, kt, t0:TOK], f[:, kt, t0:TOK], ALU.add).then_inc(k.h_new, 1)
        if norm.pre_sum is not None and kt:
            lo(kt - 1)
    if norm.pre_sum is not None:
        lo(DT - 1)
        dve.wait_ge(k.root_ready, norm.pre_sum + 1)
        dve.reciprocal(k.rinv[:, t0:TOK], k.rinv[:, t0:TOK]).then_inc(k.rinv_ready, 1)


def vector_dense(core, dve, phase):
    k = core

    def step(i, u):
        slot = Slot(phase, i, u)
        src = bank_cols(k, slot.pair, phase.cols)
        rinv = token_cols(k.rinv[:, :], phase.cols)
        if phase.kind not in ("gu", "in"):
            split_ahead(k, dve, split_lo, phase, i, u)
            return
        if slot.peeled and slot.local == 0:
            split_ahead(k, dve, split_lo, phase, i, u)
            dve.wait_ge(k.rinv_ready, phase.before.pre_sum + 1)
        dve.wait_ge(k.slot_used, slot.count())
        if phase.kind == "in":
            rows = P
            if slot.peeled and slot.local == phase.slots - 1:
                rows = RANK if phase.layer else EVEN_GATES
            if slot.peeled:
                tile = k.proj[phase.layer][0:rows, slot.local, :]
                src = k.psum[0:rows, 2 * slot.pair:2 * slot.pair + 2, 0:HALF]
                rinv = token_cols(k.rinv[0:rows, :], phase.cols)
            else:
                tile = tile_at(k.proj[phase.layer], slot.local)
            dve.tensor_tensor(token_cols(tile, FULL), src, rinv, ALU.mult).then_inc(k.scaled, 1)
        elif u % 2 == 0:
            dve.tensor_tensor(token_cols(k.t_gate[:, :], phase.cols), src, rinv, ALU.mult).then_inc(k.scaled, 1)
        else:
            t = i * 2 + u // 2
            if not (slot.peeled and slot.local == 1 and phase.a0 == 0):
                dve.wait_ge(k.act_lo, t + phase.a0)
            up, gate = token_cols(k.t_up[:, :], phase.cols), token_cols(k.t_gate[:, :], phase.cols)
            dve.tensor_tensor(up, src, rinv, ALU.mult).then_inc(k.scaled, 1)
            dve.wait_ge(k.scaled, slot.local + (phase.evac0 + 1))
            dve.wait_ge(k.gate_silu, t + (phase.a0 + 1))
            dve.tensor_tensor(up, up, gate, ALU.mult).then_inc(k.act_full, 1)
        if not (slot.peeled and slot.local == 0):
            split_ahead(k, dve, split_lo, phase, i, u)
        if phase.kind == "gu" and u % 2:
            dve.wait_ge(k.act_hi, t + (phase.a0 + 1))
            hi = token_cols(tile_at(k.acts[:, 0], t), phase.cols).bitcast(F32)
            dve.tensor_tensor(token_cols(tile_at(k.acts[:, 1], t), phase.cols), up, hi, ALU.subtract)\
               .then_inc(k.act_lo, 1)

    walk(k, phase, dve, step, AHEAD)


def vector_program(core, dve):
    k = core
    dve.memset(k.ones[:, :], 1.0).then_inc(k.consts_set, 1)
    dve.memset(k.eps[:, 0:1], EPS).then_inc(k.consts_set, 1)
    dve.memset(k.eps[:, 1:2], 4 * EPS).then_inc(k.consts_set, 1)
    dve.memset(k.eps[:, 2:3], DN_DIM * EPS).then_inc(k.consts_set, 1)
    dve.memset(k.table[BUCKETS:BUCKETS + 1, :], MASKED).then_inc(k.consts_set, 1)
    for kt in range(DT):
        pair = (kt + 2) % RING
        dve.wait_ge(k.tok_flip, kt + 1)
        dve.tensor_copy(k.h[:, kt, 0:META + 2 * P], k.psum[:, 2 * pair, 0:META + 2 * P])
        dve.tensor_copy(k.h[:, kt, META + 2 * P:TOK], k.psum[:, 2 * pair + 1, 0:2 * P]).then_inc(k.h_new, 1)
    for u in range(AHEAD):
        split_lo(k, dve, Slot(k.phases[0], 0, u), (DT, P))
    for kind, step in k.steps:
        if kind == "dense":
            vector_dense(k, dve, step)
        elif kind == "norm":
            vector_norm(k, dve, step)
        elif step.layer == 0:
            even_vector(k, dve, step)
        else:
            odd_vector(k, dve, step)
    for b in range(NBLK):
        dve.wait_ge(k.out_flip, 2 * b + 2)
        dve.tensor_copy(k.rows_out[:, b, 512:D], k.psum[:, 4 * (b % 2) + 1, :]).then_inc(k.out_right, 1)



def add_squares(core, pool, n, cols):
    k = core
    t0 = META if cols == TAIL else 0
    for m in range(DT):
        buf = (k.t_up if m % 2 else k.t_gate)[:, t0:TOK]
        if m == 0:
            if n:
                pool.wait_ge(k.sum_ready, n)
            pool.wait_ge(k.sq_made, DT * n + 1)
            pool.tensor_copy(k.sq_sum[:, t0:TOK], buf).then_inc(k.sq_added, 1)
        else:
            pool.wait_ge(k.sq_made, DT * n + m + 1)
            pool.wait_ge(k.sq_added, DT * n + m)
            pool.tensor_tensor(k.sq_sum[:, t0:TOK], k.sq_sum[:, t0:TOK], buf, ALU.add).then_inc(k.sq_added, 1)


def gpsimd_program(core, pool, a):
    k = core
    rows = [
        (k.ident[:, :], a["masks"][:, C_ID:C_ID + P]),
        (k.rows_norm[0:12 * DT, :], a["norm_w"].rearrange("l n (k p) -> (l n k) p", p=P)),
        (k.rows_vec[0:48, :], a["even_conv_w"][0].rearrange("c (k p) -> (c k) p", p=P)),
        (k.rows_vec[48:52, :], a["gla_b_gate"][0:1, :].rearrange("a (k p) -> (a k) p", p=P)),
        (k.rows_vec[52:54, :], a["gla_norm_w"][0:1, :].rearrange("a (k p) -> (a k) p", p=P)),
        (k.rows_vec[54:55, :], a["dn_norm_w"][0:1, :]),
        (k.table[0:BUCKETS, :], a["rel_bias_table"]),
        (k.bucket_hot[:, :], a["bucket_hot"]),
        (k.heads[:, 0:QH], a["swa_sinks"][0:1, :].broadcast_to([P, QH])),
        (k.heads[:, QH:QH + DH], a["dn_a_log"][0:1, :].broadcast_to([P, DH])),
        (k.heads[:, QH + DH:QH + 2 * DH], a["dn_dt_bias"][0:1, :].broadcast_to([P, DH])),
    ]
    assert len(rows) == CONST_LOADS
    for dst, src in rows:
        pool.dma_start(dst, src).then_inc(k.consts_in, 16)
    pool.wait_ge(k.cols_ready, 4)
    pool.dma_start(a["bias_scratch"], k.bias_row[0:QH, :]).then_inc(k.bias_stored, 16)
    for kind, step in k.steps:
        if kind == "norm":
            if step.post_sum is not None:
                add_squares(k, pool, step.post_sum, step.cols)
            if step.pre_sum is not None:
                add_squares(k, pool, step.pre_sum, step.cols)
        elif kind == "mix" and step.layer == 0:
            even_gpsimd(k, pool, step, a)
        elif kind == "mix":
            odd_gpsimd(k, pool, step, a)
    pool.wait_ge(k.bias_stored, 16)



Q_TILE, K_TILE, V_TILE, DN_TILE, Z_TILE, GATE_TILE = 0, 4, 5, 6, 18, 22
BANDS = META + 2 * P
BLOCKS = [(0, META)] + [(META + b * P, P) for b in range(NBLK)]
UNITS = [(b, kv) for b in range(NBLK + 1) for kv in range(KVH)]


class Even:

    def __init__(self, core):
        at, a, x = core.at, core.arena, core.x_at
        tile = 4 * TOK
        self.proj = at("even_proj", [P, EVEN_TILES + 1, TOK], a)
        self.conv = at("conv", [P, 3 * DH, TOK], a + 23 * tile)
        self.o_swa = at("o_swa", [P, 4, TOK], a + 35 * tile)
        self.o_dn = at("o_dn", [P, DH, TOK], a + 31 * tile)
        tail = a + 39 * tile
        self.bias = at("bias", [P, QH, BANDS], tail)
        self.bias_near = at("bias_near", [P, QH, META], tail + 8704)
        self.bias_self = at("bias_self", [META, QH, META], tail + 9216)
        self.flip = at("flip", [P, P], tail + 9728)
        self.scores = at("scores", [P, 2, GRP, BANDS], x)
        self.probs_t = at("probs_t", [P, 2, 3, GRP * P], x + 8704)
        self.v_rows = at("v_rows", [P, NBLK + 1, P], x + 20992)
        self.bias_rows = at("bias_rows", [P, QH, BANDS], x + 23552)
        self.near_rows = at("near_rows", [P, QH, META], x + 32256)
        self.self_rows = at("self_rows", [META, QH, META], x + 32768)
        self.stats = at("swa_stats", [P, 2, 6, GRP], x + 33280)

        big = 4 * (NBLK + 1) * DH * P
        p = a + DN_TILE * tile
        self.masks = at("dn_masks", [P, 9, P], tail)
        self.wide = at("dn_wide", [P, 2, DH * P], tail + 4608)
        self.gates = at("dn_gates", [P, 12, NBLK + 1, DH], tail + 8704)
        self.half_x = at("half_x", [P, NBLK + 1, DH, P], p)
        self.u = at("dn_u", [P, NBLK + 1, DH, P], p)
        self.attn = at("dn_attn", [P, NBLK + 1, DH, P], p + big)
        self.wide2 = at("dn_wide2", [P, 2, DH * P], p + 2 * big)
        self.a_t = at("dn_a", [P, NBLK + 1, DH, P], x)
        self.k_dec = at("dn_k_dec", [P, NBLK + 1, DH, P], x)
        self.inv = at("dn_inv", [P, NBLK + 1, DH, P], x + big)
        self.w_t = at("dn_w", [P, NBLK + 1, DH, P], x + big)
        self.inv_t = at("dn_inv_t", [P, NBLK + 1, DH, P], x + 2 * big)
        self.wide3 = at("dn_wide3", [P, DH * P], x + 3 * big)
        self.rows_in = core.sem("e_rows_in")
        self.masks_in = core.sem("e_masks_in")
        self.v_flip = core.sem("e_v_flip")
        self.bias_flip = core.sem("e_bias_flip")
        self.v_rows_set = core.sem("e_v_rows_set")
        self.bias_set = core.sem("e_bias_set")
        self.scored = core.sem("e_scored")
        self.swa_dve = core.sem("e_swa_dve")
        self.s_made = core.sem("e_s_made")
        self.exped = core.sem("e_exped")
        self.probs = core.sem("e_probs")
        self.p_flip = core.sem("e_p_flip")
        self.p_copied = core.sem("e_p_copied")
        self.o_made = core.sem("e_o_made")
        self.o_copied = core.sem("e_o_copied")
        self.conv_first = core.sem("e_conv_first")
        self.conv_tap = core.sem("e_conv_tap")
        self.conv_done = core.sem("e_conv_done")
        self.conv_sq = core.sem("e_conv_sq")
        self.gate_flip = core.sem("e_gate_flip")
        self.gates_dve = core.sem("e_gates_dve")
        self.gates_act = core.sem("e_gates_act")
        self.gate_sums = core.sem("e_gate_sums")
        self.spread_set = core.sem("e_spread_set")
        self.spread = core.sem("e_spread")
        self.gc_col = core.sem("e_gc_col")
        self.decay = core.sem("e_decay")
        self.diff = core.sem("e_diff")
        self.k_beta = core.sem("e_k_beta")
        self.kk = core.sem("e_kk")
        self.qk = core.sem("e_qk")
        self.a_set = core.sem("e_a_set")
        self.attn_set = core.sem("e_attn_set")
        self.q_decayed = core.sem("e_q_decayed")
        self.level_mask = core.sem("e_level_mask")
        self.x_flip = core.sem("e_x_flip")
        self.x_start = core.sem("e_x_start")
        self.x_mid = core.sem("e_x_mid")
        self.x_mid_set = core.sem("e_x_mid_set")
        self.x_step = core.sem("e_x_step")
        self.x_set = core.sem("e_x_set")
        self.tok_flip2 = core.sem("e_tok_flip2")
        self.tok_scaled = core.sem("e_tok_scaled")
        self.w_made = core.sem("e_w_made")
        self.w_set = core.sem("e_w_set")
        self.read_made = core.sem("e_read_made")
        self.v_new = core.sem("e_v_new")
        self.o_dn_made = core.sem("e_o_dn_made")
        self.state = core.sem("e_state")
        self.o_dn_set = core.sem("e_o_dn_set")
        self.o_sq = core.sem("e_o_sq")
        self.o_sums = core.sem("e_o_sums")
        self.o_gates = core.sem("e_o_gates")
        self.z_silu = core.sem("e_z_silu")
        self.o_normed = core.sem("e_o_normed")
        self.o_full = core.sem("e_o_full")
        self.gates_raw = core.sem("e_gates_raw")
        self.gates_set = core.sem("e_gates_set")
        self.x_first = core.sem("e_x_first")
        self.o_spread = core.sem("e_o_spread")
        self.o_spread_set = core.sem("e_o_spread_set")
        self.dl_set = core.sem("e_dl_set")
        self.cols_decay = core.sem("e_cols_decay")
        self.state_made = core.sem("e_state_made")
        self.o_roots = core.sem("e_o_roots")


def bias_flips():
    return QH + 2


def keys(b):
    if b == 0:
        return 0, 0
    if b == 1:
        return META, P
    return META + (b - 2) * P, 2 * P


def even_gpsimd(core, pool, mix, a):
    k, e = core, core.even
    pool.wait_ge(k.slot_used, mix.slots)
    pool.wait_ge(k.bias_stored, 16)
    scratch = a["bias_scratch"]
    tensor = scratch.tensor

    def skewed(first, rows, n):
        return bass.AP(tensor, first, [[1, rows], [V_ALL, QH], [1, n]])

    pool.dma_start(e.bias_rows[:, :, META:BANDS], skewed(V_BAND, P, 2 * P)).then_inc(e.rows_in, 16)
    pool.dma_start(e.bias_rows[:, :, 0:META], skewed(V_FAR, P, META)).then_inc(e.rows_in, 16)
    pool.dma_start(e.near_rows[:, :, :], skewed(V_NEAR, P, META)).then_inc(e.rows_in, 16)
    pool.dma_start(e.self_rows[:, :, :], skewed(V_SELF, META, META)).then_inc(e.rows_in, 16)
    pool.dma_start(e.flip[:, :], a["masks"][:, C_FLIP:C_FLIP + P]).then_inc(e.rows_in, 16)
    pool.wait_ge(e.probs, len(UNITS))
    pool.dma_start(e.masks[:, 0:2, :], a["masks"][:, C_UP:C_UP + 2 * P].rearrange("p (n q) -> p n q", q=P))\
        .then_inc(e.masks_in, 16)
    pool.dma_start(e.masks[:, 2:9, :], a["masks"][:, C_LVL:C_LVL + LEVELS * P].rearrange("p (n q) -> p n q", q=P))\
        .then_inc(e.masks_in, 16)
    even_gpsimd_delta(k, e, pool)


def even_tensor(core, pe, mix):
    k, e = core, core.even
    ps, proj = k.psum, e.proj
    pe.wait_ge(k.scaled, mix.evac0)
    for c, (t0, n) in enumerate(BLOCKS):
        op = pe.transpose(ps[0:n, 4 + c // 4, (c % 4) * P:(c % 4 + 1) * P], proj[:, V_TILE, t0:t0 + n], k.ident[:])
    op.then_inc(e.v_flip, 1)
    pe.wait_ge(e.rows_in, 80)
    for h in range(QH):
        if h >= 4:
            pe.wait_ge(e.bias_set, h - 3)
        pe.matmul(ps[:, h % 4, 0:BANDS], e.flip[:], e.bias_rows[:, h, :], start=True, stop=True).then_inc(e.bias_flip, 1)
    pe.matmul(ps[:, 6, 0:P], e.flip[:], e.near_rows[:].rearrange("p h m -> p (h m)"), start=True,
              stop=True).then_inc(e.bias_flip, 1)
    pe.matmul(ps[0:META, 7, 0:P], e.flip[0:META, P - META:P], e.self_rows[:].rearrange("p h m -> p (h m)"), start=True,
              stop=True).then_inc(e.bias_flip, 1)
    pe.wait_ge(e.bias_set, bias_flips())
    pe.wait_ge(e.v_rows_set, 2)

    def scores(i):
        b, kv = UNITS[i]
        t0, n = BLOCKS[b]
        rows = slice(HD * kv, HD * (kv + 1))
        first, count = keys(b)
        if i:
            pe.wait_ge(e.scored, i)
        spans = [(0, 0, META)] + ([(META, first, count)] if count else [])
        for h in range(GRP):
            for to, of, w in spans:
                op = pe.matmul(ps[0:n, h, to:to + w], proj[rows, Q_TILE + h, t0:t0 + n], proj[rows, K_TILE, of:of + w],
                               start=True, stop=True)
        op.then_inc(e.s_made, 1)

    scores(0)
    for i, (b, kv) in enumerate(UNITS):
        if i + 1 < len(UNITS):
            scores(i + 1)
        t0, n = BLOCKS[b]
        pieces = [META] + [P] * (keys(b)[1] // P)
        pe.wait_ge(e.probs, i + 1)
        if i:
            pe.wait_ge(e.p_copied, 2 * i)
        for h in range(GRP):
            at = 0
            for j, w in enumerate(pieces):
                op = pe.transpose(ps[0:w, 4 + j, h * P:h * P + n], e.scores[0:n, i % 2, h, at:at + w],
                                  k.ident[0:n, 0:n])
                at += w
        op.then_inc(e.p_flip, 1)
        pe.wait_ge(e.p_copied, 2 * i + 2)
        if i:
            pe.wait_ge(e.o_copied, i)
        for odd in range(2):
            out = ps[HD * odd:HD * (odd + 1), 7, :].rearrange("p (g q) -> p g q", q=P)[:, 0:2, 0:n]
            for j, w in enumerate(pieces):
                block = 0 if j == 0 else (1 if b == 1 else b - 2 + j)
                moving = e.probs_t[0:w, i % 2, j, :].rearrange("p (g o q) -> p g o q", o=2, q=P)[:, :, odd, 0:n]
                op = pe.matmul(out, e.v_rows[0:w, block, HD * kv:HD * (kv + 1)], moving, start=j == 0,
                               stop=j == len(pieces) - 1)
        op.then_inc(e.o_made, 1)
    even_tensor_delta(k, e, pe, mix)


def even_scalar(core, act, mix):
    k, e = core, core.even
    ps = k.psum
    act.wait_ge(e.v_flip, 1)
    act.activation(e.v_rows[0:META, 0, :], ps[0:META, 4, 0:P], ACT.Copy).then_inc(e.v_rows_set, 1)
    act.activation(e.v_rows[:, 1:4, :], ps[:, 4, P:4 * P].rearrange("p (c d) -> p c d", d=P), ACT.Copy)\
        .then_inc(e.v_rows_set, 1)
    act.activation(e.v_rows[:, 4, :], ps[:, 5, 0:P], ACT.Copy).then_inc(e.v_rows_set, 1)
    for t in range(3 * DH):
        conv_first(k, e, act, t, mix)
    for i, (b, kv) in enumerate(UNITS):
        n = BLOCKS[b][1]
        width = META + keys(b)[1]
        st = e.stats[0:n, i % 2]
        act.wait_ge(e.swa_dve, 5 * i + 3)
        for h in range(GRP):
            tile = e.scores[0:n, i % 2, h, 0:width]
            act.activation(tile, tile, ACT.Exp, bias=st[:, 1, h:h + 1], accum_out=st[:, 2, h:h + 1])
        act.activation(st[:, 3, :], st[:, 3, :], ACT.Exp).then_inc(e.exped, 1)
        pieces = 1 + keys(b)[1] // P
        act.wait_ge(e.p_flip, i + 1)
        if i >= 2:
            act.wait_ge(e.o_made, i - 1)
        act.activation(spread_cols(e.probs_t[0:META, i % 2, 0, :], n), spread_cols(ps[0:META, 4, :], n),
                       ACT.Copy).then_inc(e.p_copied, 1)
        if pieces > 1:
            act.activation(e.probs_t[:, i % 2, 1:pieces, :], ps[:, 5:4 + pieces, :], ACT.Copy)\
                .then_inc(e.p_copied, 1)
        else:
            act.activation(st[:, 3, 0:1], st[:, 3, 0:1], ACT.Copy).then_inc(e.p_copied, 1)
        act.wait_ge(e.o_made, i + 1)
        t0 = BLOCKS[b][0]
        act.activation(e.o_swa[:, 2 * kv:2 * kv + 2, t0:t0 + n],
                       ps[:, 7, :].rearrange("p (g q) -> p g q", q=P)[:, 0:2, 0:n], ACT.Copy).then_inc(e.o_copied, 1)
    even_scalar_delta(k, e, act, mix)


def spread_cols(row, n):
    return row.rearrange("p (h q) -> p h q", q=P)[:, :, 0:n]


def conv_first(k, e, act, t, mix):
    if t == 0:
        act.wait_ge(k.scaled, mix.evac0)
    col = (CONV - 1) * 3 * DH + t
    act.activation(e.conv[:, t, :], e.proj[:, DN_TILE + t, :], ACT.Copy,
                   scale=k.vec_cols[:, col:col + 1]).then_inc(e.conv_first, 1)


def conv_taps(k, e, dve, pair):
    for back in range(1, CONV):
        for t in (2 * pair, 2 * pair + 1):
            done = (CONV - 1) * 2 * pair + 2 * (back - 1) + t % 2
            if back == 1:
                dve.wait_ge(e.conv_first, t + 1)
            else:
                dve.wait_ge(e.conv_tap, done - 1)
            col = (CONV - 1 - back) * 3 * DH + t
            out = e.conv[:, t, back:TOK]
            dve.scalar_tensor_tensor(out, e.proj[:, DN_TILE + t, 0:TOK - back], k.vec_cols[:, col:col + 1], out,
                                     ALU.mult, ALU.add).then_inc(e.conv_tap, 1)


def even_vector(core, dve, mix):
    k, e = core, core.even
    ps = k.psum
    for h in range(QH):
        dve.wait_ge(e.bias_flip, h + 1)
        dve.tensor_copy(e.bias[:, h, :], ps[:, h % 4, 0:BANDS]).then_inc(e.bias_set, 1)
    dve.wait_ge(e.bias_flip, bias_flips())
    dve.tensor_copy(e.bias_near[:].rearrange("p h m -> p (h m)"), ps[:, 6, 0:P]).then_inc(e.bias_set, 1)
    dve.tensor_copy(e.bias_self[:].rearrange("p h m -> p (h m)"), ps[0:META, 7, 0:P]).then_inc(e.bias_set, 1)
    dve.wait_ge(e.bias_set, bias_flips())
    scale = HD ** -0.5
    steps = 0
    for i, (b, kv) in enumerate(UNITS):
        n = BLOCKS[b][1]
        heads = slice(GRP * kv, GRP * (kv + 1))
        width = META + keys(b)[1]
        sc = e.scores[0:n, i % 2]
        st = e.stats[0:n, i % 2]
        dve.wait_ge(e.s_made, i + 1)
        if i >= 2:
            dve.wait_ge(e.p_flip, i - 1)
        if b < 2:
            near = e.bias_self if b == 0 else e.bias_near
            op = dve.scalar_tensor_tensor(sc[:, :, 0:META], ps[0:n, 0:GRP, 0:META], scale, near[0:n, heads, :],
                                          ALU.mult, ALU.add)
            if b:
                op = dve.scalar_tensor_tensor(sc[:, :, META:width], ps[0:n, 0:GRP, META:width], scale,
                                              e.bias[:, heads, META + P:BANDS], ALU.mult, ALU.add)
        else:
            op = dve.scalar_tensor_tensor(sc, ps[0:n, 0:GRP, 0:BANDS], scale, e.bias[:, heads, :], ALU.mult, ALU.add)
        op.then_inc(e.scored, 1)
        dve.wait_ge(e.scored, i + 1)
        dve.tensor_reduce(st[:, 0, :], sc[:, :, 0:width], AX.X, ALU.max).then_inc(e.swa_dve, 1)
        dve.wait_ge(e.swa_dve, 5 * i + 1)
        dve.tensor_tensor(st[:, 0, :], st[:, 0, :], k.heads[0:n, heads], ALU.max).then_inc(e.swa_dve, 1)
        dve.wait_ge(e.swa_dve, 5 * i + 2)
        dve.tensor_scalar(st[:, 1, :], st[:, 0, :], -1.0, None, ALU.mult)
        dve.tensor_tensor(st[:, 3, :], k.heads[0:n, heads], st[:, 0, :], ALU.subtract).then_inc(e.swa_dve, 1)
        if i < 3 * DH // 2:
            conv_taps(k, e, dve, i)
        dve.wait_ge(e.exped, i + 1)
        dve.tensor_tensor(st[:, 4, :], st[:, 2, :], st[:, 3, :], ALU.add).then_inc(e.swa_dve, 1)
        dve.wait_ge(e.swa_dve, 5 * i + 4)
        dve.reciprocal(st[:, 5, :], st[:, 4, :]).then_inc(e.swa_dve, 1)
        dve.wait_ge(e.swa_dve, 5 * i + 5)
        dve.tensor_tensor(sc[:, :, 0:width], sc[:, :, 0:width], st[:, 5, :].unsqueeze(2).broadcast_to([n, GRP, width]),
                          ALU.mult).then_inc(e.probs, 1)
    even_vector_delta(k, e, dve, mix)


G_B, G_A, G_SQ, G_SK, G_BETA, G_LOG, G_RQ, G_RK, G_CUM, G_BEG, G_KD, G_DL = range(12)
M_UP, M_ADD, M_LVL = 0, 1, 2
SPREADS = ((M_UP, G_LOG), (None, G_RK), (None, G_RQ), (None, G_BETA))
LEVEL_ITEMS = [(lv, c) for lv in range(1, LEVELS) for c in range(NBLK + 1) if (1 << lv) < BLOCKS[c][1]]


class Chain:

    def __init__(self, engine, sem):
        self.engine, self.sem, self.n = engine, sem, 0

    def then(self, op):
        op.then_inc(self.sem, 1)
        self.n += 1
        self.engine.wait_ge(self.sem, self.n)


def heads_view(buf, rows, n):
    flat = buf[0:rows]
    if len(flat.shape) == 2:
        flat = flat.rearrange("p (h q) -> p h q", q=P)
    return flat[:, :, 0:n]


def along(col, rows, n):
    return col.unsqueeze(2).broadcast_to([rows, DH, n])


def over_heads(mask, rows, n):
    return mask.unsqueeze(1).broadcast_to([rows, DH, n])


def even_gpsimd_delta(k, e, pool):
    pool.wait_ge(e.masks_in, 32)
    pool.wait_ge(e.gates_set, 1)
    for c, (t0, n) in enumerate(BLOCKS):
        for q, (mask, gate) in enumerate(SPREADS):
            j = 4 * c + q
            if j >= 2:
                pool.wait_ge(e.spread, j - 1)
            m = k.ident[0:n, 0:n] if mask is None else e.masks[0:n, mask, 0:n]
            pool.tensor_tensor(heads_view(e.wide[:, j % 2, :], n, n), over_heads(m, n, n),
                               along(e.gates[0:n, gate, c, :], n, n), ALU.mult).then_inc(e.spread_set, 1)
    for c, (t0, n) in enumerate(BLOCKS):
        pool.wait_ge(e.a_set, c + 1)
        if c >= 2:
            pool.wait_ge(e.x_first, c - 1)
        buf = k.t_up if c % 2 else k.t_gate
        pool.tensor_tensor(heads_view(buf[:, 0:DH * P], n, n), heads_view(e.a_t[:, c], n, n),
                           over_heads(e.masks[0:n, M_LVL, 0:n], n, n), ALU.mult).then_inc(e.level_mask, 1)
    for j, (lv, c) in enumerate(LEVEL_ITEMS):
        n = BLOCKS[c][1]
        at = j + NBLK + 1
        if j == 0:
            pool.wait_ge(e.x_first, NBLK + 1)
        elif j >= 2:
            pool.wait_ge(e.x_mid, j - 1)
        buf = k.t_up if at % 2 else k.t_gate
        pool.tensor_tensor(heads_view(buf[:, 0:DH * P], n, n), heads_view(e.a_t[:, c], n, n),
                           over_heads(e.masks[0:n, M_LVL + lv, 0:n], n, n), ALU.mult).then_inc(e.level_mask, 1)
    pool.wait_ge(e.o_gates, 1)
    for c, (t0, n) in enumerate(BLOCKS):
        if c >= 2:
            pool.wait_ge(e.o_spread, c - 1)
        pool.tensor_tensor(heads_view(e.wide[:, c % 2, :], n, n), over_heads(k.ident[0:n, 0:n], n, n),
                           along(e.gates[0:n, G_SK, c, :], n, n), ALU.mult).then_inc(e.o_spread_set, 1)


def even_tensor_delta(k, e, pe, mix):
    ps = k.psum
    pe.wait_ge(e.p_copied, 2 * len(UNITS))
    for c, (t0, n) in enumerate(BLOCKS):
        op = pe.transpose(ps[0:n, 4, c * 8:(c + 1) * 8], e.proj[0:2 * DH, GATE_TILE, t0:t0 + n],
                          k.ident[0:2 * DH, 0:2 * DH])
    op.then_inc(e.gate_flip, 1)
    for t in range(2 * DH):
        pe.wait_ge(e.conv_sq, t + 1)
        sq = k.t_up if t % 2 else k.t_gate
        for c, (t0, n) in enumerate(BLOCKS):
            op = pe.matmul(ps[0:n, 5, c * 8 + t:c * 8 + t + 1], sq[:, t0:t0 + n], k.ones[:, 0:1], start=True, stop=True)
        op.then_inc(e.gate_sums, 1)
    pe.wait_ge(e.o_copied, len(UNITS))
    for c, (t0, n) in enumerate(BLOCKS):
        for q in range(4):
            pe.wait_ge(e.spread_set, 4 * c + q + 1)
            if q == 0 and c:
                pe.wait_ge(e.decay, 2 * c)
                pe.wait_ge(e.k_beta, c)
            pe.matmul(heads_view(ps[:, q, :], P, n), k.ones[0:n, :], heads_view(e.wide[:, (4 * c + q) % 2, :], n, n),
                      start=True, stop=True).then_inc(e.spread, 1)
            if q == 0:
                pe.matmul(ps[0:n, 6, 0:DH], e.masks[0:n, M_UP, 0:n], e.gates[0:n, G_LOG, c, :], start=True,
                          stop=True).then_inc(e.gc_col, 1)
        if c:
            pe.wait_ge(e.attn_set, c)
        pe.wait_ge(e.k_beta, c + 1)
        for h in range(DH):
            op = pe.matmul(ps[0:n, 4, h * P:h * P + n], e.conv[:, DH + h, t0:t0 + n], e.wide3[:, h * P:h * P + n],
                           start=True, stop=True)
        op.then_inc(e.kk, 1)
        for h in range(DH):
            op = pe.matmul(ps[0:n, 5, h * P:h * P + n], e.conv[:, DH + h, t0:t0 + n], e.conv[:, h, t0:t0 + n],
                           start=True, stop=True)
        op.then_inc(e.qk, 1)
    pe.wait_ge(e.attn_set, NBLK + 1)
    for c, (t0, n) in enumerate(BLOCKS):
        pe.wait_ge(e.x_first, c + 1)
        if c >= 2:
            pe.wait_ge(e.x_start, c - 1)
        for h in range(DH):
            op = pe.transpose(ps[0:n, c % 2, h * P:h * P + n], e.inv_t[0:n, c, h, 0:n], k.ident[0:n, 0:n])
        op.then_inc(e.x_flip, 1)
    pe.wait_ge(e.x_start, NBLK + 1)

    def middle(j):
        lv, c = LEVEL_ITEMS[j]
        n = BLOCKS[c][1]
        pe.wait_ge(e.level_mask, NBLK + 1 + j + 1)
        before = [i for i, (_, other) in enumerate(LEVEL_ITEMS[:j]) if other == c]
        if before:
            pe.wait_ge(e.x_set, before[-1] + 1)
        if j >= 2:
            pe.wait_ge(e.x_mid_set, j - 1)
        buf = k.t_up if (NBLK + 1 + j) % 2 else k.t_gate
        for h in range(DH):
            op = pe.matmul(ps[0:n, j % 2, h * P:h * P + n], buf[0:n, h * P:h * P + n], e.inv[0:n, c, h, 0:n],
                           start=True, stop=True)
        op.then_inc(e.x_mid, 1)

    middle(0)
    for j, (lv, c) in enumerate(LEVEL_ITEMS):
        n = BLOCKS[c][1]
        if j + 1 < len(LEVEL_ITEMS):
            middle(j + 1)
        pe.wait_ge(e.x_mid_set, j + 1)
        if j >= 2:
            pe.wait_ge(e.x_set, j - 1)
        for h in range(DH):
            pe.matmul(ps[0:n, 2 + j % 2, h * P:h * P + n], e.inv_t[0:n, c, h, 0:n], e.half_x[0:n, c, h, 0:n],
                      start=True, stop=True)
            op = pe.matmul(ps[0:n, 4 + j % 2, h * P:h * P + n], e.half_x[0:n, c, h, 0:n], e.inv_t[0:n, c, h, 0:n],
                           start=True, stop=True)
        op.then_inc(e.x_step, 1)
    pe.wait_ge(e.x_set, len(LEVEL_ITEMS))
    for c, (t0, n) in enumerate(BLOCKS):
        if c >= 2:
            pe.wait_ge(e.tok_scaled, 3 * (c - 1))
        for h in range(DH):
            op = pe.transpose(ps[0:n, c % 2, h * P:(h + 1) * P], e.conv[:, DH + h, t0:t0 + n], k.ident[:])
        op.then_inc(e.tok_flip2, 1)
        for h in range(DH):
            op = pe.transpose(ps[0:n, 2 + c % 2, h * P:(h + 1) * P], e.conv[:, 2 * DH + h, t0:t0 + n], k.ident[:])
        op.then_inc(e.tok_flip2, 1)
        pe.wait_ge(e.tok_scaled, 3 * c + 3)
        if c >= 2:
            pe.wait_ge(e.w_set, 2 * (c - 1))
        for h in range(DH):
            op = pe.matmul(ps[:, 4 + c % 2, h * P:h * P + n], e.wide[0:n, c % 2, h * P:(h + 1) * P],
                           e.inv_t[0:n, c, h, 0:n], start=True, stop=True)
        op.then_inc(e.w_made, 1)
        for h in range(DH):
            op = pe.matmul(ps[0:n, 6 + c % 2, h * P:(h + 1) * P], e.inv_t[0:n, c, h, 0:n],
                           e.wide2[0:n, c % 2, h * P:(h + 1) * P], start=True, stop=True)
        op.then_inc(e.w_made, 1)
    pe.wait_ge(e.w_set, 2 * (NBLK + 1))

    def out_sums(c):
        n = BLOCKS[c][1]
        pe.wait_ge(e.o_sq, c + 1)
        for h in range(DH):
            op = pe.matmul(ps[0:n, 6, c * DH + h:c * DH + h + 1], e.wide[:, c % 2, h * P:h * P + n], k.ones[:, 0:1],
                           start=True, stop=True)
        op.then_inc(e.o_sums, 1)

    for c, (t0, n) in enumerate(BLOCKS):
        if c:
            pe.wait_ge(e.state, c)
            for h in range(DH):
                op = pe.matmul(ps[0:n, 0, h * P:(h + 1) * P], e.w_t[:, c, h, 0:n], e.wide3[:, h * P:(h + 1) * P],
                               start=True, stop=True)
            op.then_inc(e.read_made, 1)
            pe.wait_ge(e.v_new, c)
        if c >= 2:
            pe.wait_ge(e.o_dn_set, c - 1)
        for h in range(DH):
            out = ps[:, 2 + c % 2, h * P:h * P + n]
            if c:
                pe.matmul(out, e.wide3[:, h * P:(h + 1) * P], e.conv[:, h, t0:t0 + n], start=True, stop=False)
            op = pe.matmul(out, e.u[0:n, c, h, :], e.attn[0:n, c, h, 0:n], start=c == 0, stop=True)
        op.then_inc(e.o_dn_made, 1)
        if c < NBLK:
            for h in range(DH):
                op = pe.matmul(ps[:, 4, h * P:(h + 1) * P], e.k_dec[0:n, c, h, :], e.u[0:n, c, h, :], start=True,
                               stop=True)
            op.then_inc(e.state_made, 1)
        if c:
            out_sums(c - 1)
    out_sums(NBLK)
    for c, (t0, n) in enumerate(BLOCKS):
        pe.wait_ge(e.o_spread_set, c + 1)
        if c >= 2:
            pe.wait_ge(e.o_normed, c - 1)
        pe.matmul(heads_view(ps[:, c % 2, :], P, n), k.ones[0:n, :], heads_view(e.wide[:, c % 2, :], n, n),
                  start=True, stop=True).then_inc(e.o_spread, 1)


def even_scalar_delta(k, e, act, mix):
    ps = k.psum
    for t in range(3 * DH):
        act.wait_ge(e.conv_tap, 2 * (CONV - 1) * (t // 2) + 2 * (CONV - 2) + t % 2 + 1)
        act.activation(e.conv[:, t, :], e.conv[:, t, :], ACT.Silu).then_inc(e.conv_done, 1)
        if t < 2 * DH:
            act.wait_ge(e.conv_done, t + 1)
            if t >= 2:
                act.wait_ge(e.gate_sums, t - 1)
            act.activation((k.t_up if t % 2 else k.t_gate)[:, :], e.conv[:, t, :], ACT.Square).then_inc(e.conv_sq, 1)
    for h in range(DH):
        act.activation(e.proj[:, Z_TILE + h, :], e.proj[:, Z_TILE + h, :], ACT.Silu).then_inc(e.z_silu, 1)
    g = e.gates
    act.wait_ge(e.gates_raw, 3)
    act.activation(g[:, G_B], g[:, G_B], ACT.Exp, scale=-1.0).then_inc(e.gates_act, 1)
    act.activation(g[:, G_A], g[:, G_A], ACT.Exp).then_inc(e.gates_act, 1)
    act.activation(k.heads[:, QH:QH + DH], k.heads[:, QH:QH + DH], ACT.Exp).then_inc(e.gates_act, 1)
    act.wait_ge(e.gates_act, 3)
    act.activation(g[:, G_A], g[:, G_A], ACT.Ln, bias=k.ones[:, 0:1]).then_inc(e.gates_act, 1)
    act.wait_ge(e.gates_raw, 4)
    act.activation(g[:, G_RQ], g[:, G_SQ], ACT.Sqrt, bias=k.eps[:, 2:3], scale=float(DN_DIM)).then_inc(e.gates_act, 1)
    act.activation(g[:, G_RK], g[:, G_SK], ACT.Sqrt, bias=k.eps[:, 0:1]).then_inc(e.gates_act, 1)
    for c, (t0, n) in enumerate(BLOCKS):
        act.wait_ge(e.spread, 4 * c + 1)
        if c:
            act.wait_ge(e.q_decayed, c)
            act.wait_ge(e.dl_set, c)
        act.activation(heads_view(e.wide2[:, 0, :], P, n), heads_view(ps[:, 0, :], P, n), ACT.Exp).then_inc(e.decay, 1)
        act.wait_ge(e.diff, 3 * c + 1)
        act.activation(g[0:n, G_BEG, c], g[0:n, G_CUM, c], ACT.Exp)
        act.activation(g[0:n, G_KD, c], g[0:n, G_KD, c], ACT.Exp).then_inc(e.cols_decay, 1)
        act.wait_ge(e.diff, 3 * c + 3)
        gamma = heads_view(e.wide2[:, 1, :], n, n)
        act.activation(gamma, gamma, ACT.Exp).then_inc(e.decay, 1)
    for c, (t0, n) in enumerate(BLOCKS):
        act.wait_ge(e.x_flip, c + 1)
        act.activation(heads_view(e.inv[:, c], n, n), heads_view(ps[:, c % 2, :], n, n), ACT.Copy)\
            .then_inc(e.x_start, 1)
    for j, (lv, c) in enumerate(LEVEL_ITEMS):
        n = BLOCKS[c][1]
        act.wait_ge(e.x_mid, j + 1)
        before = [i for i, (_, other) in enumerate(LEVEL_ITEMS[:j]) if other == c]
        if before:
            act.wait_ge(e.x_step, before[-1] + 1)
        act.activation(heads_view(e.half_x[:, c], n, n), heads_view(ps[:, j % 2, :], n, n), ACT.Copy)\
            .then_inc(e.x_mid_set, 1)
    act.wait_ge(e.x_set, len(LEVEL_ITEMS))
    for c, (t0, n) in enumerate(BLOCKS):
        act.wait_ge(e.w_made, 2 * c + 1)
        act.activation(heads_view(e.w_t[:, c], P, n), heads_view(ps[:, 4 + c % 2, :], P, n), ACT.Copy)\
            .then_inc(e.w_set, 1)
        act.wait_ge(e.w_made, 2 * c + 2)
        act.activation(heads_view(e.u[:, c], n, P), heads_view(ps[:, 6 + c % 2, :], n, P), ACT.Copy)\
            .then_inc(e.w_set, 1)
    for c, (t0, n) in enumerate(BLOCKS):
        act.wait_ge(e.o_dn_made, c + 1)
        if c >= 2:
            act.wait_ge(e.o_sums, c - 1)
        src = heads_view(ps[:, 2 + c % 2, :], P, n)
        act.activation(heads_view(e.wide[:, c % 2, :], P, n), src, ACT.Square).then_inc(e.o_sq, 1)
        act.activation(e.o_dn[:, :, t0:t0 + n], src, ACT.Copy).then_inc(e.o_dn_set, 1)
    act.wait_ge(e.o_sums, NBLK + 1)
    act.activation(g[0:META, G_SQ, 0], ps[0:META, 6, 0:DH], ACT.Sqrt, bias=k.eps[0:META, 0:1], scale=1.0 / DN_DIM)
    act.activation(g[:, G_SQ, 1:], ps[:, 6, DH:(NBLK + 1) * DH].rearrange("p (c h) -> p c h", h=DH), ACT.Sqrt,
                   bias=k.eps[:, 0:1], scale=1.0 / DN_DIM).then_inc(e.o_roots, 1)
    for kt in range(DT):
        if kt < 4:
            tile = e.o_swa[:, kt, :]
        else:
            act.wait_ge(e.o_full, kt - 3)
            tile = e.o_dn[:, kt - 4, :]
        act.activation(k.x_hl[:, 0, kt, :], tile, ACT.Copy).then_inc(k.x_hi, 1)


def even_vector_delta(k, e, dve, mix):
    ps, g = k.psum, e.gates
    chain = Chain(dve, e.gates_dve)
    chain.then(dve.memset(g[:], 1.0))
    dve.wait_ge(e.gate_flip, 1)
    raw = ps[:, 4, 0:8 * (NBLK + 1)].rearrange("p (c q h) -> p q c h", q=2, h=DH)
    dve.tensor_copy(g[0:META, 0:2, 0], raw[0:META, :, 0])
    chain.then(dve.tensor_copy(g[:, 0:2, 1:], raw[:, :, 1:]))
    dt = k.heads[:, QH + DH:QH + 2 * DH].unsqueeze(1).broadcast_to([P, NBLK + 1, DH])
    a_log = k.heads[:, QH:QH + DH].unsqueeze(1).broadcast_to([P, NBLK + 1, DH])
    x, neg = g[:, G_LOG], g[:, G_BEG]
    chain.then(dve.tensor_tensor(x, g[:, G_A], dt, ALU.add))
    dve.sem_inc(e.gates_raw, 2)
    chain.then(dve.tensor_scalar(neg, x, -1.0, None, ALU.mult))
    dve.tensor_tensor(g[:, G_A], x, neg, ALU.min).then_inc(e.gates_raw, 1)
    dve.wait_ge(e.gates_act, 1)
    chain.then(dve.tensor_scalar(g[:, G_BETA], g[:, G_B], 1.0, None, ALU.add))
    chain.then(dve.reciprocal(g[:, G_BETA], g[:, G_BETA]))
    dve.wait_ge(e.gates_act, 4)
    chain.then(dve.scalar_tensor_tensor(x, x, 0.0, g[:, G_A], ALU.max, ALU.add))
    chain.then(dve.scalar_tensor_tensor(x, x, -1.0, a_log, ALU.mult, ALU.mult))
    dve.wait_ge(e.gate_sums, 2 * DH)
    sums = ps[:, 5, 0:8 * (NBLK + 1)].rearrange("p (c q h) -> p q c h", q=2, h=DH)
    dve.tensor_copy(g[0:META, G_SQ:G_SQ + 2, 0], sums[0:META, :, 0])
    dve.tensor_copy(g[:, G_SQ:G_SQ + 2, 1:], sums[:, :, 1:]).then_inc(e.gates_raw, 1)
    dve.wait_ge(e.gates_act, 6)
    dve.reciprocal(g[:, G_RQ:G_RQ + 2], g[:, G_RQ:G_RQ + 2]).then_inc(e.gates_set, 1)
    dve.wait_ge(e.masks_in, 32)
    for c, (t0, n) in enumerate(BLOCKS):
        diff = heads_view(e.wide2[:, 1, :], n, n)
        cum = heads_view(ps[:, 0, :], n, n)
        toks = slice(t0, t0 + n)
        dve.wait_ge(e.gc_col, c + 1)
        chain.then(dve.tensor_copy(g[0:n, G_CUM, c], ps[0:n, 6, 0:DH]))
        dve.wait_ge(e.decay, 2 * c + 1)
        dve.tensor_tensor(g[0:n, G_KD, c], cum[:, :, n - 1], g[0:n, G_CUM, c], ALU.subtract).then_inc(e.diff, 1)
        if c:
            dve.wait_ge(e.attn_set, c)
        dve.tensor_tensor(diff, cum, along(g[0:n, G_CUM, c], n, n), ALU.subtract).then_inc(e.diff, 1)
        dve.wait_ge(e.diff, 3 * c + 2)
        dve.scalar_tensor_tensor(diff, diff, 0.0, over_heads(e.masks[0:n, M_ADD, 0:n], n, n), ALU.min, ALU.add)\
            .then_inc(e.diff, 1)
        dve.wait_ge(e.spread, 4 * c + 2)
        keys_t = e.conv[:, DH:2 * DH, toks]
        chain.then(dve.tensor_tensor(keys_t, keys_t, heads_view(ps[:, 1, :], P, n), ALU.mult))
        dve.wait_ge(e.spread, 4 * c + 3)
        queries_t = e.conv[:, 0:DH, toks]
        chain.then(dve.tensor_tensor(queries_t, queries_t, heads_view(ps[:, 2, :], P, n), ALU.mult))
        dve.wait_ge(e.spread, 4 * c + 4)
        if c:
            dve.wait_ge(e.kk, c)
        dve.tensor_tensor(heads_view(e.wide3[:, :], P, n), keys_t, heads_view(ps[:, 3, :], P, n), ALU.mult)\
            .then_inc(e.k_beta, 1)
        dve.wait_ge(e.decay, 2 * c + 2)
        dve.tensor_copy(g[:, G_DL, c], heads_view(e.wide2[:, 0, :], P, n)[:, :, n - 1]).then_inc(e.dl_set, 1)
        dve.wait_ge(e.cols_decay, c + 1)
        dve.tensor_tensor(g[0:n, G_BEG, c], g[0:n, G_BEG, c], g[0:n, G_BETA, c], ALU.mult)
        dve.wait_ge(e.kk, c + 1)
        dve.tensor_tensor(heads_view(e.a_t[:, c], n, n), heads_view(ps[:, 4, :], n, n), diff, ALU.mult)\
            .then_inc(e.a_set, 1)
        dve.wait_ge(e.qk, c + 1)
        dve.tensor_tensor(heads_view(e.attn[:, c], n, n), heads_view(ps[:, 5, :], n, n), diff, ALU.mult)\
            .then_inc(e.attn_set, 1)
        dve.tensor_tensor(queries_t, queries_t, heads_view(e.wide2[:, 0, :], P, n), ALU.mult).then_inc(e.q_decayed, 1)
    for c, (t0, n) in enumerate(BLOCKS):
        dve.wait_ge(e.level_mask, c + 1)
        buf = k.t_up if c % 2 else k.t_gate
        dve.tensor_tensor(heads_view(e.inv_t[:, c], n, n), over_heads(k.ident[0:n, 0:n], n, n),
                          heads_view(buf[:, 0:DH * P], n, n), ALU.subtract).then_inc(e.x_first, 1)
    for j, (lv, c) in enumerate(LEVEL_ITEMS):
        n = BLOCKS[c][1]
        dve.wait_ge(e.x_step, j + 1)
        inv, inv_t = heads_view(e.inv[:, c], n, n), heads_view(e.inv_t[:, c], n, n)
        dve.tensor_tensor(inv, inv, heads_view(ps[:, 2 + j % 2, :], n, n), ALU.subtract)
        dve.tensor_tensor(inv_t, inv_t, heads_view(ps[:, 4 + j % 2, :], n, n), ALU.subtract).then_inc(e.x_set, 1)
    dve.wait_ge(e.level_mask, NBLK + 1 + len(LEVEL_ITEMS))
    for c, (t0, n) in enumerate(BLOCKS):
        dve.wait_ge(e.tok_flip2, 2 * c + 1)
        if c >= 2:
            dve.wait_ge(e.w_made, 2 * (c - 1))
        keys_c, values_c = heads_view(ps[:, c % 2, :], n, P), heads_view(ps[:, 2 + c % 2, :], n, P)
        dve.tensor_tensor(heads_view(e.wide[:, c % 2, :], n, P), keys_c, along(g[0:n, G_BEG, c], n, P), ALU.mult)\
            .then_inc(e.tok_scaled, 1)
        dve.tensor_tensor(heads_view(e.k_dec[:, c], n, P), keys_c, along(g[0:n, G_KD, c], n, P), ALU.mult)\
            .then_inc(e.tok_scaled, 1)
        dve.wait_ge(e.tok_flip2, 2 * c + 2)
        dve.tensor_tensor(heads_view(e.wide2[:, c % 2, :], n, P), values_c, along(g[0:n, G_BETA, c], n, P), ALU.mult)\
            .then_inc(e.tok_scaled, 1)
    for c, (t0, n) in enumerate(BLOCKS):
        u = heads_view(e.u[:, c], n, P)
        if c:
            dve.wait_ge(e.read_made, c)
            dve.tensor_tensor(u, u, heads_view(ps[:, 0, :], n, P), ALU.subtract).then_inc(e.v_new, 1)
        if c == NBLK:
            break
        dve.wait_ge(e.state_made, c + 1)
        if c == 0:
            dve.tensor_copy(e.wide3[:, :], ps[:, 4, :]).then_inc(e.state, 1)
            continue
        dve.wait_ge(e.state, c)
        for h in range(DH):
            s = e.wide3[:, h * P:(h + 1) * P]
            op = dve.scalar_tensor_tensor(s, s, g[:, G_DL, c, h:h + 1], ps[:, 4, h * P:(h + 1) * P], ALU.mult, ALU.add)
        op.then_inc(e.state, 1)
    dve.wait_ge(e.o_roots, 1)
    dve.reciprocal(g[:, G_SK], g[:, G_SQ]).then_inc(e.o_gates, 1)
    dve.wait_ge(e.o_dn_set, NBLK + 1)
    for c, (t0, n) in enumerate(BLOCKS):
        dve.wait_ge(e.o_spread, c + 1)
        out = e.o_dn[:, :, t0:t0 + n]
        dve.tensor_tensor(out, out, heads_view(ps[:, c % 2, :], P, n), ALU.mult).then_inc(e.o_normed, 1)
    dve.wait_ge(e.o_normed, NBLK + 1)
    dve.wait_ge(e.z_silu, DH)
    weight = k.vec_cols[:, VEC_ROWS - 1:VEC_ROWS]
    for h in range(DH):
        dve.scalar_tensor_tensor(e.o_dn[:, h, :], e.o_dn[:, h, :], weight, e.proj[:, Z_TILE + h, :], ALU.mult,
                                 ALU.mult).then_inc(e.o_full, 1)
    for kt in range(DT):
        dve.wait_ge(k.x_hi, mix.x0 + kt + 1)
        tile = e.o_swa[:, kt, :] if kt < 4 else e.o_dn[:, kt - 4, :]
        dve.tensor_tensor(k.x_hl[:, 1, kt, :], tile, k.x_hl[:, 0, kt, :].bitcast(F32), ALU.subtract).then_inc(k.x_lo, 1)



GQ, GK, GV, GG, GATE_LOW = 0, 4, 8, 16, 24
VD = 2 * P
NORM_GATE = 16.0
CHUNKS = [(0, 0, 0, META)] + [(1 + s // 2, CH * (s % 2), META + s * CH, CH) for s in range(SEQ // CH)]


class Odd:

    def __init__(self, core):
        at, a, x = core.at, core.arena, core.x_at
        tile = 4 * TOK
        self.proj = at("odd_proj", [P, ODD_TILES + 1, TOK], a)
        free = a + (ODD_TILES + 1) * tile
        self.ex = at("gla_ex", [P, 6, TOK], free)
        self.squares = at("gla_squares", [P, 2, 2 * GH, P], free)
        self.diag = at("gla_diag", [P, 2, GH * P], free + 8192)
        self.k_grow = at("gla_k_grow", [P, GH, TOK], free + 6 * tile)
        self.attn = at("gla_attn", [P, NBLK, GH, P], free + 10 * tile)
        self.state = at("gla_state", [P, 2, GH, VD], free + 10 * tile + 8192)
        self.keep = at("gla_keep", [P, TOK], free + 10 * tile + 16384)
        self.cols = at("gla_cols", [P, 2 * NBLK * GH + GH * len(CHUNKS)], free + 11 * tile + 16384)
        self.v_rows = at("gla_v_rows", [P, NBLK + 1, GH * VD], x)
        self.k_rows = at("gla_k_rows", [P, NBLK + 1, GH * P], x + 4 * (NBLK + 1) * GH * VD)
        self.gate_up = at("gla_gate_up", [RANK, GH * P], x + 4 * (NBLK + 1) * GH * (VD + P))
        self.mask = at("gla_mask", [P, P], x + 4 * (NBLK + 1) * GH * (VD + P) + 4 * GH * P)
        self.decay = self.cols[:, 2 * NBLK * GH:].rearrange("p (h s) -> p h s", h=GH)
        self.roots = self.cols[:, 0:NBLK * GH].rearrange("p (c h) -> p c h", h=GH)
        self.inverse = self.cols[:, NBLK * GH:2 * NBLK * GH].rearrange("p (c h) -> p c h", h=GH)
        self.s_in = core.sem("o_in")
        self.s_gate_lin = core.sem("o_gate_lin")
        self.s_gate_x = core.sem("o_gate_x")
        self.s_gate_neg = core.sem("o_gate_neg")
        self.s_gate_exp = core.sem("o_gate_exp")
        self.s_gate_log = core.sem("o_gate_log")
        self.s_gate_min = core.sem("o_gate_min")
        self.s_cum = core.sem("o_cum")
        self.s_kd_arg = core.sem("o_kd_arg")
        self.s_grown = core.sem("o_grown")
        self.s_q_dec = core.sem("o_q_dec")
        self.s_k_grow = core.sem("o_k_grow")
        self.s_k_dec = core.sem("o_k_dec")
        self.s_v_flip = core.sem("o_v_flip")
        self.s_v_set = core.sem("o_v_set")
        self.s_k_flip = core.sem("o_k_flip")
        self.s_k_set = core.sem("o_k_set")
        self.s_attn_made = core.sem("o_attn_made")
        self.s_attn_set = core.sem("o_attn_set")
        self.s_kv_made = core.sem("o_kv_made")
        self.s_state = core.sem("o_state")
        self.s_o_made = core.sem("o_o_made")
        self.s_o_sq = core.sem("o_o_sq")
        self.s_o_set = core.sem("o_o_set")
        self.s_o_sums = core.sem("o_o_sums")
        self.s_o_roots = core.sem("o_o_roots")
        self.s_o_inverse = core.sem("o_o_inverse")
        self.s_diag_set = core.sem("o_diag_set")
        self.s_diag_used = core.sem("o_diag_used")
        self.s_o_normed = core.sem("o_o_normed")
        self.s_g_silu = core.sem("o_g_silu")
        self.s_o_full = core.sem("o_o_full")


def odd_gpsimd(core, pool, mix, a):
    k, o = core, core.odd
    pool.wait_ge(k.slot_used, mix.slots)
    pool.dma_start(o.gate_up[:, :], a["gla_w_gate_up"][0]).then_inc(o.s_in, 16)
    pool.dma_start(o.keep[:, :], a["scan_keep"]).then_inc(o.s_in, 16)
    pool.dma_start(o.mask[:, :], a["masks"][:, C_GLA:C_GLA + P]).then_inc(o.s_in, 16)
    pool.wait_ge(o.s_o_inverse, 1)
    for c in range(NBLK):
        if c >= 2:
            pool.wait_ge(o.s_diag_used, c - 1)
        pool.tensor_tensor(heads_view(o.diag[:, c % 2, :], P, P), over_heads(k.ident[:, :], P, P),
                           along(o.inverse[:, c], P, P), ALU.mult).then_inc(o.s_diag_set, 1)


def odd_tensor(core, pe, mix):
    k, o = core, core.odd
    ps, proj = k.psum, o.proj
    pe.wait_ge(k.scaled, mix.evac0)
    pe.wait_ge(o.s_in, 48)
    for h in range(GH):
        for b, (t0, n) in enumerate(halves(FULL)):
            op = pe.matmul(ps[:, 2 * h + b, 0:n], o.gate_up[:, h * P:(h + 1) * P], proj[0:RANK, GATE_LOW, t0:t0 + n],
                           start=True, stop=True)
        op.then_inc(o.s_gate_lin, 1)
    pe.wait_ge(o.s_gate_x, GH)
    for c, (t0, n) in enumerate(BLOCKS):
        if c >= 2:
            pe.wait_ge(o.s_v_set, c - 1)
        for j in range(2 * GH):
            op = pe.transpose(ps[0:n, 2 * (c % 2) + j // 4, (j % 4) * P:(j % 4 + 1) * P], proj[:, GV + j, t0:t0 + n],
                              k.ident[:])
        op.then_inc(o.s_v_flip, 1)
    pe.wait_ge(o.s_k_dec, GH)
    for c, (t0, n) in enumerate(BLOCKS):
        if c >= 2:
            pe.wait_ge(o.s_k_set, c - 1)
        for h in range(GH):
            op = pe.transpose(ps[0:n, 4 + c % 2, h * P:(h + 1) * P], proj[:, GK + h, t0:t0 + n], k.ident[:])
        op.then_inc(o.s_k_flip, 1)
        if c == 0:
            continue
        if c > 2:
            pe.wait_ge(o.s_attn_set, c - 2)
        for h in range(GH):
            op = pe.matmul(ps[:, 6 + c % 2, h * P:(h + 1) * P], o.k_grow[:, h, t0:t0 + n], proj[:, GQ + h, t0:t0 + n],
                           start=True, stop=True)
        op.then_inc(o.s_attn_made, 1)
    pe.wait_ge(o.s_v_set, NBLK + 1)
    pe.wait_ge(o.s_k_set, NBLK + 1)

    def sums(c):
        pe.wait_ge(o.s_o_sq, 2 * c)
        for h in range(GH):
            for j in range(2):
                op = pe.matmul(ps[:, 6, (c - 1) * GH + h:(c - 1) * GH + h + 1], o.squares[:, c % 2, 2 * h + j, :],
                               k.ones[:, 0:1], start=j == 0, stop=j == 1)
        op.then_inc(o.s_o_sums, 1)

    for s, (c, r0, t0, n) in enumerate(CHUNKS):
        rows = slice(r0, r0 + n)
        if s < len(CHUNKS) - 1:
            if s >= 2:
                pe.wait_ge(o.s_state, s - 1)
            for h in range(GH):
                out = ps[:, 2 * (s % 2) + h // 2, (h % 2) * VD:(h % 2 + 1) * VD]
                op = pe.matmul(out, o.k_rows[rows, c, h * P:(h + 1) * P], o.v_rows[rows, c, h * VD:(h + 1) * VD],
                               start=True, stop=True)
            op.then_inc(o.s_kv_made, 1)
        if s == 0:
            continue
        if s == 1:
            pe.wait_ge(o.s_attn_set, NBLK)
        if s > 2:
            pe.wait_ge(o.s_o_set, s - 2)
        pe.wait_ge(o.s_state, s)
        for j in range(2 * GH):
            h = j // 2
            out = ps[:, 4 + s % 2, j * CH:(j + 1) * CH]
            pe.matmul(out, o.state[:, s % 2, h, (j % 2) * P:(j % 2 + 1) * P], proj[:, GQ + h, t0:t0 + n], start=True,
                      stop=False)
            op = pe.matmul(out, o.v_rows[rows, c, j * P:(j + 1) * P], o.attn[rows, c - 1, h, r0:r0 + n], start=False,
                           stop=True)
        op.then_inc(o.s_o_made, 1)
        if s % 2 == 1 and s > 1:
            sums((s - 1) // 2)
    sums(NBLK)
    for c in range(NBLK):
        pe.wait_ge(o.s_diag_set, c + 1)
        if c >= 2:
            pe.wait_ge(o.s_o_normed, c - 1)
        pe.matmul(ps[:, c % 2, :], k.ones[:], o.diag[:, c % 2, :], start=True, stop=True).then_inc(o.s_diag_used, 1)


def chunk_ends(tile):
    return tile[:, META:TOK].rearrange("p (s t) -> p s t", t=CH)[:, :, CH - 1:CH]


def odd_scalar(core, act, mix):
    k, o = core, core.odd
    ps, proj = k.psum, o.proj
    for h in range(GH):
        act.wait_ge(o.s_gate_lin, h + 1)
        act.activation(token_cols(o.ex[:, h, :], FULL), bank_cols(k, h, FULL), ACT.Identity,
                       bias=k.vec_cols[:, 48 + h:49 + h]).then_inc(o.s_gate_x, 1)
    for pair in range(GH // 2):
        heads = (2 * pair, 2 * pair + 1)
        for h in heads:
            u = o.ex[:, 4 + h % 2, :]
            act.wait_ge(o.s_gate_neg, h + 1)
            act.activation(u, u, ACT.Exp).then_inc(o.s_gate_exp, 1)
        for h in heads:
            u = o.ex[:, 4 + h % 2, :]
            act.wait_ge(o.s_gate_exp, h + 1)
            act.activation(u, u, ACT.Ln, bias=k.ones[:, 0:1]).then_inc(o.s_gate_log, 1)
        if pair == 0:
            for c in (0, 1):
                value_rows(k, o, act, c)
        for h in heads:
            cum, scale = o.ex[:, h, :], 1.0 / NORM_GATE
            act.wait_ge(o.s_cum, h + 1)
            if h >= 2:
                act.wait_ge(o.s_q_dec, h - 1)
            act.activation((k.t_up if h % 2 else k.t_gate)[:, :], cum, ACT.Exp, scale=scale)
            act.activation(o.k_grow[:, h, :], cum, ACT.Exp, scale=-scale)
            act.activation(o.decay[:, h, 0:1], cum[:, META - 1:META], ACT.Exp, scale=scale)
            act.activation(o.decay[:, h, 1:].unsqueeze(2), chunk_ends(cum), ACT.Exp, scale=scale)
            act.wait_ge(o.s_kd_arg, h + 1)
            u = o.ex[:, 4 + h % 2, :]
            act.activation(u, u, ACT.Exp, scale=scale).then_inc(o.s_grown, 1)
        for c in ((2, 3) if pair == 0 else (4,)):
            value_rows(k, o, act, c)
    for c, (t0, n) in enumerate(BLOCKS):
        act.wait_ge(o.s_k_flip, c + 1)
        act.activation(o.k_rows[0:n, c, :], ps[0:n, 4 + c % 2, :], ACT.Copy).then_inc(o.s_k_set, 1)
    for j in range(2 * GH):
        g = proj[:, GG + j, META:TOK]
        act.activation(g, g, ACT.Silu).then_inc(o.s_g_silu, 1)
    for s, (c, r0, t0, n) in enumerate(CHUNKS):
        if s == 0:
            continue
        act.wait_ge(o.s_o_made, s)
        if s > 4:
            act.wait_ge(o.s_o_sums, (s - 1) // 2 - 1)
        src = ps[:, 4 + s % 2, :].rearrange("p (j t) -> p j t", t=CH)
        act.activation(o.squares[:, c % 2, :, r0:r0 + n], src, ACT.Square).then_inc(o.s_o_sq, 1)
        act.activation(proj[:, GV:GV + 2 * GH, t0:t0 + n], src, ACT.Copy).then_inc(o.s_o_set, 1)
    act.wait_ge(o.s_o_sums, NBLK)
    act.activation(o.roots, ps[:, 6, 0:NBLK * GH].rearrange("p (c h) -> p c h", h=GH), ACT.Sqrt, bias=k.eps[:, 0:1],
                   scale=1.0 / VD).then_inc(o.s_o_roots, 1)
    for kt in range(DT):
        act.wait_ge(o.s_o_full, kt + 1)
        act.activation(k.x_hl[:, 0, kt, META:TOK], proj[:, GV + kt, META:TOK], ACT.Copy).then_inc(k.x_hi, 1)


def value_rows(k, o, act, c):
    n = BLOCKS[c][1]
    act.wait_ge(o.s_v_flip, c + 1)
    act.activation(o.v_rows[0:n, c, :].rearrange("p (b q) -> p b q", b=2), k.psum[0:n, 2 * (c % 2):2 * (c % 2) + 2, :],
                   ACT.Copy).then_inc(o.s_v_set, 1)


def odd_vector(core, dve, mix):
    k, o = core, core.odd
    ps, proj = k.psum, o.proj
    dve.wait_ge(o.s_in, 48)
    for pair in range(GH // 2):
        heads = (2 * pair, 2 * pair + 1)
        for h in heads:
            x, u = o.ex[:, h, :], o.ex[:, 4 + h % 2, :]
            dve.wait_ge(o.s_gate_x, h + 1)
            if pair:
                dve.wait_ge(o.s_k_dec, h - 1)
            dve.scalar_tensor_tensor(u, x, -1.0, x, ALU.mult, ALU.min).then_inc(o.s_gate_neg, 1)
        for h in heads:
            x, u = o.ex[:, h, :], o.ex[:, 4 + h % 2, :]
            dve.wait_ge(o.s_gate_log, h + 1)
            dve.scalar_tensor_tensor(x, x, 0.0, u, ALU.min, ALU.subtract).then_inc(o.s_gate_min, 1)
        for h in heads:
            x, u = o.ex[:, h, :], o.ex[:, 4 + h % 2, :]
            dve.wait_ge(o.s_gate_min, h + 1)
            dve.tensor_tensor_scan(x, o.keep[:, :], x, 0.0, ALU.mult, ALU.add).then_inc(o.s_cum, 1)
            dve.wait_ge(o.s_cum, h + 1)
            dve.tensor_tensor(u[:, 0:META], x[:, META - 1:META].broadcast_to([P, META]), x[:, 0:META], ALU.subtract)
            rest = u[:, META:TOK].rearrange("p (s t) -> p s t", t=CH)
            cum = x[:, META:TOK].rearrange("p (s t) -> p s t", t=CH)
            dve.tensor_tensor(rest, chunk_ends(x).broadcast_to([P, SEQ // CH, CH]), cum, ALU.subtract)\
                .then_inc(o.s_kd_arg, 1)
        for h in heads:
            dve.wait_ge(o.s_grown, h + 1)
            q, key = proj[:, GQ + h, :], proj[:, GK + h, :]
            dve.scalar_tensor_tensor(q, q, float(P) ** -0.5, (k.t_up if h % 2 else k.t_gate)[:, :], ALU.mult, ALU.mult)\
                .then_inc(o.s_q_dec, 1)
            grow = o.k_grow[:, h, :]
            dve.tensor_tensor(grow, grow, key, ALU.mult).then_inc(o.s_k_grow, 1)
            dve.wait_ge(o.s_k_grow, h + 1)
            dve.tensor_tensor(key, key, o.ex[:, 4 + h % 2, :], ALU.mult).then_inc(o.s_k_dec, 1)
    for c in range(1, NBLK + 1):
        dve.wait_ge(o.s_attn_made, c)
        dve.tensor_tensor(o.attn[:, c - 1], heads_view(ps[:, 6 + c % 2, :], P, P), over_heads(o.mask[:, :], P, P),
                          ALU.mult).then_inc(o.s_attn_set, 1)
    dve.wait_ge(o.s_attn_set, NBLK)
    for s in range(len(CHUNKS) - 1):
        dve.wait_ge(o.s_kv_made, s + 1)
        kv = ps[:, 2 * (s % 2):2 * (s % 2) + 2, :].rearrange("p b (h v) -> p (b h) v", v=VD)
        to = o.state[:, (s + 1) % 2]
        if s == 0:
            dve.tensor_copy(to.rearrange("p (b h) v -> p b (h v)", b=2), ps[:, 0:2, :]).then_inc(o.s_state, 1)
            continue
        if s >= 2:
            dve.wait_ge(o.s_o_made, s - 1)
        dve.wait_ge(o.s_state, s)
        for h in range(GH):
            op = dve.scalar_tensor_tensor(to[:, h], o.state[:, s % 2, h], o.decay[:, h, s:s + 1],
                                          ps[:, 2 * (s % 2) + h // 2, (h % 2) * VD:(h % 2 + 1) * VD], ALU.mult, ALU.add)
        op.then_inc(o.s_state, 1)
    dve.wait_ge(o.s_o_roots, 1)
    dve.reciprocal(o.inverse, o.roots).then_inc(o.s_o_inverse, 1)
    dve.wait_ge(o.s_o_set, 2 * NBLK)
    for c in range(NBLK):
        dve.wait_ge(o.s_diag_used, c + 1)
        t0 = META + c * P
        out = proj[:, GV:GV + 2 * GH, t0:t0 + P].rearrange("p (h j) t -> p h j t", j=2)
        factor = heads_view(ps[:, c % 2, :], P, P).unsqueeze(2).broadcast_to([P, GH, 2, P])
        dve.tensor_tensor(out, out, factor, ALU.mult).then_inc(o.s_o_normed, 1)
    dve.wait_ge(o.s_o_normed, NBLK)
    dve.wait_ge(o.s_g_silu, 2 * GH)

    def gated(j):
        out = proj[:, GV + j, META:TOK]
        dve.scalar_tensor_tensor(out, out, k.vec_cols[:, 52 + j % 2:53 + j % 2], proj[:, GG + j, META:TOK], ALU.mult,
                                 ALU.mult).then_inc(o.s_o_full, 1)

    gated(0)
    for kt in range(DT):
        if kt + 1 < DT:
            gated(kt + 1)
        dve.wait_ge(k.x_hi, mix.x0 + kt + 1)
        dve.tensor_tensor(k.x_hl[:, 1, kt, META:TOK], proj[:, GV + kt, META:TOK],
                          k.x_hl[:, 0, kt, META:TOK].bitcast(F32), ALU.subtract).then_inc(k.x_lo, 1)


INPUTS = ["x", "meta_tokens", "norm_w", "ffn_w_gate", "ffn_w_up", "ffn_w_down", "rel_bias_table", "even_w_in",
          "even_conv_w", "swa_sinks", "dn_a_log", "dn_dt_bias", "dn_norm_w", "even_w_out", "odd_w_in",
          "gla_w_gate_up", "gla_b_gate", "gla_norm_w", "odd_w_out"]


def trunk(nc, a, stop=None):
    steps = linked(plan(stop))
    with ExitStack() as ctx:
        core = Core(nc, ctx, steps)
        block = ctx.enter_context(nc.Block())

        @block.sync
        def _(sp):
            sync_program(core, sp, a)

        @block.tensor
        def _(pe):
            tensor_program(core, pe)

        @block.scalar
        def _(act):
            scalar_program(core, act)

        @block.vector
        def _(dve):
            vector_program(core, dve)

        @block.gpsimd
        def _(pool):
            gpsimd_program(core, pool, a)


def kernel(**inputs):
    import concourse.bacc as bacc
    from concourse.bass_utils import run_bass_kernel_spmd

    nc = bacc.Bacc("TRN2", target_bir_lowering=False, num_devices=1)
    masks, hot, scan = shape_constants()
    arrays, args = {}, {}
    for name in INPUTS:
        arrays[name] = np.ascontiguousarray(inputs[name])
    arrays.update(masks=masks, bucket_hot=hot, scan_keep=scan)
    for name, array in arrays.items():
        args[name] = nc.dram_tensor(name, array.shape, mybir.dt.from_np(array.dtype), kind="ExternalInput").ap()
    args["bias_scratch"] = nc.dram_tensor("bias_scratch", (QH, V_ALL), F32, kind="Internal").ap()
    args["out"] = nc.dram_tensor("out", (1, SEQ, D), F32, kind="ExternalOutput").ap()
    trunk(nc, args)
    r = run_bass_kernel_spmd(nc, [arrays], core_ids=[0])
    return r.results[0]["out"]
```

```python
from contextlib import ExitStack

import numpy as np

import concourse.bass as bass
from concourse import mybir

ACT = mybir.ActivationFunctionType
ALU = mybir.AluOpType
AX = mybir.AxisListType
F32 = mybir.dt.float32
F32R = mybir.dt.float32r

P = 128
META = 16
SEQ = 512
TOK = META + SEQ
D = 1024
DT = D // P
FF = 2816
FT = FF // P
FH = FT // 2
EPS = 1e-6
MASKED = -1e30
BUCKETS = 32
MAX_DIST = 128
QH, KVH, HD = 8, 2, 64
GRP = QH // KVH
NBLK = SEQ // P
DH = 4
CONV = 4
GH = 4
CH = 64
RING = 4
AHEAD = 3
POOL_SCALES = 3
EVEN_TILES = 22
EVEN_GATES = 2 * DH
ODD_TILES = 24
RANK = 16
DN_DIM = 128
CONST_LOADS = 11
VEC_ROWS = CONV * 3 * DH + 4 + 2 + 1
HALF = TOK // 2
FULL = "full"
TAIL = "tail"

BAND_N = 3 * P - 1
META_N = P + META - 1
SELF_N = 2 * META - 1
V_BAND, V_NEAR, V_FAR, V_SELF = 0, BAND_N, BAND_N + META_N, BAND_N + 2 * META_N
V_ALL = V_SELF + SELF_N

LEVELS = 7
C_ID, C_FLIP, C_UP, C_ADD, C_LVL = 0, P, 2 * P, 3 * P, 4 * P
C_GLA = C_LVL + LEVELS * P
C_ALL = C_GLA + P


def shape_constants():
    j = np.arange(P)[:, None]
    i = np.arange(P)[None, :]
    masks = np.zeros((P, C_ALL), np.float32)
    masks[:, C_ID:C_ID + P] = i == j
    masks[:, C_FLIP:C_FLIP + P] = i + j == P - 1
    masks[:, C_UP:C_UP + P] = j <= i
    masks[:, C_ADD:C_ADD + P] = np.where(j <= i, 0.0, MASKED)
    for n in range(LEVELS):
        s = 1 << n
        level = (i // (2 * s) == j // (2 * s)) & ((i // s) % 2 == 1) & ((j // s) % 2 == 0)
        masks[:, C_LVL + n * P:C_LVL + (n + 1) * P] = level
    masks[:, C_GLA:C_GLA + P] = (j <= i) & (i // CH == j // CH)

    def bucket(n):
        exact = BUCKETS // 2
        far = np.log(np.maximum(n, 1).astype(np.float32) / np.float32(exact)) / np.float32(np.log(MAX_DIST / exact))
        far = np.minimum(exact + (far * np.float32(BUCKETS - exact)).astype(np.int32), BUCKETS - 1)
        return np.where(n < exact, n, far)

    hot = np.zeros((BUCKETS + 1, V_ALL), np.float32)

    def put(first, rel, valid):
        cols = first + np.arange(len(rel))
        hot[np.where(valid, bucket(np.maximum(rel, 0)), BUCKETS), cols] = 1.0

    rel = 2 * P - 1 - np.arange(BAND_N)
    put(V_BAND, rel, (rel >= 0) & (rel < P))
    rel = P + META - 1 - np.arange(META_N)
    put(V_NEAR, rel, rel >= 0)
    put(V_FAR, rel + P, rel >= 0)
    hot[:, V_FAR:V_FAR + META_N] = 0.0
    hot[BUCKETS - 1, V_FAR:V_FAR + META_N] = 1.0
    rel = META - 1 - np.arange(SELF_N)
    put(V_SELF, rel, rel >= 0)
    scan = np.ones((P, TOK), np.float32)
    scan[:, 0] = 0.0
    scan[:, META::CH] = 0.0
    return masks, hot, scan


class Phase:

    def __init__(self, kind, layer, slots, cols, before, ffn=None):
        self.kind, self.layer, self.slots, self.cols, self.ffn = kind, layer, slots, cols, ffn
        self.slot0 = before["slots"]
        self.evac0 = before["evac"]
        self.f0 = before["f"]
        self.x0 = before["x"]
        self.a0 = before["a"]
        before["slots"] += slots
        if kind in ("gu", "in"):
            before["evac"] += slots
        if kind == "gu":
            before["a"] += slots // 2
        if kind in ("down", "out"):
            before["f"] += DT


class Norm:

    def __init__(self, layer, post, pre, half, cols, h0, x0, sum0, pair, last, sum_pair):
        self.post_col = None if post is None else (6 * layer + post) * DT
        self.pre_col = None if pre is None else (6 * layer + pre) * DT
        self.half, self.cols, self.h0, self.x0, self.pair, self.last = half, cols, h0, x0, pair, last
        self.f0 = h0 - DT
        self.post_sum = None if post is None else sum0
        self.pre_sum = None if pre is None else sum0 + (post is not None)
        self.posts = max(h0 // DT - 1, 0)
        self.post_added = None if post is None else DT * sum0 - self.posts
        self.pre_added = None if pre is None else DT * self.pre_sum - (self.posts + (post is not None))
        self.sum_pair = sum_pair
        self.copy_pair = None if pre is None else (pair + RING - 1) % RING
        self.t0 = META if cols == TAIL else 0
        self.blocks, self.block = (SEQ // P, P) if cols == TAIL else (6, TOK // 6)


class Mix:

    def __init__(self, layer, x0, evac0, slots):
        self.layer, self.x0, self.evac0, self.slots = layer, x0, evac0, slots


def plan(stop=None):
    n = {"slots": 0, "evac": 0, "f": 0, "x": 0, "a": 0}
    steps = []
    norms = 0
    sums = 0

    def norm(layer, post, pre, half, cols, last=False):
        nonlocal norms, sums
        steps.append(("norm", Norm(layer, post, pre, half, cols, h0=norms * DT, x0=n["x"], sum0=sums,
                                   pair=(n["slots"] + RING - 1) % RING, last=last,
                                   sum_pair=(n["slots"] + (RING - 1 if half else RING - 2)) % RING)))
        norms += 1
        sums += (post is not None) + (pre is not None)
        if pre is not None:
            n["x"] += DT

    norm(0, None, 0, False, FULL)
    for layer in range(2):
        cols = FULL
        for ffn in range(2):
            if ffn:
                cols = TAIL if layer else FULL
            steps.append(("dense", Phase("gu", layer, 2 * FT, cols, n, ffn=ffn)))
            steps.append(("dense", Phase("down", layer, 2 * DT, cols, n, ffn=ffn)))
            if stop == (layer, ffn):
                norm(layer, 1 if ffn == 0 else 5, None, True, cols, last=True)
                return steps
            if ffn:
                norm(layer, 5, None if layer else 6, True, cols, last=bool(layer))
                continue
            norm(layer, 1, 2, True, cols)
            steps.append(("dense", Phase("in", layer, (ODD_TILES if layer else EVEN_TILES) + 1, FULL, n)))
            steps.append(("mix", Mix(layer, n["x"], n["evac"], n["slots"])))
            n["x"] += DT
            steps.append(("dense", Phase("out", layer, DT, TAIL if layer else FULL, n)))
            if stop == (layer, "mix"):
                norm(layer, 3, None, False, TAIL if layer else FULL, last=True)
                return steps
            norm(layer, 3, 4, False, TAIL if layer else FULL)
    return steps


def halves(cols):
    if cols == TAIL:
        return [(META, SEQ)]
    return [(0, HALF), (HALF, HALF)]


def token_cols(tile, cols):
    if cols == TAIL:
        return tile[:, META:TOK]
    return tile.rearrange("p (a b) -> p a b", a=2)


def linked(steps):
    queries = [s.slot0 for k, s in steps if k == "dense" and s.kind == "in" and s.layer == 0]
    twice = [first + t for first in queries for t in range(QH // KVH)]
    inverses = 0
    for at, (kind, step) in enumerate(steps):
        if kind == "norm" and step.pre_sum is not None:
            step.next = steps[at + 1][1]
            step.inverses = inverses
            inverses += 1
        if kind == "dense":
            step.before = next((s for k, s in reversed(steps[:at]) if k == "norm"), None)
            step.twice = twice
            step.mix = steps[at + 1][1] if step.kind == "in" and step.layer == 0 else None
            step.after = next((s for k, s in steps[at:] if k == "norm"), None)
    return steps


class Core:

    def __init__(self, nc, ctx, steps):
        self.nc, self.steps = nc, steps
        self.phases = [s for kind, s in steps if kind == "dense"]
        last = [s for kind, s in steps if kind == "norm"][-1]
        self.h_total = last.h0 + DT

        def sb(name, shape, dt=F32):
            return ctx.enter_context(nc.sbuf_tensor(name, shape, dt))

        def sem(name):
            return ctx.enter_context(nc.semaphore(name))

        self.h = sb("h", [P, DT, TOK])
        self.w_hl = sb("w_hl", [P, RING, 2, FH * P], F32R)
        self.stage = sb("stage", [P, 2, FH * P])
        self.rinv = sb("rinv", [P, TOK])
        self.sq_sum = sb("sq_sum", [P, TOK])
        self.t_gate = sb("t_gate", [P, TOK])
        self.t_up = sb("t_up", [P, TOK])
        self.ident = sb("ident", [P, P])
        self.ones = sb("ones", [P, P])
        self.norm_cols = sb("norm_cols", [P, 12 * DT])
        self.vec_cols = sb("vec_cols", [P, 64])
        self.heads = sb("heads", [P, QH + 2 * DH])
        self.eps = sb("eps", [P, 4])
        self.by_token = sb("by_token", [P, 2, 6])
        self.x_at = (nc.sbuf_base + 31) // 32 * 32
        self.x_hl = sb("x_hl", [P, 2, DT, TOK], F32R)
        self.arena = (nc.sbuf_base + 31) // 32 * 32
        self.acts = sb("acts", [P, 2, FT, TOK], F32R)
        self.psum = ctx.enter_context(nc.psum_tensor("psum", [P, 8, 512], F32))
        self.f_down = self.at("f_down", [P, DT, TOK], self.x_at)
        self.f_mix = self.at("f_mix", [P, DT, TOK], self.arena)
        at = self.arena
        def rows_at(name, rows, width):
            nonlocal at
            buf = self.at(name, [rows, width], at)
            at += (4 * width + 31) // 32 * 32
            return buf

        self.rows_x = rows_at("rows_x", P, NBLK * D)
        self.rows_meta = rows_at("rows_meta", META, D)
        self.rows_norm = rows_at("rows_norm", 12 * DT, P)
        self.rows_vec = rows_at("rows_vec", VEC_ROWS, P)
        self.table = rows_at("table", BUCKETS + 1, QH)
        self.bucket_hot = rows_at("bucket_hot", BUCKETS + 1, V_ALL)
        self.bias_row = rows_at("bias_row", QH, V_ALL)
        self.rows_x = self.rows_x[:].rearrange("p (b d) -> p b d", b=NBLK)
        self.rows_out = self.at("rows_out", [P, NBLK, D], self.arena)

        self.w_hi = sem("w_hi")
        self.w_lo = sem("w_lo")
        self.slot_used = sem("slot_used")
        self.scaled = sem("scaled")
        self.gate_silu = sem("gate_silu")
        self.act_full = sem("act_full")
        self.act_hi = sem("act_hi")
        self.act_lo = sem("act_lo")
        self.f_out = sem("f_out")
        self.sq_made = sem("sq_made")
        self.sq_added = sem("sq_added")
        self.sum_ready = sem("sum_ready")
        self.root_ready = sem("root_ready")
        self.rinv_ready = sem("rinv_ready")
        self.f_scaled = sem("f_scaled")
        self.f_scaled_pool = sem("f_scaled_pool")
        self.inverse_ready = sem("inverse_ready")
        self.spread_set = sem("spread_set")
        self.spread_ready = sem("spread_ready")
        self.spread_copied = sem("spread_copied")
        self.table_set = sem("table_set")
        self.h_new = sem("h_new")
        self.x_hi = sem("x_hi")
        self.x_lo = sem("x_lo")
        self.consts_in = sem("consts_in")
        self.consts_set = sem("consts_set")
        self.cols_ready = sem("cols_ready")
        self.cols_flip = sem("cols_flip")
        self.tok_in = sem("tok_in")
        self.tok_flip = sem("tok_flip")
        self.bias_stored = sem("bias_stored")
        self.out_flip = sem("out_flip")
        self.out_left = sem("out_left")
        self.out_right = sem("out_right")
        self.out_stored = sem("out_stored")
        self.w_landed = [sem("w_landed_0"), sem("w_landed_1")]
        self.sem = sem
        self.tables = 0
        self.even = Even(self)
        self.odd = Odd(self)
        self.proj = [self.even.proj, self.odd.proj]

    def at(self, name, shape, offset, dt=F32):
        return self.nc.alloc_sbuf_tensor_at(name, shape, dt, offset=offset)

    def slot_kind(self, g):
        for p in self.phases:
            if p.slot0 <= g < p.slot0 + p.slots:
                if p.kind == "in" and g == p.slot0 + p.slots - 1:
                    return DT, RANK if p.layer else EVEN_GATES
                return (FH if p.kind == "down" else DT), P
        return None


class Slot:

    def __init__(self, phase, i, u, off=0):
        self.i, self.u, self.off = i, u, off
        self.base = phase.slot0 + u + off
        self.local = i * RING + (u + off)
        self.ring = self.base % RING
        self.stage = self.base % 2
        self.pair = self.ring
        self.peeled = isinstance(i, int)
        if phase.mix is not None and self.peeled and self.local >= RING:
            self.pair = 1 if self.local == RING + 1 else 0
        self.twice = phase.twice

    def count(self, lag=0):
        return self.i * RING + (self.base + 1 - lag)

    def landed(self):
        first = self.base + RING * (self.i if self.peeled else 1)
        twice = [g for g in self.twice if g <= first and g % 2 == self.stage]
        return self.i * (16 * RING // 2) + 16 * (self.base // 2 + 1 + len(twice))


def walk(core, phase, engine, step, ahead=0, between=None):
    if between is not None and phase.mix is not None:
        for s in range(phase.slots):
            step(s // RING, s % RING)
            between(core, engine, phase.mix, s)
        return
    whole = phase.slots - (1 if phase.kind == "in" else 0)
    bodies = (whole - ahead) // RING
    for u in range(RING):
        step(0, u)
    if bodies > 2:
        with engine.Fori(1, bodies) as i:
            for u in range(RING):
                step(i, u)
    else:
        bodies = 1
    for s in range(bodies * RING, phase.slots):
        step(s // RING, s % RING)


def weights(buf, tiles, cols):
    view = buf.rearrange("p (k n) -> p k n", n=P)[:, 0:tiles, :]
    return view if cols == P else view[:, :, 0:cols]


def split_hi(core, act, slot, kind):
    act.wait_ge(core.w_landed[slot.stage], slot.landed())
    if not slot.peeled or slot.count() > RING:
        act.wait_ge(core.slot_used, slot.count(RING))
    act.activation(weights(core.w_hl[:, slot.ring, 0, :], *kind), weights(core.stage[:, slot.stage, :], *kind),
                   ACT.Copy).then_inc(core.w_hi, 1)


def split_lo(core, dve, slot, kind):
    dve.wait_ge(core.w_hi, slot.count())
    dve.tensor_tensor(weights(core.w_hl[:, slot.ring, 1, :], *kind), weights(core.stage[:, slot.stage, :], *kind),
                      weights(core.w_hl[:, slot.ring, 0, :].bitcast(F32), *kind), ALU.subtract).then_inc(core.w_lo, 1)


def split_ahead(core, engine, half, phase, i, u):
    slot = Slot(phase, i, u, AHEAD)
    g = phase.slot0 + (i * RING if isinstance(i, int) else RING) + u + AHEAD
    kind = core.slot_kind(g)
    if kind:
        half(core, engine, slot, kind)



def sync_program(core, sp, a):
    sp.dma_start(core.rows_x, a["x"][0].rearrange("(b p) d -> p b d", p=P)).then_inc(core.tok_in, 16)
    sp.dma_start(core.rows_meta[:, :], a["meta_tokens"]).then_inc(core.tok_in, 16)
    for kind, phase in core.steps:
        if kind == "dense":
            walk(core, phase, sp, lambda i, u, ph=phase: load_slot(core, sp, a, ph, i, u))
    for b in range(NBLK):
        sp.wait_ge(core.out_left, b + 1)
        sp.wait_ge(core.out_right, b + 1)
        sp.dma_start(a["out"][0, b * P:(b + 1) * P, :], core.rows_out[:, b, :]).then_inc(core.out_stored, 16)
    sp.wait_ge(core.out_stored, 16 * NBLK)


def load_slot(core, sp, a, phase, i, u):
    slot = Slot(phase, i, u)
    if not slot.peeled or slot.count() > 2:
        sp.wait_ge(core.w_lo, slot.count(2))
    dst = core.stage[:, slot.stage, :]
    if phase.kind == "gu":
        w = (a["ffn_w_up"] if u % 2 else a["ffn_w_gate"])[phase.layer, phase.ffn]
        col, n, rows = (i * 2 + u // 2) * P, P, w
    elif phase.kind == "down":
        w = a["ffn_w_down"][phase.layer, phase.ffn]
        half = u % 2
        col, n, rows = (i * 2 + u // 2) * P, P, w[half * FH * P:(half + 1) * FH * P]
    else:
        rows = {("in", 0): a["even_w_in"], ("in", 1): a["odd_w_in"],
                ("out", 0): a["even_w_out"], ("out", 1): a["odd_w_out"]}[phase.kind, phase.layer][0]
        col, n = slot.local * P, P
        if phase.kind == "in" and slot.peeled and slot.local == phase.slots - 1:
            n = RANK if phase.layer else EVEN_GATES
    tiles = FH if phase.kind == "down" else DT
    dst = weights(dst, tiles, n)
    if phase.kind == "in" and phase.layer == 0 and slot.peeled and slot.local < QH // KVH:
        src = rows[:, 0:QH * HD].rearrange("(k p) (g h d) -> h p k g d", p=P, g=KVH, d=HD)[slot.local]
        dst = dst.rearrange("p k (g d) -> p k g d", g=KVH)
        for g in range(KVH):
            sp.dma_start(dst[:, :, g, :], src[:, :, g, :]).then_inc(core.w_landed[slot.stage], 16)
        return
    src = rows[:, bass.ds(col, n)].rearrange("(k p) n -> p k n", p=P)
    sp.dma_start(dst, src).then_inc(core.w_landed[slot.stage], 16)



def products(core, pe, phase, slot, kt, w_tile, moving, first, last):
    for part, moved in ((0, 0), (0, 1), (1, 0)):
        lhs = core.w_hl[:, slot.ring, part, w_tile * P:(w_tile + 1) * P]
        for b, (t0, n) in enumerate(halves(phase.cols)):
            out = core.psum[:, 2 * slot.out_pair + b, 0:n]
            op = pe.matmul(out, lhs, moving[:, moved, kt, t0:t0 + n], start=first and part + moved == 0,
                           stop=last and part == 1)
    return op


def tensor_dense(core, pe, phase):
    k = core

    def weights_ready(slot):
        pe.wait_ge(k.w_lo, slot.count())

    if phase.kind == "down":
        def step(i, u):
            slot = Slot(phase, i, u)
            slot.out_pair = (phase.slot0 + u - u % 2) % RING
            m = i * 2 + u // 2
            weights_ready(slot)
            if u % 2 == 0:
                if isinstance(i, int) and i == 0:
                    pe.wait_ge(k.scaled, phase.evac0 - RING + 1 + u)
                else:
                    pe.wait_ge(k.f_out, m + (phase.f0 - 1))
            for kk in range(FH):
                kt = (u % 2) * FH + kk
                if isinstance(i, int) and i == 0 and u < 2:
                    pe.wait_ge(k.act_lo, phase.a0 - FT + kt + 1)
                op = products(k, pe, phase, slot, kt, kk, k.acts, kt == 0, kt == FT - 1)
            op.then_inc(k.slot_used, 1)

        walk(k, phase, pe, step)
        return

    early = phase.kind != "out"
    if early:
        if phase.before.post_sum is not None:
            pe.wait_ge(k.spread_copied, phase.before.posts + 1)
        group = [Slot(phase, 0, u) for u in range(RING - 1)]
        for slot in group:
            weights_ready(slot)
            slot.out_pair = slot.pair
        for kt in range(DT):
            pe.wait_ge(k.x_lo, phase.x0 - DT + kt + 1)
            for slot in group:
                op = products(k, pe, phase, slot, kt, kt, k.x_hl, kt == 0, kt == DT - 1)
                if kt == DT - 1:
                    op.then_inc(k.slot_used, 1)
        if phase.before.post_sum is not None:
            pe.wait_ge(k.f_scaled, phase.before.posts * (DT - POOL_SCALES) + DT - POOL_SCALES)
        token_sum(k, pe, phase.before, phase.before.pre_sum)
    else:
        pe.wait_ge(k.x_lo, phase.x0)

    def step(i, u):
        if early and isinstance(i, int) and i == 0 and u < RING - 1:
            return
        slot = Slot(phase, i, u)
        slot.out_pair = slot.pair
        weights_ready(slot)
        if early and isinstance(i, int) and i == 0:
            pe.wait_ge(k.root_ready, phase.before.pre_sum + 1)
        elif not (isinstance(i, int) and i == 0):
            if phase.mix is not None:
                last = slot.local - 1 if slot.local > RING + 1 else slot.local - RING
                if slot.local == RING + 2:
                    last = RING
                pe.wait_ge(k.scaled, phase.evac0 + last + 1)
            elif phase.kind == "out":
                pe.wait_ge(k.f_out, i * RING + (u + phase.f0 - RING + 1))
            else:
                pe.wait_ge(k.scaled, i * RING + (u + phase.evac0 - RING + 1))
        for kt in range(DT):
            op = products(k, pe, phase, slot, kt, kt, k.x_hl, kt == 0, kt == DT - 1)
        op.then_inc(k.slot_used, 1)

    walk(k, phase, pe, step, between=even_tensor_between)


def token_sum(core, pe, norm, n):
    pe.wait_ge(core.sq_added, norm.pre_added + DT)
    for b, (t0, w) in enumerate(halves(norm.cols)):
        op = pe.matmul(core.psum[:, 2 * norm.pair + b, 0:w], core.ones[:], core.sq_sum[:, t0:t0 + w],
                       start=True, stop=True)
    op.then_inc(core.sum_ready, 1)


def token_factors(core, pe, norm):
    k, n = core, norm.post_sum
    squares = (k.sq_sum, k.t_up)
    pe.wait_ge(k.f_out, norm.f0 + (DT if norm.half else DT - 1))
    for part, buf in enumerate(squares):
        if part == 0:
            pe.wait_ge(k.sq_added, norm.post_added + DT - 1)
        else:
            pe.wait_ge(k.sq_made, DT * (n + 1))
        for c in range(norm.blocks):
            t0 = norm.t0 + c * norm.block
            at = part * norm.blocks + c
            op = pe.matmul(k.psum[0:norm.block, 2 * norm.sum_pair, at:at + 1], buf[:, t0:t0 + norm.block],
                           k.ones[:, 0:1], start=True, stop=True)
    op.then_inc(k.sum_ready, 1)
    pe.wait_ge(k.spread_set, norm.posts + 1)
    pe.wait_ge(k.f_out, norm.f0 + DT)
    cols = norm.blocks * norm.block
    for pair in (norm.pair, norm.copy_pair):
        if pair is None:
            break
        for b, (t0, w) in enumerate(halves(norm.cols)):
            at = b * cols // len(halves(norm.cols))
            op = pe.matmul(k.psum[:, 2 * pair + b, 0:w], k.ones[0:norm.block, :], k.t_gate[0:norm.block, at:at + w],
                           start=True, stop=True)
        op.then_inc(k.spread_ready, 1)


def tensor_program(core, pe):
    k = core
    pe.wait_ge(k.consts_set, 5)
    pe.wait_ge(k.consts_in, 16 * CONST_LOADS)
    pe.transpose(k.psum[:, 0, 0:12 * DT], k.rows_norm[0:12 * DT, :], k.ident[0:12 * DT, 0:12 * DT])
    pe.transpose(k.psum[:, 1, 0:VEC_ROWS], k.rows_vec[0:VEC_ROWS, :], k.ident[0:VEC_ROWS, 0:VEC_ROWS])
    pe.matmul(k.psum[0:QH, 2, 0:512], k.table[:], k.bucket_hot[:, 0:512], start=True, stop=True)
    pe.matmul(k.psum[0:QH, 3, 0:V_ALL - 512], k.table[:], k.bucket_hot[:, 512:V_ALL], start=True,
              stop=True).then_inc(k.cols_flip, 1)
    pe.wait_ge(k.tok_in, 32)
    for kt in range(DT):
        pair = (kt + 2) % RING
        if kt >= 2:
            pe.wait_ge(k.h_new, max(kt - RING + 1, 1))
            pe.wait_ge(k.cols_ready, 4)
        pe.transpose(k.psum[:, 2 * pair, 0:META], k.rows_meta[0:META, kt * P:(kt + 1) * P], k.ident[0:META, 0:META])
        for b in range(NBLK):
            at = META + b * P if b < 2 else (b - 2) * P
            op = pe.transpose(k.psum[:, 2 * pair + b // 2, at:at + P], k.rows_x[:, b, kt * P:(kt + 1) * P], k.ident[:])
        op.then_inc(k.tok_flip, 1)
    pe.wait_ge(k.h_new, DT)
    for kind, step in k.steps:
        if kind == "dense":
            tensor_dense(k, pe, step)
        elif kind == "norm":
            if step.post_sum is not None:
                token_factors(k, pe, step)
        elif step.layer == 0:
            even_tensor(k, pe, step)
        else:
            odd_tensor(k, pe, step)
    for b in range(NBLK):
        if b >= 2:
            pe.wait_ge(k.out_left, b - 1)
            pe.wait_ge(k.out_right, b - 1)
        for kt in range(DT):
            if b == 0:
                pe.wait_ge(k.h_new, k.h_total - DT + kt + 1)
            bank = 4 * (b % 2) + kt // 4
            op = pe.transpose(k.psum[:, bank, (kt % 4) * P:(kt % 4 + 1) * P],
                              k.h[:, kt, META + b * P:META + (b + 1) * P], k.ident[:])
            if kt % 4 == 3:
                op.then_inc(k.out_flip, 1)



def bank_cols(core, pair, cols):
    if cols == TAIL:
        return core.psum[:, 2 * pair, 0:SEQ]
    return core.psum[:, 2 * pair:2 * pair + 2, 0:HALF]


def root(core, act, norm, n, half):
    k = core
    act.wait_ge(k.sum_ready, n + 1)
    act.activation(token_cols(k.rinv[:, :], norm.cols), bank_cols(k, norm.pair, norm.cols), ACT.Sqrt,
                   bias=k.eps[:, 1:2] if half else k.eps[:, 0:1],
                   scale=(4.0 if half else 1.0) / D).then_inc(k.root_ready, 1)


def load_table(core, act, func):
    core.tables += 1
    if core.tables > 1:
        act.wait_ge(core.table_set, core.tables - 1)
    act.activation(core.eps[0:1, 3:4], core.eps[0:1, 0:1], func).then_inc(core.table_set, 1)


def scalar_norm(core, act, norm):
    k = core
    if norm.post_sum is not None:
        act.wait_ge(k.inverse_ready, 2 * norm.posts + 1)
        act.activation(k.by_token[0:norm.block, 0, 0:norm.blocks], k.by_token[0:norm.block, 1, 0:norm.blocks], ACT.Sqrt,
                       bias=k.eps[0:norm.block, 1:2] if norm.half else k.eps[0:norm.block, 0:1],
                       scale=(4.0 if norm.half else 1.0) / D).then_inc(k.root_ready, 1)
        if norm.pre_sum is not None:
            act.wait_ge(k.spread_ready, 2 * norm.posts + 2)
            act.activation(token_cols(k.rinv[:, :], norm.cols), bank_cols(k, norm.copy_pair, norm.cols), ACT.Copy)\
                .then_inc(k.spread_copied, 1)
    if norm.pre_sum is None:
        return
    for kt in range(DT):
        act.wait_ge(k.h_new, norm.h0 + kt + 1)
        tile = k.h[:, kt, norm.t0:TOK]
        col = norm.pre_col + kt
        act.activation(k.x_hl[:, 0, kt, norm.t0:TOK], tile, ACT.Copy,
                       scale=k.norm_cols[:, col:col + 1]).then_inc(k.x_hi, 1)
        if kt >= 2:
            act.wait_ge(k.sq_added, norm.pre_added + kt - 1)
        buf = k.t_up if kt % 2 else k.t_gate
        act.activation(buf[:, norm.t0:TOK], tile, ACT.Square).then_inc(k.sq_made, 1)
    split_ahead(k, act, split_hi, norm.next, 0, 0)
    root(k, act, norm, norm.pre_sum, False)
    if norm.next.kind == "gu":
        load_table(k, act, ACT.Silu)


def scalar_dense(core, act, phase):
    k = core
    early = phase.kind in ("gu", "in")
    if not early:
        load_table(k, act, ACT.Sqrt)

    def step(i, u):
        if not (early and isinstance(i, int) and i + u == 0):
            split_ahead(k, act, split_hi, phase, i, u)
        slot = Slot(phase, i, u)
        if phase.kind == "gu":
            t = i * 2 + u // 2
            if u % 2 == 0:
                act.wait_ge(k.scaled, slot.local + (phase.evac0 + 1))
                act.activation(token_cols(k.t_gate[:, :], phase.cols), token_cols(k.t_gate[:, :], phase.cols),
                               ACT.Silu).then_inc(k.gate_silu, 1)
            else:
                act.wait_ge(k.act_full, t + (phase.a0 + 1))
                act.activation(token_cols(tile_at(k.acts[:, 0], t), phase.cols), token_cols(k.t_up[:, :], phase.cols),
                               ACT.Copy).then_inc(k.act_hi, 1)
        elif phase.kind == "down" and u % 2:
            pair = (phase.slot0 + u - 1) % RING
            result_tile(k, act, phase, slot, pair, i * 2 + u // 2, u // 2, k.f_down)
        elif phase.kind == "out":
            result_tile(k, act, phase, slot, slot.pair, slot.local, u % 2, k.f_mix)

    walk(k, phase, act, step, AHEAD, even_scalar_between)


def tile_at(buf, t):
    if isinstance(t, int):
        return buf[:, t, :]
    return buf[:, bass.ds(t, 1), :].rearrange("p a t -> p (a t)")


def result_tile(core, act, phase, slot, pair, m, odd, buf):
    k, norm = core, phase.after
    src = bank_cols(k, pair, phase.cols)
    act.wait_ge(k.slot_used, slot.count())
    if not (isinstance(m, int) and m < 2):
        act.wait_ge(k.sq_added, m + (norm.post_added - 1))
    squares = k.t_up if odd else k.t_gate
    act.activation(token_cols(squares[:, :], phase.cols), src, ACT.Square).then_inc(k.sq_made, 1)
    col = norm.post_col + m
    scale = k.norm_cols[:, col:col + 1] if isinstance(m, int) else k.norm_cols[:, bass.ds(col, 1)]
    act.activation(token_cols(tile_at(buf, m), phase.cols), src, ACT.Copy, scale=scale).then_inc(k.f_out, 1)


def scalar_program(core, act):
    k = core
    act.wait_ge(k.cols_flip, 1)
    act.activation(k.norm_cols[:, :], k.psum[:, 0, 0:12 * DT], ACT.Copy).then_inc(k.cols_ready, 1)
    act.activation(k.vec_cols[:, 0:VEC_ROWS], k.psum[:, 1, 0:VEC_ROWS], ACT.Copy).then_inc(k.cols_ready, 1)
    act.activation(k.bias_row[0:QH, 0:512], k.psum[0:QH, 2, 0:512], ACT.Copy).then_inc(k.cols_ready, 1)
    act.activation(k.bias_row[0:QH, 512:V_ALL], k.psum[0:QH, 3, 0:V_ALL - 512], ACT.Copy).then_inc(k.cols_ready, 1)
    act.wait_ge(k.consts_set, 5)
    act.wait_ge(k.bias_stored, 16)
    for u in range(AHEAD):
        split_hi(k, act, Slot(k.phases[0], 0, u), (DT, P))
    for kind, step in k.steps:
        if kind == "dense":
            scalar_dense(k, act, step)
        elif kind == "norm":
            scalar_norm(k, act, step)
        elif step.layer == 0:
            even_scalar(k, act, step)
        else:
            odd_scalar(k, act, step)
    for b in range(NBLK):
        act.wait_ge(k.out_flip, 2 * b + 1)
        act.activation(k.rows_out[:, b, 0:512], k.psum[:, 4 * (b % 2), :], ACT.Copy).then_inc(k.out_left, 1)



def vector_norm(core, dve, norm):
    k, t0 = core, norm.t0
    if norm.post_sum is not None:
        f = k.f_down if norm.half else k.f_mix
        n, blocks = norm.block, norm.blocks
        dve.wait_ge(k.sum_ready, norm.post_sum + 1)
        part = k.psum[0:n, 2 * norm.sum_pair, 0:2 * blocks]
        dve.tensor_reduce(k.by_token[0:n, 1, 0:blocks], part.rearrange("p (a b) -> p b a", a=2), AX.X, ALU.add)\
           .then_inc(k.inverse_ready, 1)
        dve.wait_ge(k.root_ready, norm.post_sum + 1)
        dve.reciprocal(k.by_token[0:n, 0, 0:blocks], k.by_token[0:n, 0, 0:blocks]).then_inc(k.inverse_ready, 1)
        dve.wait_ge(k.inverse_ready, 2 * norm.posts + 2)
        dve.tensor_tensor(k.t_gate[0:n, 0:blocks * n].rearrange("p (b q) -> p b q", q=n),
                          k.ident[0:n, 0:n].unsqueeze(1).broadcast_to([n, blocks, n]),
                          k.by_token[0:n, 0, 0:blocks].unsqueeze(2).broadcast_to([n, blocks, n]), ALU.mult)\
           .then_inc(k.spread_set, 1)
        dve.wait_ge(k.spread_ready, 2 * norm.posts + 1)
        shared = POOL_SCALES if norm.pre_sum is not None else 0
        scaled0 = norm.posts * (DT - POOL_SCALES)

    def scale_f(kt):
        if kt >= DT - shared:
            return
        tile = token_cols(f[:, kt, :], norm.cols)
        dve.tensor_tensor(tile, tile, bank_cols(k, norm.pair, norm.cols), ALU.mult).then_inc(k.f_scaled, 1)

    def lo(kt):
        dve.wait_ge(k.x_hi, norm.x0 + kt + 1)
        col = norm.pre_col + kt
        dve.scalar_tensor_tensor(k.x_hl[:, 1, kt, t0:TOK], k.h[:, kt, t0:TOK], k.norm_cols[:, col:col + 1],
                                 k.x_hl[:, 0, kt, t0:TOK].bitcast(F32), ALU.mult, ALU.subtract).then_inc(k.x_lo, 1)

    for kt in range(DT):
        if norm.post_sum is not None:
            if kt == 0:
                scale_f(0)
            if kt + 1 < DT:
                scale_f(kt + 1)
            if kt < DT - shared:
                dve.wait_ge(k.f_scaled, scaled0 + kt + 1)
            else:
                dve.wait_ge(k.f_scaled_pool, norm.posts * POOL_SCALES + kt - (DT - POOL_SCALES) + 1)
            dve.tensor_tensor(k.h[:, kt, t0:TOK], k.h[:, kt, t0:TOK], f[:, kt, t0:TOK], ALU.add).then_inc(k.h_new, 1)
        if norm.pre_sum is not None and kt:
            lo(kt - 1)
    if norm.pre_sum is not None:
        lo(DT - 1)
        split_ahead(k, dve, split_lo, norm.next, 0, 0)
        dve.wait_ge(k.root_ready, norm.pre_sum + 1)
        dve.reciprocal(k.rinv[:, t0:TOK], k.rinv[:, t0:TOK]).then_inc(k.rinv_ready, 1)


def vector_dense(core, dve, phase):
    k = core

    def step(i, u):
        slot = Slot(phase, i, u)
        src = bank_cols(k, slot.pair, phase.cols)
        rinv = token_cols(k.rinv[:, :], phase.cols)
        if phase.kind not in ("gu", "in"):
            split_ahead(k, dve, split_lo, phase, i, u)
            return
        if slot.peeled and slot.local == 0:
            dve.wait_ge(k.rinv_ready, phase.before.inverses + 1)
        dve.wait_ge(k.slot_used, slot.count())
        if phase.kind == "in":
            rows = P
            if slot.peeled and slot.local == phase.slots - 1:
                rows = RANK if phase.layer else EVEN_GATES
            if slot.peeled:
                tile = k.proj[phase.layer][0:rows, slot.local, :]
                src = k.psum[0:rows, 2 * slot.pair:2 * slot.pair + 2, 0:HALF]
                rinv = token_cols(k.rinv[0:rows, :], phase.cols)
            else:
                tile = tile_at(k.proj[phase.layer], slot.local)
            dve.tensor_tensor(token_cols(tile, FULL), src, rinv, ALU.mult).then_inc(k.scaled, 1)
        elif u % 2 == 0:
            dve.tensor_tensor(token_cols(k.t_gate[:, :], phase.cols), src, rinv, ALU.mult).then_inc(k.scaled, 1)
        else:
            t = i * 2 + u // 2
            if not (slot.peeled and slot.local == 1 and phase.a0 == 0):
                dve.wait_ge(k.act_lo, t + phase.a0)
            up, gate = token_cols(k.t_up[:, :], phase.cols), token_cols(k.t_gate[:, :], phase.cols)
            dve.tensor_tensor(up, src, rinv, ALU.mult).then_inc(k.scaled, 1)
            dve.wait_ge(k.scaled, slot.local + (phase.evac0 + 1))
            dve.wait_ge(k.gate_silu, t + (phase.a0 + 1))
            dve.tensor_tensor(up, up, gate, ALU.mult).then_inc(k.act_full, 1)
        if not (slot.peeled and slot.local == 0):
            split_ahead(k, dve, split_lo, phase, i, u)
        if phase.kind == "gu" and u % 2:
            dve.wait_ge(k.act_hi, t + (phase.a0 + 1))
            hi = token_cols(tile_at(k.acts[:, 0], t), phase.cols).bitcast(F32)
            dve.tensor_tensor(token_cols(tile_at(k.acts[:, 1], t), phase.cols), up, hi, ALU.subtract)\
               .then_inc(k.act_lo, 1)

    walk(k, phase, dve, step, AHEAD, even_vector_between)


def vector_program(core, dve):
    k = core
    dve.memset(k.ones[:, :], 1.0).then_inc(k.consts_set, 1)
    dve.memset(k.eps[:, 0:1], EPS).then_inc(k.consts_set, 1)
    dve.memset(k.eps[:, 1:2], 4 * EPS).then_inc(k.consts_set, 1)
    dve.memset(k.eps[:, 2:3], DN_DIM * EPS).then_inc(k.consts_set, 1)
    dve.memset(k.table[BUCKETS:BUCKETS + 1, :], MASKED).then_inc(k.consts_set, 1)
    for kt in range(DT):
        pair = (kt + 2) % RING
        dve.wait_ge(k.tok_flip, kt + 1)
        dve.tensor_copy(k.h[:, kt, 0:META + 2 * P], k.psum[:, 2 * pair, 0:META + 2 * P])
        dve.tensor_copy(k.h[:, kt, META + 2 * P:TOK], k.psum[:, 2 * pair + 1, 0:2 * P]).then_inc(k.h_new, 1)
    for u in range(AHEAD):
        split_lo(k, dve, Slot(k.phases[0], 0, u), (DT, P))
    for kind, step in k.steps:
        if kind == "dense":
            vector_dense(k, dve, step)
        elif kind == "norm":
            vector_norm(k, dve, step)
        elif step.layer == 0:
            even_vector(k, dve, step)
        else:
            odd_vector(k, dve, step)
    for b in range(NBLK):
        dve.wait_ge(k.out_flip, 2 * b + 2)
        dve.tensor_copy(k.rows_out[:, b, 512:D], k.psum[:, 4 * (b % 2) + 1, :]).then_inc(k.out_right, 1)



def add_squares(core, pool, n, cols, added, tiles):
    k = core
    t0 = META if cols == TAIL else 0
    for m in range(tiles):
        buf = (k.t_up if m % 2 else k.t_gate)[:, t0:TOK]
        if m == 0:
            if n:
                pool.wait_ge(k.sum_ready, n)
            pool.wait_ge(k.sq_made, DT * n + 1)
            pool.tensor_copy(k.sq_sum[:, t0:TOK], buf).then_inc(k.sq_added, 1)
        else:
            pool.wait_ge(k.sq_made, DT * n + m + 1)
            pool.wait_ge(k.sq_added, added + m)
            pool.tensor_tensor(k.sq_sum[:, t0:TOK], k.sq_sum[:, t0:TOK], buf, ALU.add).then_inc(k.sq_added, 1)


def scale_results(core, pool, norm):
    k = core
    pool.wait_ge(k.spread_copied, norm.posts + 1)
    f = k.f_down if norm.half else k.f_mix
    for kt in range(DT - POOL_SCALES, DT):
        tile = f[:, kt, norm.t0:TOK]
        pool.tensor_tensor(tile, tile, k.rinv[:, norm.t0:TOK], ALU.mult).then_inc(k.f_scaled_pool, 1)


def gpsimd_program(core, pool, a):
    k = core
    rows = [
        (k.ident[:, :], a["masks"][:, C_ID:C_ID + P]),
        (k.rows_norm[0:12 * DT, :], a["norm_w"].rearrange("l n (k p) -> (l n k) p", p=P)),
        (k.rows_vec[0:48, :], a["even_conv_w"][0].rearrange("c (k p) -> (c k) p", p=P)),
        (k.rows_vec[48:52, :], a["gla_b_gate"][0:1, :].rearrange("a (k p) -> (a k) p", p=P)),
        (k.rows_vec[52:54, :], a["gla_norm_w"][0:1, :].rearrange("a (k p) -> (a k) p", p=P)),
        (k.rows_vec[54:55, :], a["dn_norm_w"][0:1, :]),
        (k.table[0:BUCKETS, :], a["rel_bias_table"]),
        (k.bucket_hot[:, :], a["bucket_hot"]),
        (k.heads[:, 0:QH], a["swa_sinks"][0:1, :].broadcast_to([P, QH])),
        (k.heads[:, QH:QH + DH], a["dn_a_log"][0:1, :].broadcast_to([P, DH])),
        (k.heads[:, QH + DH:QH + 2 * DH], a["dn_dt_bias"][0:1, :].broadcast_to([P, DH])),
    ]
    assert len(rows) == CONST_LOADS
    for dst, src in rows:
        pool.dma_start(dst, src).then_inc(k.consts_in, 16)
    pool.wait_ge(k.cols_ready, 4)
    pool.dma_start(a["bias_scratch"], k.bias_row[0:QH, :]).then_inc(k.bias_stored, 16)
    for kind, step in k.steps:
        if kind == "norm":
            if step.post_sum is not None:
                add_squares(k, pool, step.post_sum, step.cols, step.post_added, DT - 1)
            if step.pre_sum is not None:
                if step.post_sum is not None:
                    scale_results(k, pool, step)
                add_squares(k, pool, step.pre_sum, step.cols, step.pre_added, DT)
        elif kind == "mix" and step.layer == 0:
            even_gpsimd(k, pool, step, a)
        elif kind == "mix":
            odd_gpsimd(k, pool, step, a)
    pool.wait_ge(k.bias_stored, 16)



Q_TILE, K_TILE, V_TILE, DN_TILE, Z_TILE, GATE_TILE = 0, 4, 5, 6, 18, 22
BANDS = META + 2 * P
BLOCKS = [(0, META)] + [(META + b * P, P) for b in range(NBLK)]
UNITS = [(b, kv) for b in range(NBLK + 1) for kv in range(KVH)]
LAST_SLOT = GATE_TILE
SCORED_AT = {5: [0, 1]}
PROBS_AT = {5: [0, 1]}
FLIPPED_AT = {6: [0], 7: [1]}
OUTPUT_AT = {7: [0], 8: [1]}
for unit in range(2, len(UNITS)):
    SCORED_AT[2 * unit + 2] = [unit]
    PROBS_AT[2 * unit + 3] = [unit]
    FLIPPED_AT[2 * unit + 4] = [unit]
    OUTPUT_AT[2 * unit + 5] = [unit]
FLIPS_AT = 5
SILU_AT = {11: 0, 15: DH, 19: 2 * DH}
SUMS_AT = {13: 0, 17: DH}
SUMS_READ_AT = 17
BIAS_FLIPS = QH + 2
FLIP_BANKS = (2, 3, 6, 7)


class Even:

    def __init__(self, core):
        at, a, x = core.at, core.arena, core.x_at
        tile = 4 * TOK
        self.proj = at("even_proj", [P, EVEN_TILES + 1, TOK], a)
        self.o_swa = at("o_swa", [P, 4, TOK], a)
        self.conv_k = at("conv_k", [P, DH, TOK], a + DN_TILE * tile)
        self.conv_v = at("conv_v", [P, DH, TOK], a + (DN_TILE + DH) * tile)
        self.conv_q = at("conv_q", [P, DH, TOK], a + 23 * tile)
        self.o_dn = at("o_dn", [P, DH, TOK], a + (DN_TILE + DH) * tile)
        self.squares = at("conv_squares", [P, DH, TOK], a + Z_TILE * tile)
        rows = a + Z_TILE * tile
        self.bias_rows = at("bias_rows", [P, QH, BANDS], rows)
        self.near_rows = at("near_rows", [P, QH, META], rows + 8704)
        self.self_rows = at("self_rows", [META, QH, META], rows + 9216)
        free = a + 27 * tile
        self.bias = at("bias", [P, QH, BANDS], free)
        self.bias_near = at("bias_near", [P, QH, META], free + 8704)
        self.bias_self = at("bias_self", [META, QH, META], free + 9216)
        self.flip = at("flip", [P, P], free + 9728)
        self.scores = at("scores", [P, 2, GRP, BANDS], free + 10240)
        self.probs_t = at("probs_t", [P, 3, GRP * P], free + 18944)
        self.v_rows = at("v_rows", [P, NBLK + 1, P], free + 25088)
        self.stats = at("swa_stats", [P, 2, 6, GRP], free + 27648)
        self.masks = at("dn_masks", [P, 9, P], free + 27840)
        self.gates = at("dn_gates", [P, 12, NBLK + 1, DH], free + 27840 + 4608)

        big = 4 * (NBLK + 1) * DH * P
        self.wide = at("dn_wide", [P, 2, DH * P], a + 14 * tile)
        self.wide2 = at("dn_wide2", [P, 2, DH * P], a + 14 * tile + 4096)
        self.half_x = at("half_x", [P, NBLK + 1, DH, P], free)
        self.u = at("dn_u", [P, NBLK + 1, DH, P], free)
        self.attn = at("dn_attn", [P, NBLK + 1, DH, P], free + big)
        self.a_t = at("dn_a", [P, NBLK + 1, DH, P], x)
        self.k_dec = at("dn_k_dec", [P, NBLK + 1, DH, P], x)
        self.inv = at("dn_inv", [P, NBLK + 1, DH, P], x + big)
        self.w_t = at("dn_w", [P, NBLK + 1, DH, P], x + big)
        self.inv_t = at("dn_inv_t", [P, NBLK + 1, DH, P], x + 2 * big)
        self.wide3 = at("dn_wide3", [P, DH * P], x + 3 * big)
        self.rows_in = core.sem("e_rows_in")
        self.masks_in = core.sem("e_masks_in")
        self.v_flip = core.sem("e_v_flip")
        self.bias_flip = core.sem("e_bias_flip")
        self.v_rows_set = core.sem("e_v_rows_set")
        self.bias_set = core.sem("e_bias_set")
        self.scored = core.sem("e_scored")
        self.s_made = core.sem("e_s_made")
        self.exped = core.sem("e_exped")
        self.probs = core.sem("e_probs")
        self.p_flip = core.sem("e_p_flip")
        self.p_copied = core.sem("e_p_copied")
        self.o_made = core.sem("e_o_made")
        self.o_copied = core.sem("e_o_copied")
        self.conv_first = core.sem("e_conv_first")
        self.conv_tap = core.sem("e_conv_tap")
        self.conv_done = core.sem("e_conv_done")
        self.conv_sq = core.sem("e_conv_sq")
        self.gate_flip = core.sem("e_gate_flip")
        self.gates_dve = core.sem("e_gates_dve")
        self.gates_act = core.sem("e_gates_act")
        self.gate_sums = core.sem("e_gate_sums")
        self.spread_set = core.sem("e_spread_set")
        self.spread = core.sem("e_spread")
        self.gc_col = core.sem("e_gc_col")
        self.decay = core.sem("e_decay")
        self.diff = core.sem("e_diff")
        self.k_beta = core.sem("e_k_beta")
        self.kk = core.sem("e_kk")
        self.qk = core.sem("e_qk")
        self.a_set = core.sem("e_a_set")
        self.attn_set = core.sem("e_attn_set")
        self.q_decayed = core.sem("e_q_decayed")
        self.level_mask = core.sem("e_level_mask")
        self.x_flip = core.sem("e_x_flip")
        self.x_start = core.sem("e_x_start")
        self.x_mid = core.sem("e_x_mid")
        self.x_mid_set = core.sem("e_x_mid_set")
        self.x_step = core.sem("e_x_step")
        self.x_set = core.sem("e_x_set")
        self.tok_flip2 = core.sem("e_tok_flip2")
        self.tok_scaled = core.sem("e_tok_scaled")
        self.w_made = core.sem("e_w_made")
        self.w_set = core.sem("e_w_set")
        self.read_made = core.sem("e_read_made")
        self.v_new = core.sem("e_v_new")
        self.o_dn_made = core.sem("e_o_dn_made")
        self.state = core.sem("e_state")
        self.o_dn_set = core.sem("e_o_dn_set")
        self.o_sq = core.sem("e_o_sq")
        self.o_sums = core.sem("e_o_sums")
        self.o_gates = core.sem("e_o_gates")
        self.z_silu = core.sem("e_z_silu")
        self.o_normed = core.sem("e_o_normed")
        self.o_full = core.sem("e_o_full")
        self.gates_raw = core.sem("e_gates_raw")
        self.gates_set = core.sem("e_gates_set")
        self.x_first = core.sem("e_x_first")
        self.o_spread = core.sem("e_o_spread")
        self.o_spread_set = core.sem("e_o_spread_set")
        self.dl_set = core.sem("e_dl_set")
        self.cols_decay = core.sem("e_cols_decay")
        self.state_made = core.sem("e_state_made")
        self.o_roots = core.sem("e_o_roots")
        self.swa_max = core.sem("e_swa_max")
        self.swa_den = core.sem("e_swa_den")
        self.gates_clear = core.sem("e_gates_clear")

    def conv(self, t):
        return (self.conv_q, self.conv_k, self.conv_v)[t // DH][:, t % DH, :]


def units_before(table, s):
    return sum(len(units) for at, units in table.items() if at < s)


def keys(b):
    if b == 0:
        return 0, 0
    if b == 1:
        return META, P
    return META + (b - 2) * P, 2 * P


def meta_scores(core, rows):
    return core.psum[0:rows, 7, 2 * P:2 * P + GRP * META].rearrange("p (h m) -> p h m", m=META)


def even_gpsimd(core, pool, mix, a):
    k, e = core, core.even
    pool.wait_ge(k.slot_used, mix.slots - EVEN_TILES - 1)
    pool.wait_ge(k.bias_stored, 16)
    scratch = a["bias_scratch"]
    tensor = scratch.tensor

    def skewed(first, rows, n):
        return bass.AP(tensor, first, [[1, rows], [V_ALL, QH], [1, n]])

    pool.dma_start(e.bias_rows[:, :, META:BANDS], skewed(V_BAND, P, 2 * P)).then_inc(e.rows_in, 16)
    pool.dma_start(e.bias_rows[:, :, 0:META], skewed(V_FAR, P, META)).then_inc(e.rows_in, 16)
    pool.dma_start(e.near_rows[:, :, :], skewed(V_NEAR, P, META)).then_inc(e.rows_in, 16)
    pool.dma_start(e.self_rows[:, :, :], skewed(V_SELF, META, META)).then_inc(e.rows_in, 16)
    pool.dma_start(e.flip[:, :], a["masks"][:, C_FLIP:C_FLIP + P]).then_inc(e.rows_in, 16)
    pool.dma_start(e.masks[:, 0:2, :], a["masks"][:, C_UP:C_UP + 2 * P].rearrange("p (n q) -> p n q", q=P))\
        .then_inc(e.masks_in, 16)
    pool.dma_start(e.masks[:, 2:9, :], a["masks"][:, C_LVL:C_LVL + LEVELS * P].rearrange("p (n q) -> p n q", q=P))\
        .then_inc(e.masks_in, 16)
    even_gpsimd_delta(k, e, pool)


def even_tensor_between(core, pe, mix, s):
    k, e = core, core.even
    ps, proj = k.psum, e.proj
    if s == FLIPS_AT:
        pe.wait_ge(k.scaled, mix.evac0 - EVEN_TILES - 1 + FLIPS_AT + 1)
        for c, (t0, n) in enumerate(BLOCKS):
            op = pe.transpose(ps[0:n, 4 + c // 4, (c % 4) * P:(c % 4 + 1) * P], proj[:, V_TILE, t0:t0 + n], k.ident[:])
        op.then_inc(e.v_flip, 1)
        pe.wait_ge(e.rows_in, 80)
        for j in range(BIAS_FLIPS):
            if j >= len(FLIP_BANKS):
                pe.wait_ge(e.bias_set, j - len(FLIP_BANKS) + 1)
            bank = FLIP_BANKS[j % len(FLIP_BANKS)]
            if j < QH:
                op = pe.matmul(ps[:, bank, 0:BANDS], e.flip[:], e.bias_rows[:, j, :], start=True, stop=True)
            elif j == QH:
                op = pe.matmul(ps[:, bank, 0:P], e.flip[:], e.near_rows[:].rearrange("p h m -> p (h m)"), start=True,
                               stop=True)
            else:
                op = pe.matmul(ps[0:META, bank, 0:P], e.flip[0:META, P - META:P],
                               e.self_rows[:].rearrange("p h m -> p (h m)"), start=True, stop=True)
            op.then_inc(e.bias_flip, 1)
        pe.wait_ge(e.bias_set, BIAS_FLIPS)
        pe.wait_ge(e.v_rows_set, 3)
    if s in SUMS_AT:
        first = SUMS_AT[s]
        pe.wait_ge(e.conv_sq, first + DH)
        pe.wait_ge(e.o_copied, OUTPUT_AT[s][0])
        pe.wait_ge(e.scored, units_before(SCORED_AT, s))
        for t in range(DH):
            for c, (t0, n) in enumerate(BLOCKS):
                at = SUMS_COL + c * 2 * DH + first + t
                op = pe.matmul(ps[0:n, 7, at:at + 1], e.squares[:, t, t0:t0 + n], k.ones[:, 0:1], start=True, stop=True)
        op.then_inc(e.gate_sums, 1)
    for i in OUTPUT_AT.get(s, []):
        b, kv = UNITS[i]
        n = BLOCKS[b][1]
        pe.wait_ge(e.p_copied, i + 1)
        pe.wait_ge(e.scored, units_before(SCORED_AT, s))
        if i:
            pe.wait_ge(e.o_copied, i)
        pieces = [META] + [P] * (keys(b)[1] // P)
        for odd in range(2):
            out = ps[HD * odd:HD * (odd + 1), 7, :].rearrange("p (g q) -> p g q", q=P)[:, 0:2, 0:n]
            for j, w in enumerate(pieces):
                block = 0 if j == 0 else (1 if b == 1 else b - 2 + j)
                moving = e.probs_t[0:w, j, :].rearrange("p (g o q) -> p g o q", o=2, q=P)[:, :, odd, 0:n]
                op = pe.matmul(out, e.v_rows[0:w, block, HD * kv:HD * (kv + 1)], moving, start=j == 0,
                               stop=j == len(pieces) - 1)
        op.then_inc(e.o_made, 1)
    for i in SCORED_AT.get(s, []):
        b, kv = UNITS[i]
        t0, n = BLOCKS[b]
        rows = slice(HD * kv, HD * (kv + 1))
        first, count = keys(b)
        if i:
            pe.wait_ge(e.scored, i)
        if i >= 2:
            outputs = units_before(OUTPUT_AT, s + 1)
            if outputs:
                pe.wait_ge(e.o_copied, outputs)
        if s > SUMS_READ_AT:
            pe.wait_ge(e.gates_raw, 1)
        for h in range(GRP):
            if count:
                pe.matmul(ps[0:n, 2 + h // 2, (h % 2) * 2 * P:(h % 2) * 2 * P + count], proj[rows, Q_TILE + h, t0:t0 + n],
                          proj[rows, K_TILE, first:first + count], start=True, stop=True)
            op = pe.matmul(meta_scores(k, n)[:, h, :], proj[rows, Q_TILE + h, t0:t0 + n], proj[rows, K_TILE, 0:META],
                           start=True, stop=True)
        op.then_inc(e.s_made, 1)
    for i in FLIPPED_AT.get(s, []):
        b, kv = UNITS[i]
        n = BLOCKS[b][1]
        pe.wait_ge(e.probs, i + 1)
        if i:
            pe.wait_ge(e.p_copied, i)
        for h in range(GRP):
            at = 0
            for j, w in enumerate([META] + [P] * (keys(b)[1] // P)):
                op = pe.transpose(ps[0:w, 4 + j, h * P:h * P + n], e.scores[0:n, i % 2, h, at:at + w],
                                  k.ident[0:n, 0:n])
                at += w
        op.then_inc(e.p_flip, 1)


def even_scalar_between(core, act, mix, s):
    k, e = core, core.even
    ps = k.psum
    if s == FLIPS_AT:
        act.wait_ge(e.v_flip, 1)
        act.activation(e.v_rows[0:META, 0, :], ps[0:META, 4, 0:P], ACT.Copy).then_inc(e.v_rows_set, 1)
        act.activation(e.v_rows[:, 1:4, :], ps[:, 4, P:4 * P].rearrange("p (c d) -> p c d", d=P), ACT.Copy)\
            .then_inc(e.v_rows_set, 1)
        act.activation(e.v_rows[:, 4, :], ps[:, 5, 0:P], ACT.Copy).then_inc(e.v_rows_set, 1)
    for i in OUTPUT_AT.get(s, []):
        b, kv = UNITS[i]
        t0, n = BLOCKS[b]
        act.wait_ge(e.o_made, i + 1)
        act.activation(e.o_swa[:, 2 * kv:2 * kv + 2, t0:t0 + n],
                       ps[:, 7, :].rearrange("p (g q) -> p g q", q=P)[:, 0:2, 0:n], ACT.Copy).then_inc(e.o_copied, 1)
    for i in FLIPPED_AT.get(s, []):
        b, kv = UNITS[i]
        n = BLOCKS[b][1]
        pieces = 1 + keys(b)[1] // P
        act.wait_ge(e.p_flip, i + 1)
        if i:
            act.wait_ge(e.o_made, i)
        op = act.activation(spread_cols(e.probs_t[0:META, 0, :], n), spread_cols(ps[0:META, 4, :], n), ACT.Copy)
        if pieces > 1:
            op = act.activation(e.probs_t[:, 1:pieces, :], ps[:, 5:4 + pieces, :], ACT.Copy)
        op.then_inc(e.p_copied, 1)
    t = s - DN_TILE
    if 0 <= t < 3 * DH:
        act.wait_ge(k.scaled, mix.evac0 - EVEN_TILES - 1 + s + 1)
        if t >= DH:
            act.wait_ge(e.conv_tap, (CONV - 1) * (t - DH + 1))
        col = (CONV - 1) * 3 * DH + t
        act.activation(e.conv(t), e.proj[:, DN_TILE + t, :], ACT.Copy, scale=k.vec_cols[:, col:col + 1])\
            .then_inc(e.conv_first, 1)
    for i in SCORED_AT.get(s, []):
        b, kv = UNITS[i]
        n = BLOCKS[b][1]
        st = e.stats[0:n, i % 2]
        act.wait_ge(e.swa_max, 3 * i + 3)
        for h in range(GRP):
            tile = e.scores[0:n, i % 2, h, 0:META + keys(b)[1]]
            act.activation(tile, tile, ACT.Exp, bias=st[:, 1, h:h + 1], accum_out=st[:, 2, h:h + 1])
        act.activation(st[:, 3, :], st[:, 3, :], ACT.Exp).then_inc(e.exped, 1)
    if s in SILU_AT:
        first = SILU_AT[s]
        act.wait_ge(e.conv_tap, (CONV - 1) * (first + DH))
        for t in range(first, first + DH):
            act.activation(e.conv(t), e.conv(t), ACT.Silu).then_inc(e.conv_done, 1)
        if first < 2 * DH:
            act.wait_ge(e.conv_done, first + DH)
            if first:
                act.wait_ge(e.gate_sums, 1)
            else:
                act.wait_ge(e.bias_set, BIAS_FLIPS)
            for t in range(DH):
                act.activation(e.squares[:, t, :], e.conv(first + t), ACT.Square).then_inc(e.conv_sq, 1)


def spread_cols(row, n):
    return row.rearrange("p (h q) -> p h q", q=P)[:, :, 0:n]


def even_vector_between(core, dve, mix, s):
    k, e = core, core.even
    ps = k.psum
    if s == FLIPS_AT:
        for j in range(BIAS_FLIPS):
            bank = FLIP_BANKS[j % len(FLIP_BANKS)]
            dve.wait_ge(e.bias_flip, j + 1)
            if j < QH:
                op = dve.tensor_copy(e.bias[:, j, :], ps[:, bank, 0:BANDS])
            elif j == QH:
                op = dve.tensor_copy(e.bias_near[:].rearrange("p h m -> p (h m)"), ps[:, bank, 0:P])
            else:
                op = dve.tensor_copy(e.bias_self[:].rearrange("p h m -> p (h m)"), ps[0:META, bank, 0:P])
            op.then_inc(e.bias_set, 1)
        dve.wait_ge(e.bias_set, BIAS_FLIPS)
        dve.memset(e.gates[:], 1.0).then_inc(e.gates_clear, 1)
    scale = HD ** -0.5
    for i in SCORED_AT.get(s, []):
        b, kv = UNITS[i]
        n = BLOCKS[b][1]
        heads = slice(GRP * kv, GRP * (kv + 1))
        count = keys(b)[1]
        width = META + count
        sc = e.scores[0:n, i % 2]
        st = e.stats[0:n, i % 2]
        dve.wait_ge(e.s_made, i + 1)
        if i >= 2:
            dve.wait_ge(e.p_flip, i - 1)
        meta_bias = (e.bias_self, e.bias_near, e.bias)[min(b, 2)][0:n, heads, 0:META]
        op = dve.scalar_tensor_tensor(sc[:, :, 0:META], meta_scores(k, n), scale, meta_bias, ALU.mult, ALU.add)
        if count:
            made = ps[0:n, 2:4, :].rearrange("p a (b c) -> p (a b) c", b=2)[:, :, 0:count]
            op = dve.scalar_tensor_tensor(sc[:, :, META:width], made, scale, e.bias[:, heads, BANDS - count:BANDS],
                                          ALU.mult, ALU.add)
        op.then_inc(e.scored, 1)
        dve.wait_ge(e.scored, i + 1)
        dve.tensor_reduce(st[:, 0, :], sc[:, :, 0:width], AX.X, ALU.max).then_inc(e.swa_max, 1)
        dve.wait_ge(e.swa_max, 3 * i + 1)
        dve.tensor_tensor(st[:, 0, :], st[:, 0, :], k.heads[0:n, heads], ALU.max).then_inc(e.swa_max, 1)
        dve.wait_ge(e.swa_max, 3 * i + 2)
        dve.tensor_scalar(st[:, 1, :], st[:, 0, :], -1.0, None, ALU.mult)
        dve.tensor_tensor(st[:, 3, :], k.heads[0:n, heads], st[:, 0, :], ALU.subtract).then_inc(e.swa_max, 1)
    t = s - DN_TILE - 1
    taps = [] if t < 0 or t >= 3 * DH else list(range(1, CONV))
    units = PROBS_AT.get(s, [])
    for i in units:
        b, kv = UNITS[i]
        n = BLOCKS[b][1]
        width = META + keys(b)[1]
        sc = e.scores[0:n, i % 2]
        st = e.stats[0:n, i % 2]
        dve.wait_ge(e.exped, i + 1)
        dve.tensor_tensor(st[:, 4, :], st[:, 2, :], st[:, 3, :], ALU.add).then_inc(e.swa_den, 1)
        dve.wait_ge(e.swa_den, 2 * i + 1)
        dve.reciprocal(st[:, 5, :], st[:, 4, :]).then_inc(e.swa_den, 1)
        dve.wait_ge(e.swa_den, 2 * i + 2)
        dve.tensor_tensor(sc[:, :, 0:width], sc[:, :, 0:width], st[:, 5, :].unsqueeze(2).broadcast_to([n, GRP, width]),
                          ALU.mult).then_inc(e.probs, 1)
    for back in taps:
        if back == 1:
            dve.wait_ge(e.conv_first, t + 1)
        else:
            dve.wait_ge(e.conv_tap, (CONV - 1) * t + back - 1)
        col = (CONV - 1 - back) * 3 * DH + t
        out = e.conv(t)[:, back:TOK]
        dve.scalar_tensor_tensor(out, e.proj[:, DN_TILE + t, 0:TOK - back], k.vec_cols[:, col:col + 1], out,
                                 ALU.mult, ALU.add).then_inc(e.conv_tap, 1)
    if s == SUMS_READ_AT:
        dve.wait_ge(e.gate_sums, 2)
        dve.wait_ge(e.gates_clear, 1)
        dve.wait_ge(e.o_copied, OUTPUT_AT[s][0] + 1)
        sums = ps[:, 7, SUMS_COL:SUMS_COL + 8 * (NBLK + 1)].rearrange("p (c q h) -> p q c h", q=2, h=DH)
        dve.tensor_copy(e.gates[0:META, G_SQ:G_SQ + 2, 0], sums[0:META, :, 0])
        dve.tensor_copy(e.gates[:, G_SQ:G_SQ + 2, 1:], sums[:, :, 1:]).then_inc(e.gates_raw, 1)


def even_rest(core, engine, mix, between):
    for s in range(LAST_SLOT + 1, max(OUTPUT_AT) + 1):
        between(core, engine, mix, s)


def even_tensor(core, pe, mix):
    even_rest(core, pe, mix, even_tensor_between)
    even_tensor_delta(core, core.even, pe, mix)


def even_scalar(core, act, mix):
    even_rest(core, act, mix, even_scalar_between)
    even_scalar_delta(core, core.even, act, mix)


def even_vector(core, dve, mix):
    even_rest(core, dve, mix, even_vector_between)
    even_vector_delta(core, core.even, dve, mix)


SUMS_COL = 2 * P + GRP * META


G_B, G_A, G_SQ, G_SK, G_BETA, G_LOG, G_RQ, G_RK, G_CUM, G_BEG, G_KD, G_DL = range(12)
M_UP, M_ADD, M_LVL = 0, 1, 2
SPREADS = ((M_UP, G_LOG), (None, G_RK), (None, G_RQ), (None, G_BETA))
LEVEL_ITEMS = [(lv, c) for lv in range(1, LEVELS) for c in range(NBLK + 1) if (1 << lv) < BLOCKS[c][1]]


class Chain:

    def __init__(self, engine, sem):
        self.engine, self.sem, self.n = engine, sem, 0

    def then(self, op):
        op.then_inc(self.sem, 1)
        self.n += 1
        self.engine.wait_ge(self.sem, self.n)


def heads_view(buf, rows, n):
    flat = buf[0:rows]
    if len(flat.shape) == 2:
        flat = flat.rearrange("p (h q) -> p h q", q=P)
    return flat[:, :, 0:n]


def along(col, rows, n):
    return col.unsqueeze(2).broadcast_to([rows, DH, n])


def over_heads(mask, rows, n):
    return mask.unsqueeze(1).broadcast_to([rows, DH, n])


def even_gpsimd_delta(k, e, pool):
    pool.wait_ge(e.masks_in, 32)
    pool.wait_ge(e.gates_set, 1)
    for c, (t0, n) in enumerate(BLOCKS):
        for q, (mask, gate) in enumerate(SPREADS):
            j = 4 * c + q
            if j >= 2:
                pool.wait_ge(e.spread, j - 1)
            m = k.ident[0:n, 0:n] if mask is None else e.masks[0:n, mask, 0:n]
            pool.tensor_tensor(heads_view(e.wide[:, j % 2, :], n, n), over_heads(m, n, n),
                               along(e.gates[0:n, gate, c, :], n, n), ALU.mult).then_inc(e.spread_set, 1)
    for c, (t0, n) in enumerate(BLOCKS):
        pool.wait_ge(e.a_set, c + 1)
        if c >= 2:
            pool.wait_ge(e.x_first, c - 1)
        buf = k.t_up if c % 2 else k.t_gate
        pool.tensor_tensor(heads_view(buf[:, 0:DH * P], n, n), heads_view(e.a_t[:, c], n, n),
                           over_heads(e.masks[0:n, M_LVL, 0:n], n, n), ALU.mult).then_inc(e.level_mask, 1)
    for j, (lv, c) in enumerate(LEVEL_ITEMS):
        n = BLOCKS[c][1]
        at = j + NBLK + 1
        if j == 0:
            pool.wait_ge(e.x_first, NBLK + 1)
        elif j >= 2:
            pool.wait_ge(e.x_mid, j - 1)
        buf = k.t_up if at % 2 else k.t_gate
        pool.tensor_tensor(heads_view(buf[:, 0:DH * P], n, n), heads_view(e.a_t[:, c], n, n),
                           over_heads(e.masks[0:n, M_LVL + lv, 0:n], n, n), ALU.mult).then_inc(e.level_mask, 1)
    pool.wait_ge(e.o_gates, 1)
    for c, (t0, n) in enumerate(BLOCKS):
        if c >= 2:
            pool.wait_ge(e.o_spread, c - 1)
        pool.tensor_tensor(heads_view(e.wide[:, c % 2, :], n, n), over_heads(k.ident[0:n, 0:n], n, n),
                           along(e.gates[0:n, G_SK, c, :], n, n), ALU.mult).then_inc(e.o_spread_set, 1)


def even_tensor_delta(k, e, pe, mix):
    ps = k.psum
    pe.wait_ge(k.scaled, mix.evac0)
    pe.wait_ge(e.p_copied, len(UNITS))
    for c, (t0, n) in enumerate(BLOCKS):
        op = pe.transpose(ps[0:n, 4, c * 8:(c + 1) * 8], e.proj[0:2 * DH, GATE_TILE, t0:t0 + n],
                          k.ident[0:2 * DH, 0:2 * DH])
    op.then_inc(e.gate_flip, 1)
    pe.wait_ge(e.o_copied, len(UNITS))
    for c, (t0, n) in enumerate(BLOCKS):
        for q in range(4):
            pe.wait_ge(e.spread_set, 4 * c + q + 1)
            if q == 0 and c:
                pe.wait_ge(e.decay, 2 * c)
                pe.wait_ge(e.k_beta, c)
            pe.matmul(heads_view(ps[:, q, :], P, n), k.ones[0:n, :], heads_view(e.wide[:, (4 * c + q) % 2, :], n, n),
                      start=True, stop=True).then_inc(e.spread, 1)
            if q == 0:
                pe.matmul(ps[0:n, 6, 0:DH], e.masks[0:n, M_UP, 0:n], e.gates[0:n, G_LOG, c, :], start=True,
                          stop=True).then_inc(e.gc_col, 1)
        if c:
            pe.wait_ge(e.attn_set, c)
        pe.wait_ge(e.k_beta, c + 1)
        for h in range(DH):
            op = pe.matmul(ps[0:n, 4, h * P:h * P + n], e.conv_k[:, h, t0:t0 + n], e.wide3[:, h * P:h * P + n],
                           start=True, stop=True)
        op.then_inc(e.kk, 1)
        for h in range(DH):
            op = pe.matmul(ps[0:n, 5, h * P:h * P + n], e.conv_k[:, h, t0:t0 + n], e.conv_q[:, h, t0:t0 + n],
                           start=True, stop=True)
        op.then_inc(e.qk, 1)
    pe.wait_ge(e.attn_set, NBLK + 1)
    for c, (t0, n) in enumerate(BLOCKS):
        pe.wait_ge(e.x_first, c + 1)
        if c >= 2:
            pe.wait_ge(e.x_start, c - 1)
        for h in range(DH):
            op = pe.transpose(ps[0:n, c % 2, h * P:h * P + n], e.inv_t[0:n, c, h, 0:n], k.ident[0:n, 0:n])
        op.then_inc(e.x_flip, 1)
    pe.wait_ge(e.x_start, NBLK + 1)

    def middle(j):
        lv, c = LEVEL_ITEMS[j]
        n = BLOCKS[c][1]
        pe.wait_ge(e.level_mask, NBLK + 1 + j + 1)
        before = [i for i, (_, other) in enumerate(LEVEL_ITEMS[:j]) if other == c]
        if before:
            pe.wait_ge(e.x_set, before[-1] + 1)
        if j >= 2:
            pe.wait_ge(e.x_mid_set, j - 1)
        buf = k.t_up if (NBLK + 1 + j) % 2 else k.t_gate
        for h in range(DH):
            op = pe.matmul(ps[0:n, j % 2, h * P:h * P + n], buf[0:n, h * P:h * P + n], e.inv[0:n, c, h, 0:n],
                           start=True, stop=True)
        op.then_inc(e.x_mid, 1)

    middle(0)
    for j, (lv, c) in enumerate(LEVEL_ITEMS):
        n = BLOCKS[c][1]
        if j + 1 < len(LEVEL_ITEMS):
            middle(j + 1)
        pe.wait_ge(e.x_mid_set, j + 1)
        if j >= 2:
            pe.wait_ge(e.x_set, j - 1)
        for h in range(DH):
            pe.matmul(ps[0:n, 2 + j % 2, h * P:h * P + n], e.inv_t[0:n, c, h, 0:n], e.half_x[0:n, c, h, 0:n],
                      start=True, stop=True)
            op = pe.matmul(ps[0:n, 4 + j % 2, h * P:h * P + n], e.half_x[0:n, c, h, 0:n], e.inv_t[0:n, c, h, 0:n],
                           start=True, stop=True)
        op.then_inc(e.x_step, 1)
    pe.wait_ge(e.x_set, len(LEVEL_ITEMS))
    for c, (t0, n) in enumerate(BLOCKS):
        if c >= 2:
            pe.wait_ge(e.tok_scaled, 3 * (c - 1))
        for h in range(DH):
            op = pe.transpose(ps[0:n, c % 2, h * P:(h + 1) * P], e.conv_k[:, h, t0:t0 + n], k.ident[:])
        op.then_inc(e.tok_flip2, 1)
        for h in range(DH):
            op = pe.transpose(ps[0:n, 2 + c % 2, h * P:(h + 1) * P], e.conv_v[:, h, t0:t0 + n], k.ident[:])
        op.then_inc(e.tok_flip2, 1)
        pe.wait_ge(e.tok_scaled, 3 * c + 3)
        if c >= 2:
            pe.wait_ge(e.w_set, 2 * (c - 1))
        for h in range(DH):
            op = pe.matmul(ps[:, 4 + c % 2, h * P:h * P + n], e.wide[0:n, c % 2, h * P:(h + 1) * P],
                           e.inv_t[0:n, c, h, 0:n], start=True, stop=True)
        op.then_inc(e.w_made, 1)
        for h in range(DH):
            op = pe.matmul(ps[0:n, 6 + c % 2, h * P:(h + 1) * P], e.inv_t[0:n, c, h, 0:n],
                           e.wide2[0:n, c % 2, h * P:(h + 1) * P], start=True, stop=True)
        op.then_inc(e.w_made, 1)
    pe.wait_ge(e.w_set, 2 * (NBLK + 1))

    def out_sums(c):
        n = BLOCKS[c][1]
        pe.wait_ge(e.o_sq, c + 1)
        for h in range(DH):
            op = pe.matmul(ps[0:n, 6, c * DH + h:c * DH + h + 1], e.wide[:, c % 2, h * P:h * P + n], k.ones[:, 0:1],
                           start=True, stop=True)
        op.then_inc(e.o_sums, 1)

    for c, (t0, n) in enumerate(BLOCKS):
        if c:
            pe.wait_ge(e.state, c)
            for h in range(DH):
                op = pe.matmul(ps[0:n, 0, h * P:(h + 1) * P], e.w_t[:, c, h, 0:n], e.wide3[:, h * P:(h + 1) * P],
                               start=True, stop=True)
            op.then_inc(e.read_made, 1)
            pe.wait_ge(e.v_new, c)
        if c >= 2:
            pe.wait_ge(e.o_dn_set, c - 1)
        for h in range(DH):
            out = ps[:, 2 + c % 2, h * P:h * P + n]
            if c:
                pe.matmul(out, e.wide3[:, h * P:(h + 1) * P], e.conv_q[:, h, t0:t0 + n], start=True, stop=False)
            op = pe.matmul(out, e.u[0:n, c, h, :], e.attn[0:n, c, h, 0:n], start=c == 0, stop=True)
        op.then_inc(e.o_dn_made, 1)
        if c < NBLK:
            for h in range(DH):
                op = pe.matmul(ps[:, 4, h * P:(h + 1) * P], e.k_dec[0:n, c, h, :], e.u[0:n, c, h, :], start=True,
                               stop=True)
            op.then_inc(e.state_made, 1)
        if c:
            out_sums(c - 1)
    out_sums(NBLK)
    for c, (t0, n) in enumerate(BLOCKS):
        pe.wait_ge(e.o_spread_set, c + 1)
        if c >= 2:
            pe.wait_ge(e.o_normed, c - 1)
        pe.matmul(heads_view(ps[:, c % 2, :], P, n), k.ones[0:n, :], heads_view(e.wide[:, c % 2, :], n, n),
                  start=True, stop=True).then_inc(e.o_spread, 1)


def even_scalar_delta(k, e, act, mix):
    ps = k.psum
    g = e.gates
    act.wait_ge(e.gates_raw, 4)
    act.activation(g[:, G_B], g[:, G_B], ACT.Exp, scale=-1.0).then_inc(e.gates_act, 1)
    act.activation(g[:, G_A], g[:, G_A], ACT.Exp).then_inc(e.gates_act, 1)
    act.activation(k.heads[:, QH:QH + DH], k.heads[:, QH:QH + DH], ACT.Exp).then_inc(e.gates_act, 1)
    act.wait_ge(e.gates_act, 3)
    act.activation(g[:, G_A], g[:, G_A], ACT.Ln, bias=k.ones[:, 0:1]).then_inc(e.gates_act, 1)
    act.activation(g[:, G_RQ], g[:, G_SQ], ACT.Sqrt, bias=k.eps[:, 2:3], scale=float(DN_DIM)).then_inc(e.gates_act, 1)
    act.activation(g[:, G_RK], g[:, G_SK], ACT.Sqrt, bias=k.eps[:, 0:1]).then_inc(e.gates_act, 1)
    for c, (t0, n) in enumerate(BLOCKS):
        act.wait_ge(e.spread, 4 * c + 1)
        if c:
            act.wait_ge(e.q_decayed, c)
            act.wait_ge(e.dl_set, c)
        act.activation(heads_view(e.wide2[:, 0, :], P, n), heads_view(ps[:, 0, :], P, n), ACT.Exp).then_inc(e.decay, 1)
        act.wait_ge(e.diff, 3 * c + 1)
        act.activation(g[0:n, G_BEG, c], g[0:n, G_CUM, c], ACT.Exp)
        act.activation(g[0:n, G_KD, c], g[0:n, G_KD, c], ACT.Exp).then_inc(e.cols_decay, 1)
        act.wait_ge(e.diff, 3 * c + 3)
        gamma = heads_view(e.wide2[:, 1, :], n, n)
        act.activation(gamma, gamma, ACT.Exp).then_inc(e.decay, 1)
    for c, (t0, n) in enumerate(BLOCKS):
        act.wait_ge(e.x_flip, c + 1)
        act.activation(heads_view(e.inv[:, c], n, n), heads_view(ps[:, c % 2, :], n, n), ACT.Copy)\
            .then_inc(e.x_start, 1)
    for j, (lv, c) in enumerate(LEVEL_ITEMS):
        n = BLOCKS[c][1]
        act.wait_ge(e.x_mid, j + 1)
        before = [i for i, (_, other) in enumerate(LEVEL_ITEMS[:j]) if other == c]
        if before:
            act.wait_ge(e.x_step, before[-1] + 1)
        act.activation(heads_view(e.half_x[:, c], n, n), heads_view(ps[:, j % 2, :], n, n), ACT.Copy)\
            .then_inc(e.x_mid_set, 1)
    act.wait_ge(e.x_set, len(LEVEL_ITEMS))
    for c, (t0, n) in enumerate(BLOCKS):
        act.wait_ge(e.w_made, 2 * c + 1)
        act.activation(heads_view(e.w_t[:, c], P, n), heads_view(ps[:, 4 + c % 2, :], P, n), ACT.Copy)\
            .then_inc(e.w_set, 1)
        act.wait_ge(e.w_made, 2 * c + 2)
        act.activation(heads_view(e.u[:, c], n, P), heads_view(ps[:, 6 + c % 2, :], n, P), ACT.Copy)\
            .then_inc(e.w_set, 1)
    for h in range(DH):
        act.activation(e.proj[:, Z_TILE + h, :], e.proj[:, Z_TILE + h, :], ACT.Silu).then_inc(e.z_silu, 1)
    for c, (t0, n) in enumerate(BLOCKS):
        act.wait_ge(e.o_dn_made, c + 1)
        if c >= 2:
            act.wait_ge(e.o_sums, c - 1)
        src = heads_view(ps[:, 2 + c % 2, :], P, n)
        act.activation(heads_view(e.wide[:, c % 2, :], P, n), src, ACT.Square).then_inc(e.o_sq, 1)
        act.activation(e.o_dn[:, :, t0:t0 + n], src, ACT.Copy).then_inc(e.o_dn_set, 1)
    act.wait_ge(e.o_sums, NBLK + 1)
    act.activation(g[0:META, G_SQ, 0], ps[0:META, 6, 0:DH], ACT.Sqrt, bias=k.eps[0:META, 0:1], scale=1.0 / DN_DIM)
    act.activation(g[:, G_SQ, 1:], ps[:, 6, DH:(NBLK + 1) * DH].rearrange("p (c h) -> p c h", h=DH), ACT.Sqrt,
                   bias=k.eps[:, 0:1], scale=1.0 / DN_DIM).then_inc(e.o_roots, 1)
    for kt in range(DT):
        if kt < 4:
            tile = e.o_swa[:, kt, :]
        else:
            act.wait_ge(e.o_full, kt - 3)
            tile = e.o_dn[:, kt - 4, :]
        act.activation(k.x_hl[:, 0, kt, :], tile, ACT.Copy).then_inc(k.x_hi, 1)


def even_vector_delta(k, e, dve, mix):
    ps, g = k.psum, e.gates
    chain = Chain(dve, e.gates_dve)
    dve.wait_ge(e.gate_flip, 1)
    raw = ps[:, 4, 0:8 * (NBLK + 1)].rearrange("p (c q h) -> p q c h", q=2, h=DH)
    dve.tensor_copy(g[0:META, 0:2, 0], raw[0:META, :, 0])
    chain.then(dve.tensor_copy(g[:, 0:2, 1:], raw[:, :, 1:]))
    dt = k.heads[:, QH + DH:QH + 2 * DH].unsqueeze(1).broadcast_to([P, NBLK + 1, DH])
    a_log = k.heads[:, QH:QH + DH].unsqueeze(1).broadcast_to([P, NBLK + 1, DH])
    x, neg = g[:, G_LOG], g[:, G_BEG]
    chain.then(dve.tensor_tensor(x, g[:, G_A], dt, ALU.add))
    dve.sem_inc(e.gates_raw, 2)
    chain.then(dve.tensor_scalar(neg, x, -1.0, None, ALU.mult))
    dve.tensor_tensor(g[:, G_A], x, neg, ALU.min).then_inc(e.gates_raw, 1)
    dve.wait_ge(e.gates_act, 1)
    chain.then(dve.tensor_scalar(g[:, G_BETA], g[:, G_B], 1.0, None, ALU.add))
    chain.then(dve.reciprocal(g[:, G_BETA], g[:, G_BETA]))
    dve.wait_ge(e.gates_act, 4)
    chain.then(dve.scalar_tensor_tensor(x, x, 0.0, g[:, G_A], ALU.max, ALU.add))
    chain.then(dve.scalar_tensor_tensor(x, x, -1.0, a_log, ALU.mult, ALU.mult))
    dve.wait_ge(e.gates_act, 6)
    dve.reciprocal(g[:, G_RQ:G_RQ + 2], g[:, G_RQ:G_RQ + 2]).then_inc(e.gates_set, 1)
    dve.wait_ge(e.masks_in, 32)
    for c, (t0, n) in enumerate(BLOCKS):
        diff = heads_view(e.wide2[:, 1, :], n, n)
        cum = heads_view(ps[:, 0, :], n, n)
        toks = slice(t0, t0 + n)
        dve.wait_ge(e.gc_col, c + 1)
        chain.then(dve.tensor_copy(g[0:n, G_CUM, c], ps[0:n, 6, 0:DH]))
        dve.wait_ge(e.decay, 2 * c + 1)
        dve.tensor_tensor(g[0:n, G_KD, c], cum[:, :, n - 1], g[0:n, G_CUM, c], ALU.subtract).then_inc(e.diff, 1)
        if c:
            dve.wait_ge(e.attn_set, c)
        dve.tensor_tensor(diff, cum, along(g[0:n, G_CUM, c], n, n), ALU.subtract).then_inc(e.diff, 1)
        dve.wait_ge(e.diff, 3 * c + 2)
        dve.scalar_tensor_tensor(diff, diff, 0.0, over_heads(e.masks[0:n, M_ADD, 0:n], n, n), ALU.min, ALU.add)\
            .then_inc(e.diff, 1)
        dve.wait_ge(e.spread, 4 * c + 2)
        keys_t = e.conv_k[:, :, toks]
        chain.then(dve.tensor_tensor(keys_t, keys_t, heads_view(ps[:, 1, :], P, n), ALU.mult))
        dve.wait_ge(e.spread, 4 * c + 3)
        queries_t = e.conv_q[:, :, toks]
        chain.then(dve.tensor_tensor(queries_t, queries_t, heads_view(ps[:, 2, :], P, n), ALU.mult))
        dve.wait_ge(e.spread, 4 * c + 4)
        if c:
            dve.wait_ge(e.kk, c)
        dve.tensor_tensor(heads_view(e.wide3[:, :], P, n), keys_t, heads_view(ps[:, 3, :], P, n), ALU.mult)\
            .then_inc(e.k_beta, 1)
        dve.wait_ge(e.decay, 2 * c + 2)
        dve.tensor_copy(g[:, G_DL, c], heads_view(e.wide2[:, 0, :], P, n)[:, :, n - 1]).then_inc(e.dl_set, 1)
        dve.wait_ge(e.cols_decay, c + 1)
        dve.tensor_tensor(g[0:n, G_BEG, c], g[0:n, G_BEG, c], g[0:n, G_BETA, c], ALU.mult)
        dve.wait_ge(e.kk, c + 1)
        dve.tensor_tensor(heads_view(e.a_t[:, c], n, n), heads_view(ps[:, 4, :], n, n), diff, ALU.mult)\
            .then_inc(e.a_set, 1)
        dve.wait_ge(e.qk, c + 1)
        dve.tensor_tensor(heads_view(e.attn[:, c], n, n), heads_view(ps[:, 5, :], n, n), diff, ALU.mult)\
            .then_inc(e.attn_set, 1)
        dve.tensor_tensor(queries_t, queries_t, heads_view(e.wide2[:, 0, :], P, n), ALU.mult).then_inc(e.q_decayed, 1)
    for c, (t0, n) in enumerate(BLOCKS):
        dve.wait_ge(e.level_mask, c + 1)
        buf = k.t_up if c % 2 else k.t_gate
        dve.tensor_tensor(heads_view(e.inv_t[:, c], n, n), over_heads(k.ident[0:n, 0:n], n, n),
                          heads_view(buf[:, 0:DH * P], n, n), ALU.subtract).then_inc(e.x_first, 1)
    for j, (lv, c) in enumerate(LEVEL_ITEMS):
        n = BLOCKS[c][1]
        dve.wait_ge(e.x_step, j + 1)
        inv, inv_t = heads_view(e.inv[:, c], n, n), heads_view(e.inv_t[:, c], n, n)
        dve.tensor_tensor(inv, inv, heads_view(ps[:, 2 + j % 2, :], n, n), ALU.subtract)
        dve.tensor_tensor(inv_t, inv_t, heads_view(ps[:, 4 + j % 2, :], n, n), ALU.subtract).then_inc(e.x_set, 1)
    dve.wait_ge(e.level_mask, NBLK + 1 + len(LEVEL_ITEMS))
    for c, (t0, n) in enumerate(BLOCKS):
        dve.wait_ge(e.tok_flip2, 2 * c + 1)
        if c >= 2:
            dve.wait_ge(e.w_made, 2 * (c - 1))
        keys_c, values_c = heads_view(ps[:, c % 2, :], n, P), heads_view(ps[:, 2 + c % 2, :], n, P)
        dve.tensor_tensor(heads_view(e.wide[:, c % 2, :], n, P), keys_c, along(g[0:n, G_BEG, c], n, P), ALU.mult)\
            .then_inc(e.tok_scaled, 1)
        dve.tensor_tensor(heads_view(e.k_dec[:, c], n, P), keys_c, along(g[0:n, G_KD, c], n, P), ALU.mult)\
            .then_inc(e.tok_scaled, 1)
        dve.wait_ge(e.tok_flip2, 2 * c + 2)
        dve.tensor_tensor(heads_view(e.wide2[:, c % 2, :], n, P), values_c, along(g[0:n, G_BETA, c], n, P), ALU.mult)\
            .then_inc(e.tok_scaled, 1)
    for c, (t0, n) in enumerate(BLOCKS):
        u = heads_view(e.u[:, c], n, P)
        if c:
            dve.wait_ge(e.read_made, c)
            dve.tensor_tensor(u, u, heads_view(ps[:, 0, :], n, P), ALU.subtract).then_inc(e.v_new, 1)
        if c == NBLK:
            break
        dve.wait_ge(e.state_made, c + 1)
        if c == 0:
            dve.tensor_copy(e.wide3[:, :], ps[:, 4, :]).then_inc(e.state, 1)
            continue
        dve.wait_ge(e.state, c)
        for h in range(DH):
            s = e.wide3[:, h * P:(h + 1) * P]
            op = dve.scalar_tensor_tensor(s, s, g[:, G_DL, c, h:h + 1], ps[:, 4, h * P:(h + 1) * P], ALU.mult, ALU.add)
        op.then_inc(e.state, 1)
    dve.wait_ge(e.o_roots, 1)
    dve.reciprocal(g[:, G_SK], g[:, G_SQ]).then_inc(e.o_gates, 1)
    dve.wait_ge(e.o_dn_set, NBLK + 1)
    for c, (t0, n) in enumerate(BLOCKS):
        dve.wait_ge(e.o_spread, c + 1)
        out = e.o_dn[:, :, t0:t0 + n]
        dve.tensor_tensor(out, out, heads_view(ps[:, c % 2, :], P, n), ALU.mult).then_inc(e.o_normed, 1)
    dve.wait_ge(e.o_normed, NBLK + 1)
    dve.wait_ge(e.z_silu, DH)
    weight = k.vec_cols[:, VEC_ROWS - 1:VEC_ROWS]
    for h in range(DH):
        dve.scalar_tensor_tensor(e.o_dn[:, h, :], e.o_dn[:, h, :], weight, e.proj[:, Z_TILE + h, :], ALU.mult,
                                 ALU.mult).then_inc(e.o_full, 1)
    for kt in range(DT):
        dve.wait_ge(k.x_hi, mix.x0 + kt + 1)
        tile = e.o_swa[:, kt, :] if kt < 4 else e.o_dn[:, kt - 4, :]
        dve.tensor_tensor(k.x_hl[:, 1, kt, :], tile, k.x_hl[:, 0, kt, :].bitcast(F32), ALU.subtract).then_inc(k.x_lo, 1)



GQ, GK, GV, GG, GATE_LOW = 0, 4, 8, 16, 24
VD = 2 * P
NORM_GATE = 16.0
CHUNKS = [(0, 0, 0, META)] + [(1 + s // 2, CH * (s % 2), META + s * CH, CH) for s in range(SEQ // CH)]


class Odd:

    def __init__(self, core):
        at, a, x = core.at, core.arena, core.x_at
        tile = 4 * TOK
        self.proj = at("odd_proj", [P, ODD_TILES + 1, TOK], a)
        free = a + (ODD_TILES + 1) * tile
        self.ex = at("gla_ex", [P, 6, TOK], free)
        self.squares = at("gla_squares", [P, 2, 2 * GH, P], free)
        self.diag = at("gla_diag", [P, 2, GH * P], free + 8192)
        self.k_grow = at("gla_k_grow", [P, GH, TOK], free + 6 * tile)
        self.attn = at("gla_attn", [P, NBLK, GH, P], free + 10 * tile)
        self.state = at("gla_state", [P, 2, GH, VD], free + 10 * tile + 8192)
        self.keep = at("gla_keep", [P, TOK], free + 10 * tile + 16384)
        self.cols = at("gla_cols", [P, 2 * NBLK * GH + GH * len(CHUNKS)], free + 11 * tile + 16384)
        self.v_rows = at("gla_v_rows", [P, NBLK + 1, GH * VD], x)
        self.k_rows = at("gla_k_rows", [P, NBLK + 1, GH * P], x + 4 * (NBLK + 1) * GH * VD)
        self.gate_up = at("gla_gate_up", [RANK, GH * P], x + 4 * (NBLK + 1) * GH * (VD + P))
        self.mask = at("gla_mask", [P, P], x + 4 * (NBLK + 1) * GH * (VD + P) + 4 * GH * P)
        self.decay = self.cols[:, 2 * NBLK * GH:].rearrange("p (h s) -> p h s", h=GH)
        self.roots = self.cols[:, 0:NBLK * GH].rearrange("p (c h) -> p c h", h=GH)
        self.inverse = self.cols[:, NBLK * GH:2 * NBLK * GH].rearrange("p (c h) -> p c h", h=GH)
        self.s_in = core.sem("o_in")
        self.s_gate_lin = core.sem("o_gate_lin")
        self.s_gate_x = core.sem("o_gate_x")
        self.s_gate_neg = core.sem("o_gate_neg")
        self.s_gate_exp = core.sem("o_gate_exp")
        self.s_gate_log = core.sem("o_gate_log")
        self.s_gate_min = core.sem("o_gate_min")
        self.s_cum = core.sem("o_cum")
        self.s_kd_arg = core.sem("o_kd_arg")
        self.s_grown = core.sem("o_grown")
        self.s_q_dec = core.sem("o_q_dec")
        self.s_k_grow = core.sem("o_k_grow")
        self.s_k_dec = core.sem("o_k_dec")
        self.s_v_flip = core.sem("o_v_flip")
        self.s_v_set = core.sem("o_v_set")
        self.s_k_flip = core.sem("o_k_flip")
        self.s_k_set = core.sem("o_k_set")
        self.s_attn_made = core.sem("o_attn_made")
        self.s_attn_set = core.sem("o_attn_set")
        self.s_kv_made = core.sem("o_kv_made")
        self.s_state = core.sem("o_state")
        self.s_o_made = core.sem("o_o_made")
        self.s_o_sq = core.sem("o_o_sq")
        self.s_o_set = core.sem("o_o_set")
        self.s_o_sums = core.sem("o_o_sums")
        self.s_o_roots = core.sem("o_o_roots")
        self.s_o_inverse = core.sem("o_o_inverse")
        self.s_diag_set = core.sem("o_diag_set")
        self.s_diag_used = core.sem("o_diag_used")
        self.s_o_normed = core.sem("o_o_normed")
        self.s_g_silu = core.sem("o_g_silu")
        self.s_o_full = core.sem("o_o_full")


def odd_gpsimd(core, pool, mix, a):
    k, o = core, core.odd
    pool.wait_ge(k.slot_used, mix.slots)
    pool.dma_start(o.gate_up[:, :], a["gla_w_gate_up"][0]).then_inc(o.s_in, 16)
    pool.dma_start(o.keep[:, :], a["scan_keep"]).then_inc(o.s_in, 16)
    pool.dma_start(o.mask[:, :], a["masks"][:, C_GLA:C_GLA + P]).then_inc(o.s_in, 16)
    pool.wait_ge(o.s_o_inverse, 1)
    for c in range(NBLK):
        if c >= 2:
            pool.wait_ge(o.s_diag_used, c - 1)
        pool.tensor_tensor(heads_view(o.diag[:, c % 2, :], P, P), over_heads(k.ident[:, :], P, P),
                           along(o.inverse[:, c], P, P), ALU.mult).then_inc(o.s_diag_set, 1)


def odd_tensor(core, pe, mix):
    k, o = core, core.odd
    ps, proj = k.psum, o.proj
    pe.wait_ge(k.scaled, mix.evac0)
    pe.wait_ge(o.s_in, 48)
    for h in range(GH):
        for b, (t0, n) in enumerate(halves(FULL)):
            op = pe.matmul(ps[:, 2 * h + b, 0:n], o.gate_up[:, h * P:(h + 1) * P], proj[0:RANK, GATE_LOW, t0:t0 + n],
                           start=True, stop=True)
        op.then_inc(o.s_gate_lin, 1)
    pe.wait_ge(o.s_gate_x, GH)
    for c, (t0, n) in enumerate(BLOCKS):
        if c >= 2:
            pe.wait_ge(o.s_v_set, c - 1)
        for j in range(2 * GH):
            op = pe.transpose(ps[0:n, 2 * (c % 2) + j // 4, (j % 4) * P:(j % 4 + 1) * P], proj[:, GV + j, t0:t0 + n],
                              k.ident[:])
        op.then_inc(o.s_v_flip, 1)
    pe.wait_ge(o.s_k_dec, GH)
    for c, (t0, n) in enumerate(BLOCKS):
        if c >= 2:
            pe.wait_ge(o.s_k_set, c - 1)
        for h in range(GH):
            op = pe.transpose(ps[0:n, 4 + c % 2, h * P:(h + 1) * P], proj[:, GK + h, t0:t0 + n], k.ident[:])
        op.then_inc(o.s_k_flip, 1)
        if c == 0:
            continue
        if c > 2:
            pe.wait_ge(o.s_attn_set, c - 2)
        for h in range(GH):
            op = pe.matmul(ps[:, 6 + c % 2, h * P:(h + 1) * P], o.k_grow[:, h, t0:t0 + n], proj[:, GQ + h, t0:t0 + n],
                           start=True, stop=True)
        op.then_inc(o.s_attn_made, 1)
    pe.wait_ge(o.s_v_set, NBLK + 1)
    pe.wait_ge(o.s_k_set, NBLK + 1)

    def sums(c):
        pe.wait_ge(o.s_o_sq, 2 * c)
        for h in range(GH):
            for j in range(2):
                op = pe.matmul(ps[:, 6, (c - 1) * GH + h:(c - 1) * GH + h + 1], o.squares[:, c % 2, 2 * h + j, :],
                               k.ones[:, 0:1], start=j == 0, stop=j == 1)
        op.then_inc(o.s_o_sums, 1)

    for s, (c, r0, t0, n) in enumerate(CHUNKS):
        rows = slice(r0, r0 + n)
        if s < len(CHUNKS) - 1:
            if s >= 2:
                pe.wait_ge(o.s_state, s - 1)
            for h in range(GH):
                out = ps[:, 2 * (s % 2) + h // 2, (h % 2) * VD:(h % 2 + 1) * VD]
                op = pe.matmul(out, o.k_rows[rows, c, h * P:(h + 1) * P], o.v_rows[rows, c, h * VD:(h + 1) * VD],
                               start=True, stop=True)
            op.then_inc(o.s_kv_made, 1)
        if s == 0:
            continue
        if s == 1:
            pe.wait_ge(o.s_attn_set, NBLK)
        if s > 2:
            pe.wait_ge(o.s_o_set, s - 2)
        pe.wait_ge(o.s_state, s)
        for j in range(2 * GH):
            h = j // 2
            out = ps[:, 4 + s % 2, j * CH:(j + 1) * CH]
            pe.matmul(out, o.state[:, s % 2, h, (j % 2) * P:(j % 2 + 1) * P], proj[:, GQ + h, t0:t0 + n], start=True,
                      stop=False)
            op = pe.matmul(out, o.v_rows[rows, c, j * P:(j + 1) * P], o.attn[rows, c - 1, h, r0:r0 + n], start=False,
                           stop=True)
        op.then_inc(o.s_o_made, 1)
        if s % 2 == 1 and s > 1:
            sums((s - 1) // 2)
    sums(NBLK)
    for c in range(NBLK):
        pe.wait_ge(o.s_diag_set, c + 1)
        if c >= 2:
            pe.wait_ge(o.s_o_normed, c - 1)
        pe.matmul(ps[:, c % 2, :], k.ones[:], o.diag[:, c % 2, :], start=True, stop=True).then_inc(o.s_diag_used, 1)


def chunk_ends(tile):
    return tile[:, META:TOK].rearrange("p (s t) -> p s t", t=CH)[:, :, CH - 1:CH]


def odd_scalar(core, act, mix):
    k, o = core, core.odd
    ps, proj = k.psum, o.proj
    for h in range(GH):
        act.wait_ge(o.s_gate_lin, h + 1)
        act.activation(token_cols(o.ex[:, h, :], FULL), bank_cols(k, h, FULL), ACT.Identity,
                       bias=k.vec_cols[:, 48 + h:49 + h]).then_inc(o.s_gate_x, 1)
    for pair in range(GH // 2):
        heads = (2 * pair, 2 * pair + 1)
        for h in heads:
            u = o.ex[:, 4 + h % 2, :]
            act.wait_ge(o.s_gate_neg, h + 1)
            act.activation(u, u, ACT.Exp).then_inc(o.s_gate_exp, 1)
        for h in heads:
            u = o.ex[:, 4 + h % 2, :]
            act.wait_ge(o.s_gate_exp, h + 1)
            act.activation(u, u, ACT.Ln, bias=k.ones[:, 0:1]).then_inc(o.s_gate_log, 1)
        if pair == 0:
            for c in (0, 1):
                value_rows(k, o, act, c)
        for h in heads:
            cum, scale = o.ex[:, h, :], 1.0 / NORM_GATE
            act.wait_ge(o.s_cum, h + 1)
            if h >= 2:
                act.wait_ge(o.s_q_dec, h - 1)
            act.activation((k.t_up if h % 2 else k.t_gate)[:, :], cum, ACT.Exp, scale=scale)
            act.activation(o.k_grow[:, h, :], cum, ACT.Exp, scale=-scale)
            act.activation(o.decay[:, h, 0:1], cum[:, META - 1:META], ACT.Exp, scale=scale)
            act.activation(o.decay[:, h, 1:].unsqueeze(2), chunk_ends(cum), ACT.Exp, scale=scale)
            act.wait_ge(o.s_kd_arg, h + 1)
            u = o.ex[:, 4 + h % 2, :]
            act.activation(u, u, ACT.Exp, scale=scale).then_inc(o.s_grown, 1)
        for c in ((2, 3) if pair == 0 else (4,)):
            value_rows(k, o, act, c)
    for c, (t0, n) in enumerate(BLOCKS):
        act.wait_ge(o.s_k_flip, c + 1)
        act.activation(o.k_rows[0:n, c, :], ps[0:n, 4 + c % 2, :], ACT.Copy).then_inc(o.s_k_set, 1)
    for j in range(2 * GH):
        g = proj[:, GG + j, META:TOK]
        act.activation(g, g, ACT.Silu).then_inc(o.s_g_silu, 1)
    for s, (c, r0, t0, n) in enumerate(CHUNKS):
        if s == 0:
            continue
        act.wait_ge(o.s_o_made, s)
        if s > 4:
            act.wait_ge(o.s_o_sums, (s - 1) // 2 - 1)
        src = ps[:, 4 + s % 2, :].rearrange("p (j t) -> p j t", t=CH)
        act.activation(o.squares[:, c % 2, :, r0:r0 + n], src, ACT.Square).then_inc(o.s_o_sq, 1)
        act.activation(proj[:, GV:GV + 2 * GH, t0:t0 + n], src, ACT.Copy).then_inc(o.s_o_set, 1)
    act.wait_ge(o.s_o_sums, NBLK)
    act.activation(o.roots, ps[:, 6, 0:NBLK * GH].rearrange("p (c h) -> p c h", h=GH), ACT.Sqrt, bias=k.eps[:, 0:1],
                   scale=1.0 / VD).then_inc(o.s_o_roots, 1)
    for kt in range(DT):
        act.wait_ge(o.s_o_full, kt + 1)
        act.activation(k.x_hl[:, 0, kt, META:TOK], proj[:, GV + kt, META:TOK], ACT.Copy).then_inc(k.x_hi, 1)


def value_rows(k, o, act, c):
    n = BLOCKS[c][1]
    act.wait_ge(o.s_v_flip, c + 1)
    act.activation(o.v_rows[0:n, c, :].rearrange("p (b q) -> p b q", b=2), k.psum[0:n, 2 * (c % 2):2 * (c % 2) + 2, :],
                   ACT.Copy).then_inc(o.s_v_set, 1)


def odd_vector(core, dve, mix):
    k, o = core, core.odd
    ps, proj = k.psum, o.proj
    dve.wait_ge(o.s_in, 48)
    for pair in range(GH // 2):
        heads = (2 * pair, 2 * pair + 1)
        for h in heads:
            x, u = o.ex[:, h, :], o.ex[:, 4 + h % 2, :]
            dve.wait_ge(o.s_gate_x, h + 1)
            if pair:
                dve.wait_ge(o.s_k_dec, h - 1)
            dve.scalar_tensor_tensor(u, x, -1.0, x, ALU.mult, ALU.min).then_inc(o.s_gate_neg, 1)
        for h in heads:
            x, u = o.ex[:, h, :], o.ex[:, 4 + h % 2, :]
            dve.wait_ge(o.s_gate_log, h + 1)
            dve.scalar_tensor_tensor(x, x, 0.0, u, ALU.min, ALU.subtract).then_inc(o.s_gate_min, 1)
        for h in heads:
            x, u = o.ex[:, h, :], o.ex[:, 4 + h % 2, :]
            dve.wait_ge(o.s_gate_min, h + 1)
            dve.tensor_tensor_scan(x, o.keep[:, :], x, 0.0, ALU.mult, ALU.add).then_inc(o.s_cum, 1)
            dve.wait_ge(o.s_cum, h + 1)
            dve.tensor_tensor(u[:, 0:META], x[:, META - 1:META].broadcast_to([P, META]), x[:, 0:META], ALU.subtract)
            rest = u[:, META:TOK].rearrange("p (s t) -> p s t", t=CH)
            cum = x[:, META:TOK].rearrange("p (s t) -> p s t", t=CH)
            dve.tensor_tensor(rest, chunk_ends(x).broadcast_to([P, SEQ // CH, CH]), cum, ALU.subtract)\
                .then_inc(o.s_kd_arg, 1)
        for h in heads:
            dve.wait_ge(o.s_grown, h + 1)
            q, key = proj[:, GQ + h, :], proj[:, GK + h, :]
            dve.scalar_tensor_tensor(q, q, float(P) ** -0.5, (k.t_up if h % 2 else k.t_gate)[:, :], ALU.mult, ALU.mult)\
                .then_inc(o.s_q_dec, 1)
            grow = o.k_grow[:, h, :]
            dve.tensor_tensor(grow, grow, key, ALU.mult).then_inc(o.s_k_grow, 1)
            dve.wait_ge(o.s_k_grow, h + 1)
            dve.tensor_tensor(key, key, o.ex[:, 4 + h % 2, :], ALU.mult).then_inc(o.s_k_dec, 1)
    for c in range(1, NBLK + 1):
        dve.wait_ge(o.s_attn_made, c)
        dve.tensor_tensor(o.attn[:, c - 1], heads_view(ps[:, 6 + c % 2, :], P, P), over_heads(o.mask[:, :], P, P),
                          ALU.mult).then_inc(o.s_attn_set, 1)
    dve.wait_ge(o.s_attn_set, NBLK)
    for s in range(len(CHUNKS) - 1):
        dve.wait_ge(o.s_kv_made, s + 1)
        kv = ps[:, 2 * (s % 2):2 * (s % 2) + 2, :].rearrange("p b (h v) -> p (b h) v", v=VD)
        to = o.state[:, (s + 1) % 2]
        if s == 0:
            dve.tensor_copy(to.rearrange("p (b h) v -> p b (h v)", b=2), ps[:, 0:2, :]).then_inc(o.s_state, 1)
            continue
        if s >= 2:
            dve.wait_ge(o.s_o_made, s - 1)
        dve.wait_ge(o.s_state, s)
        for h in range(GH):
            op = dve.scalar_tensor_tensor(to[:, h], o.state[:, s % 2, h], o.decay[:, h, s:s + 1],
                                          ps[:, 2 * (s % 2) + h // 2, (h % 2) * VD:(h % 2 + 1) * VD], ALU.mult, ALU.add)
        op.then_inc(o.s_state, 1)
    dve.wait_ge(o.s_o_roots, 1)
    dve.reciprocal(o.inverse, o.roots).then_inc(o.s_o_inverse, 1)
    dve.wait_ge(o.s_o_set, 2 * NBLK)
    for c in range(NBLK):
        dve.wait_ge(o.s_diag_used, c + 1)
        t0 = META + c * P
        out = proj[:, GV:GV + 2 * GH, t0:t0 + P].rearrange("p (h j) t -> p h j t", j=2)
        factor = heads_view(ps[:, c % 2, :], P, P).unsqueeze(2).broadcast_to([P, GH, 2, P])
        dve.tensor_tensor(out, out, factor, ALU.mult).then_inc(o.s_o_normed, 1)
    dve.wait_ge(o.s_o_normed, NBLK)
    dve.wait_ge(o.s_g_silu, 2 * GH)

    def gated(j):
        out = proj[:, GV + j, META:TOK]
        dve.scalar_tensor_tensor(out, out, k.vec_cols[:, 52 + j % 2:53 + j % 2], proj[:, GG + j, META:TOK], ALU.mult,
                                 ALU.mult).then_inc(o.s_o_full, 1)

    gated(0)
    for kt in range(DT):
        if kt + 1 < DT:
            gated(kt + 1)
        dve.wait_ge(k.x_hi, mix.x0 + kt + 1)
        dve.tensor_tensor(k.x_hl[:, 1, kt, META:TOK], proj[:, GV + kt, META:TOK],
                          k.x_hl[:, 0, kt, META:TOK].bitcast(F32), ALU.subtract).then_inc(k.x_lo, 1)


INPUTS = ["x", "meta_tokens", "norm_w", "ffn_w_gate", "ffn_w_up", "ffn_w_down", "rel_bias_table", "even_w_in",
          "even_conv_w", "swa_sinks", "dn_a_log", "dn_dt_bias", "dn_norm_w", "even_w_out", "odd_w_in",
          "gla_w_gate_up", "gla_b_gate", "gla_norm_w", "odd_w_out"]


def trunk(nc, a, stop=None):
    steps = linked(plan(stop))
    with ExitStack() as ctx:
        core = Core(nc, ctx, steps)
        block = ctx.enter_context(nc.Block())

        @block.sync
        def _(sp):
            sync_program(core, sp, a)

        @block.tensor
        def _(pe):
            tensor_program(core, pe)

        @block.scalar
        def _(act):
            scalar_program(core, act)

        @block.vector
        def _(dve):
            vector_program(core, dve)

        @block.gpsimd
        def _(pool):
            gpsimd_program(core, pool, a)


def kernel(**inputs):
    import concourse.bacc as bacc
    from concourse.bass_utils import run_bass_kernel_spmd

    nc = bacc.Bacc("TRN2", target_bir_lowering=False, num_devices=1)
    masks, hot, scan = shape_constants()
    arrays, args = {}, {}
    for name in INPUTS:
        arrays[name] = np.ascontiguousarray(inputs[name])
    arrays.update(masks=masks, bucket_hot=hot, scan_keep=scan)
    for name, array in arrays.items():
        args[name] = nc.dram_tensor(name, array.shape, mybir.dt.from_np(array.dtype), kind="ExternalInput").ap()
    args["bias_scratch"] = nc.dram_tensor("bias_scratch", (QH, V_ALL), F32, kind="Internal").ap()
    args["out"] = nc.dram_tensor("out", (1, SEQ, D), F32, kind="ExternalOutput").ap()
    trunk(nc, args)
    r = run_bass_kernel_spmd(nc, [arrays], core_ids=[0])
    return r.results[0]["out"]
```

```python
from contextlib import ExitStack

import numpy as np

import concourse.bass as bass
from concourse import mybir

ACT = mybir.ActivationFunctionType
ALU = mybir.AluOpType
AX = mybir.AxisListType
F32 = mybir.dt.float32
F32R = mybir.dt.float32r

P = 128
META = 16
SEQ = 512
TOK = META + SEQ
GATES_OUT = 6
KEYS_FROM = 14
MIDDLE = META + SEQ // 2
D = 1024
DT = D // P
FF = 2816
FT = FF // P
FH = FT // 2
EPS = 1e-6
MASKED = -1e30
BUCKETS = 32
MAX_DIST = 128
QH, KVH, HD = 8, 2, 64
GRP = QH // KVH
NBLK = SEQ // P
DH = 4
CONV = 4
GH = 4
CH = 64
RING = 4
AHEAD = 3
POOL_SCALES = 2
EVEN_TILES = 22
EVEN_GATES = 2 * DH
ODD_TILES = 24
RANK = 16
DN_DIM = 128
CONST_LOADS = 11
SCALAR_LOADS = 6
VEC_ROWS = CONV * 3 * DH + 4 + 2 + 1
HALF = TOK // 2
FULL = "full"
TAIL = "tail"

BAND_N = 3 * P - 1
META_N = P + META - 1
SELF_N = 2 * META - 1
V_BAND, V_NEAR, V_FAR, V_SELF = 0, BAND_N, BAND_N + META_N, BAND_N + 2 * META_N
V_ALL = V_SELF + SELF_N

LEVELS = 7
C_ID, C_FLIP, C_UP, C_ADD, C_LVL = 0, P, 2 * P, 3 * P, 4 * P
C_GLA = C_LVL + LEVELS * P
C_ALL = C_GLA + P


def shape_constants():
    j = np.arange(P)[:, None]
    i = np.arange(P)[None, :]
    masks = np.zeros((P, C_ALL), np.float32)
    masks[:, C_ID:C_ID + P] = i == j
    masks[:, C_FLIP:C_FLIP + P] = i + j == P - 1
    masks[:, C_UP:C_UP + P] = j <= i
    masks[:, C_ADD:C_ADD + P] = np.where(j <= i, 0.0, MASKED)
    for n in range(LEVELS):
        s = 1 << n
        level = (i // (2 * s) == j // (2 * s)) & ((i // s) % 2 == 1) & ((j // s) % 2 == 0)
        masks[:, C_LVL + n * P:C_LVL + (n + 1) * P] = level
    masks[:, C_GLA:C_GLA + P] = (j <= i) & (i // CH == j // CH)

    def bucket(n):
        exact = BUCKETS // 2
        far = np.log(np.maximum(n, 1).astype(np.float32) / np.float32(exact)) / np.float32(np.log(MAX_DIST / exact))
        far = np.minimum(exact + (far * np.float32(BUCKETS - exact)).astype(np.int32), BUCKETS - 1)
        return np.where(n < exact, n, far)

    hot = np.zeros((BUCKETS + 1, V_ALL), np.float32)

    def put(first, rel, valid):
        cols = first + np.arange(len(rel))
        hot[np.where(valid, bucket(np.maximum(rel, 0)), BUCKETS), cols] = 1.0

    rel = 2 * P - 1 - np.arange(BAND_N)
    put(V_BAND, rel, (rel >= 0) & (rel < P))
    rel = P + META - 1 - np.arange(META_N)
    put(V_NEAR, rel, rel >= 0)
    put(V_FAR, rel + P, rel >= 0)
    hot[:, V_FAR:V_FAR + META_N] = 0.0
    hot[BUCKETS - 1, V_FAR:V_FAR + META_N] = 1.0
    rel = META - 1 - np.arange(SELF_N)
    put(V_SELF, rel, rel >= 0)
    scan = np.ones((P, TOK), np.float32)
    scan[:, 0] = 0.0
    scan[:, META::CH] = 0.0
    return masks, hot, scan


class Phase:

    def __init__(self, kind, layer, slots, cols, before, ffn=None):
        self.kind, self.layer, self.slots, self.cols, self.ffn = kind, layer, slots, cols, ffn
        self.slot0 = before["slots"]
        self.partial = 0 if layer else slots - 1
        self.lead = 1 if kind == "in" and layer else 0
        self.evac0 = before["evac"]
        self.f0 = before["f"]
        self.x0 = before["x"]
        self.a0 = before["a"]
        before["slots"] += slots
        if kind in ("gu", "in"):
            before["evac"] += slots
        if kind == "gu":
            before["a"] += slots // 2
        if kind in ("down", "out"):
            before["f"] += DT


class Norm:

    def __init__(self, layer, post, pre, half, cols, h0, x0, sum0, pair, last, sum_pair):
        self.post_col = None if post is None else (6 * layer + post) * DT
        self.pre_col = None if pre is None else (6 * layer + pre) * DT
        self.half, self.cols, self.h0, self.x0, self.pair, self.last = half, cols, h0, x0, pair, last
        self.f0 = h0 - DT
        self.post_sum = None if post is None else sum0
        self.pre_sum = None if pre is None else sum0 + (post is not None)
        self.posts = max(h0 // DT - 1, 0)
        self.post_added = None if post is None else DT * sum0 - self.posts
        self.pre_added = None if pre is None else DT * self.pre_sum - (self.posts + (post is not None))
        self.sum_pair = sum_pair
        self.copy_pair = (pair + RING - 1) % RING
        self.t0 = META if cols == TAIL else 0
        self.blocks, self.block = (SEQ // P, P) if cols == TAIL else (6, TOK // 6)


class Mix:

    def __init__(self, layer, x0, evac0, slots):
        self.layer, self.x0, self.evac0, self.slots = layer, x0, evac0, slots


def plan(stop=None):
    n = {"slots": 0, "evac": 0, "f": 0, "x": 0, "a": 0}
    steps = []
    norms = 0
    sums = 0

    def norm(layer, post, pre, half, cols, last=False):
        nonlocal norms, sums
        steps.append(("norm", Norm(layer, post, pre, half, cols, h0=norms * DT, x0=n["x"], sum0=sums,
                                   pair=(n["slots"] + RING - 1) % RING, last=last,
                                   sum_pair=(n["slots"] + (RING - 1 if half else RING - 2)) % RING)))
        norms += 1
        sums += (post is not None) + (pre is not None)
        if pre is not None:
            n["x"] += DT

    norm(0, None, 0, False, FULL)
    for layer in range(2):
        cols = FULL
        for ffn in range(2):
            if ffn:
                cols = TAIL if layer else FULL
            steps.append(("dense", Phase("gu", layer, 2 * FT, cols, n, ffn=ffn)))
            steps.append(("dense", Phase("down", layer, 2 * DT, cols, n, ffn=ffn)))
            if stop == (layer, ffn):
                norm(layer, 1 if ffn == 0 else 5, None, True, cols, last=True)
                return steps
            if ffn:
                norm(layer, 5, None if layer else 6, True, cols, last=bool(layer))
                continue
            norm(layer, 1, 2, True, cols)
            steps.append(("dense", Phase("in", layer, (ODD_TILES if layer else EVEN_TILES) + 1, FULL, n)))
            steps.append(("mix", Mix(layer, n["x"], n["evac"], n["slots"])))
            n["x"] += DT
            steps.append(("dense", Phase("out", layer, DT, TAIL if layer else FULL, n)))
            if stop == (layer, "mix"):
                norm(layer, 3, None, False, TAIL if layer else FULL, last=True)
                return steps
            norm(layer, 3, 4, False, TAIL if layer else FULL)
    return steps


def halves(cols):
    if cols == TAIL:
        return [(META, SEQ)]
    return [(0, HALF), (HALF, HALF)]


def token_cols(tile, cols):
    if cols == TAIL:
        return tile[:, META:TOK]
    return tile.rearrange("p (a b) -> p a b", a=2)


def linked(steps):
    queries = [s.slot0 for k, s in steps if k == "dense" and s.kind == "in" and s.layer == 0]
    twice = [first + t for first in queries for t in range(QH // KVH)]
    inverses = 0
    for at, (kind, step) in enumerate(steps):
        if kind == "norm" and step.pre_sum is not None:
            step.next = steps[at + 1][1]
            step.inverses = inverses
            inverses += 1
        if kind == "dense":
            step.before = next((s for k, s in reversed(steps[:at]) if k == "norm"), None)
            step.twice = twice
            step.mix = steps[at + 1][1] if step.kind == "in" else None
            step.after = next((s for k, s in steps[at:] if k == "norm"), None)
    return steps


class Core:

    def __init__(self, nc, ctx, steps):
        self.nc, self.steps = nc, steps
        self.phases = [s for kind, s in steps if kind == "dense"]
        last = [s for kind, s in steps if kind == "norm"][-1]
        self.h_total = last.h0 + DT

        def sb(name, shape, dt=F32):
            return ctx.enter_context(nc.sbuf_tensor(name, shape, dt))

        def sem(name):
            return ctx.enter_context(nc.semaphore(name))

        self.h = sb("h", [P, DT, TOK])
        self.w_hl = sb("w_hl", [P, RING, 2, FH * P], F32R)
        self.stage = sb("stage", [P, 2, FH * P])
        self.rinv = sb("rinv", [P, TOK])
        self.sq_sum = sb("sq_sum", [P, TOK])
        self.t_gate = sb("t_gate", [P, TOK])
        self.t_up = sb("t_up", [P, TOK])
        self.ident = sb("ident", [P, P])
        self.ones = sb("ones", [P, P])
        self.norm_cols = sb("norm_cols", [P, 12 * DT])
        self.vec_cols = sb("vec_cols", [P, 64])
        self.heads = sb("heads", [P, QH + 2 * DH])
        self.eps = sb("eps", [P, 4])
        self.by_token = sb("by_token", [P, 2, 6])
        self.x_at = (nc.sbuf_base + 31) // 32 * 32
        self.x_hl = sb("x_hl", [P, 2, DT, TOK], F32R)
        self.arena = (nc.sbuf_base + 31) // 32 * 32
        self.acts = sb("acts", [P, 2, FT, TOK], F32R)
        self.psum = ctx.enter_context(nc.psum_tensor("psum", [P, 8, 512], F32))
        self.f_down = self.at("f_down", [P, DT, TOK], self.x_at)
        self.f_mix = self.at("f_mix", [P, DT, TOK], self.arena)
        at = self.arena
        def rows_at(name, rows, width):
            nonlocal at
            buf = self.at(name, [rows, width], at)
            at += (4 * width + 31) // 32 * 32
            return buf

        self.rows_x = rows_at("rows_x", P, NBLK * D)
        self.rows_meta = rows_at("rows_meta", META, D)
        self.rows_norm = rows_at("rows_norm", 12 * DT, P)
        self.rows_vec = rows_at("rows_vec", VEC_ROWS, P)
        self.table = rows_at("table", BUCKETS + 1, QH)
        self.bucket_hot = rows_at("bucket_hot", BUCKETS + 1, V_ALL)
        self.bias_row = rows_at("bias_row", QH, V_ALL)
        self.rows_x = self.rows_x[:].rearrange("p (b d) -> p b d", b=NBLK)
        self.rows_out = self.at("rows_out", [P, NBLK, D], self.arena)

        self.w_hi = sem("w_hi")
        self.w_lo = sem("w_lo")
        self.slot_used = sem("slot_used")
        self.scaled = sem("scaled")
        self.gate_silu = sem("gate_silu")
        self.act_full = sem("act_full")
        self.act_hi = sem("act_hi")
        self.act_lo = sem("act_lo")
        self.f_out = sem("f_out")
        self.sq_made = sem("sq_made")
        self.sq_added = sem("sq_added")
        self.sum_ready = sem("sum_ready")
        self.root_ready = sem("root_ready")
        self.rinv_ready = sem("rinv_ready")
        self.f_scaled = sem("f_scaled")
        self.f_scaled_pool = sem("f_scaled_pool")
        self.inverse_ready = sem("inverse_ready")
        self.spread_set = sem("spread_set")
        self.spread_ready = sem("spread_ready")
        self.spread_copied = sem("spread_copied")
        self.table_set = sem("table_set")
        self.h_new = sem("h_new")
        self.x_hi = sem("x_hi")
        self.x_lo = sem("x_lo")
        self.consts_in = sem("consts_in")
        self.vectors_in = sem("vectors_in")
        self.consts_set = sem("consts_set")
        self.cols_ready = sem("cols_ready")
        self.cols_flip = sem("cols_flip")
        self.tok_in = sem("tok_in")
        self.tok_flip = sem("tok_flip")
        self.bias_stored = sem("bias_stored")
        self.out_flip = sem("out_flip")
        self.out_left = sem("out_left")
        self.out_right = sem("out_right")
        self.out_stored = sem("out_stored")
        self.w_landed = [sem("w_landed_0"), sem("w_landed_1")]
        self.sem = sem
        self.tables = 0
        self.even = Even(self)
        self.odd = Odd(self)
        self.proj = [self.even.proj, self.odd.proj]

    def at(self, name, shape, offset, dt=F32):
        return self.nc.alloc_sbuf_tensor_at(name, shape, dt, offset=offset)

    def slot_kind(self, g):
        for p in self.phases:
            if p.slot0 <= g < p.slot0 + p.slots:
                if p.kind == "in" and g == p.slot0 + p.partial:
                    return DT, RANK if p.layer else EVEN_GATES
                return (FH if p.kind == "down" else DT), P
        return None


def shared_pair(phase, s):
    if s < RING:
        return (phase.slot0 + s) % RING
    other = s == RING + 1 or (phase.layer == 1 and GATES_OUT < s < KEYS_FROM and s % 2 == 0)
    return (phase.slot0 + (1 if other else 0)) % RING


def pair_before(phase, s):
    return max(t for t in range(s) if shared_pair(phase, t) == shared_pair(phase, s))


class Slot:

    def __init__(self, phase, i, u, off=0):
        self.i, self.u, self.off = i, u, off
        self.base = phase.slot0 + u + off
        self.local = i * RING + (u + off)
        self.ring = self.base % RING
        self.stage = self.base % 2
        self.pair = self.ring
        self.peeled = isinstance(i, int)
        if phase.mix is not None and self.peeled:
            self.pair = shared_pair(phase, self.local)
        self.twice = phase.twice

    def count(self, lag=0):
        return self.i * RING + (self.base + 1 - lag)

    def landed(self):
        first = self.base + RING * (self.i if self.peeled else 1)
        twice = [g for g in self.twice if g <= first and g % 2 == self.stage]
        return self.i * (16 * RING // 2) + 16 * (self.base // 2 + 1 + len(twice))


def walk(core, phase, engine, step, ahead=0, between=None):
    if between is not None and phase.mix is not None:
        for s in range(phase.slots):
            step(s // RING, s % RING)
            between[phase.layer](core, engine, phase.mix, s)
        return
    whole = phase.slots - (1 if phase.kind == "in" and not phase.lead else 0)
    bodies = (whole - ahead) // RING
    for u in range(RING):
        step(0, u)
    if bodies > 2:
        with engine.Fori(1, bodies) as i:
            for u in range(RING):
                step(i, u)
    else:
        bodies = 1
    for s in range(bodies * RING, phase.slots):
        step(s // RING, s % RING)


def weights(buf, tiles, cols):
    view = buf.rearrange("p (k n) -> p k n", n=P)[:, 0:tiles, :]
    return view if cols == P else view[:, :, 0:cols]


def split_hi(core, act, slot, kind):
    act.wait_ge(core.w_landed[slot.stage], slot.landed())
    if not slot.peeled or slot.count() > RING:
        act.wait_ge(core.slot_used, slot.count(RING))
    act.activation(weights(core.w_hl[:, slot.ring, 0, :], *kind), weights(core.stage[:, slot.stage, :], *kind),
                   ACT.Copy).then_inc(core.w_hi, 1)


def split_lo(core, dve, slot, kind):
    dve.wait_ge(core.w_hi, slot.count())
    dve.tensor_tensor(weights(core.w_hl[:, slot.ring, 1, :], *kind), weights(core.stage[:, slot.stage, :], *kind),
                      weights(core.w_hl[:, slot.ring, 0, :].bitcast(F32), *kind), ALU.subtract).then_inc(core.w_lo, 1)


def split_ahead(core, engine, half, phase, i, u):
    slot = Slot(phase, i, u, AHEAD)
    g = phase.slot0 + (i * RING if isinstance(i, int) else RING) + u + AHEAD
    kind = core.slot_kind(g)
    if kind:
        half(core, engine, slot, kind)



def sync_program(core, sp, a):
    sp.dma_start(core.rows_x, a["x"][0].rearrange("(b p) d -> p b d", p=P)).then_inc(core.tok_in, 16)
    sp.dma_start(core.rows_meta[:, :], a["meta_tokens"]).then_inc(core.tok_in, 16)
    for kind, phase in core.steps:
        if kind == "dense":
            walk(core, phase, sp, lambda i, u, ph=phase: load_slot(core, sp, a, ph, i, u))
    for b in range(NBLK):
        sp.wait_ge(core.out_left, b + 1)
        sp.wait_ge(core.out_right, b + 1)
        sp.dma_start(a["out"][0, b * P:(b + 1) * P, :], core.rows_out[:, b, :]).then_inc(core.out_stored, 16)
    sp.wait_ge(core.out_stored, 16 * NBLK)


def load_slot(core, sp, a, phase, i, u):
    slot = Slot(phase, i, u)
    if not slot.peeled or slot.count() > 2:
        sp.wait_ge(core.w_lo, slot.count(2))
    dst = core.stage[:, slot.stage, :]
    if phase.kind == "gu":
        w = (a["ffn_w_up"] if u % 2 else a["ffn_w_gate"])[phase.layer, phase.ffn]
        col, n, rows = (i * 2 + u // 2) * P, P, w
    elif phase.kind == "down":
        w = a["ffn_w_down"][phase.layer, phase.ffn]
        half = u % 2
        col, n, rows = (i * 2 + u // 2) * P, P, w[half * FH * P:(half + 1) * FH * P]
    else:
        rows = {("in", 0): a["even_w_in"], ("in", 1): a["odd_w_in"],
                ("out", 0): a["even_w_out"], ("out", 1): a["odd_w_out"]}[phase.kind, phase.layer][0]
        col, n = (slot.local - phase.lead) * P, P
        if phase.kind == "in" and slot.peeled and slot.local == phase.partial:
            col = (phase.slots - 1) * P
            n = RANK if phase.layer else EVEN_GATES
    tiles = FH if phase.kind == "down" else DT
    dst = weights(dst, tiles, n)
    if phase.kind == "in" and phase.layer == 0 and slot.peeled and slot.local < QH // KVH:
        src = rows[:, 0:QH * HD].rearrange("(k p) (g h d) -> h p k g d", p=P, g=KVH, d=HD)[slot.local]
        dst = dst.rearrange("p k (g d) -> p k g d", g=KVH)
        for g in range(KVH):
            sp.dma_start(dst[:, :, g, :], src[:, :, g, :]).then_inc(core.w_landed[slot.stage], 16)
        return
    src = rows[:, bass.ds(col, n)].rearrange("(k p) n -> p k n", p=P)
    sp.dma_start(dst, src).then_inc(core.w_landed[slot.stage], 16)



def products(core, pe, phase, slot, kt, w_tile, moving, first, last):
    for part, moved in ((0, 0), (0, 1), (1, 0)):
        lhs = core.w_hl[:, slot.ring, part, w_tile * P:(w_tile + 1) * P]
        for b, (t0, n) in enumerate(halves(phase.cols)):
            out = core.psum[:, 2 * slot.out_pair + b, 0:n]
            op = pe.matmul(out, lhs, moving[:, moved, kt, t0:t0 + n], start=first and part + moved == 0,
                           stop=last and part == 1)
    return op


def tensor_dense(core, pe, phase):
    k = core

    def weights_ready(slot):
        pe.wait_ge(k.w_lo, slot.count())

    if phase.kind == "down":
        def step(i, u):
            slot = Slot(phase, i, u)
            slot.out_pair = (phase.slot0 + u - u % 2) % RING
            m = i * 2 + u // 2
            weights_ready(slot)
            if u % 2 == 0:
                if isinstance(i, int) and i == 0:
                    pe.wait_ge(k.scaled, phase.evac0 - RING + 1 + u)
                else:
                    pe.wait_ge(k.f_out, m + (phase.f0 - 1))
            for kk in range(FH):
                kt = (u % 2) * FH + kk
                if isinstance(i, int) and i == 0 and u < 2:
                    pe.wait_ge(k.act_lo, phase.a0 - FT + kt + 1)
                op = products(k, pe, phase, slot, kt, kk, k.acts, kt == 0, kt == FT - 1)
            op.then_inc(k.slot_used, 1)

        walk(k, phase, pe, step)
        return

    if phase.kind == "out" and phase.layer == 0:
        even_banks_read(k, pe)
    elif phase.kind != "out" and phase.before.post_sum is not None:
        pe.wait_ge(k.spread_copied, phase.before.posts + 1)
    group = [Slot(phase, 0, u) for u in range(RING - 1)]
    for slot in group:
        weights_ready(slot)
        slot.out_pair = slot.pair
    for kt in range(DT):
        pe.wait_ge(k.x_lo, phase.x0 - DT + kt + 1)
        for slot in group:
            if kt == DT - 1 and slot is group[-1] and phase.kind != "out":
                if phase.before.post_sum is not None:
                    pe.wait_ge(k.f_scaled, (phase.before.posts + 1) * (DT - POOL_SCALES))
                token_sum(k, pe, phase.before, phase.before.pre_sum)
            op = products(k, pe, phase, slot, kt, kt, k.x_hl, kt == 0, kt == DT - 1)
            if kt == DT - 1:
                op.then_inc(k.slot_used, 1)

    def step(i, u):
        if isinstance(i, int) and i == 0 and u < RING - 1:
            return
        slot = Slot(phase, i, u)
        slot.out_pair = slot.pair
        weights_ready(slot)
        if phase.kind != "out" and isinstance(i, int) and i == 0:
            pe.wait_ge(k.root_ready, phase.before.pre_sum + 1)
        elif not (isinstance(i, int) and i == 0):
            if phase.mix is not None:
                pe.wait_ge(k.scaled, phase.evac0 + pair_before(phase, slot.local) + 1)
                if phase.layer == 1 and slot.local == GATES_OUT + 2:
                    pe.wait_ge(k.odd.s_gate_x, GH)
            elif phase.kind == "out":
                pe.wait_ge(k.f_out, i * RING + (u + phase.f0 - RING + 1))
            else:
                pe.wait_ge(k.scaled, i * RING + (u + phase.evac0 - RING + 1))
        for kt in range(DT):
            op = products(k, pe, phase, slot, kt, kt, k.x_hl, kt == 0, kt == DT - 1)
        op.then_inc(k.slot_used, 1)

    walk(k, phase, pe, step, between=(even_tensor_between, odd_tensor_between))


def token_sum(core, pe, norm, n):
    pe.wait_ge(core.sq_added, norm.pre_added + DT)
    for b, (t0, w) in enumerate(halves(norm.cols)):
        op = pe.matmul(core.psum[:, 2 * norm.pair + b, 0:w], core.ones[:], core.sq_sum[:, t0:t0 + w],
                       start=True, stop=True)
    op.then_inc(core.sum_ready, 1)


def token_factors(core, pe, norm):
    k, n = core, norm.post_sum
    squares = (k.sq_sum, k.t_up)
    pe.wait_ge(k.f_out, norm.f0 + DT - 1)
    for part, buf in enumerate(squares):
        if part == 0:
            pe.wait_ge(k.sq_added, norm.post_added + DT - 1)
        else:
            pe.wait_ge(k.sq_made, DT * (n + 1))
        for c in range(norm.blocks):
            t0 = norm.t0 + c * norm.block
            at = part * norm.blocks + c
            op = pe.matmul(k.psum[0:norm.block, 2 * norm.sum_pair, at:at + 1], buf[:, t0:t0 + norm.block],
                           k.ones[:, 0:1], start=True, stop=True)
    op.then_inc(k.sum_ready, 1)
    pe.wait_ge(k.spread_set, norm.posts + 1)
    pe.wait_ge(k.f_out, norm.f0 + DT)
    cols = norm.blocks * norm.block
    for pair in (norm.pair, norm.copy_pair):
        for b, (t0, w) in enumerate(halves(norm.cols)):
            at = b * cols // len(halves(norm.cols))
            op = pe.matmul(k.psum[:, 2 * pair + b, 0:w], k.ones[0:norm.block, :], k.t_gate[0:norm.block, at:at + w],
                           start=True, stop=True)
        op.then_inc(k.spread_ready, 1)


def tensor_program(core, pe):
    k = core
    pe.wait_ge(k.consts_set, 5)
    pe.wait_ge(k.vectors_in, 16 * SCALAR_LOADS)
    pe.wait_ge(k.consts_in, 16 * (CONST_LOADS - SCALAR_LOADS))
    pe.transpose(k.psum[:, 0, 0:12 * DT], k.rows_norm[0:12 * DT, :], k.ident[0:12 * DT, 0:12 * DT])
    pe.transpose(k.psum[:, 1, 0:VEC_ROWS], k.rows_vec[0:VEC_ROWS, :], k.ident[0:VEC_ROWS, 0:VEC_ROWS])
    pe.matmul(k.psum[0:QH, 2, 0:512], k.table[:], k.bucket_hot[:, 0:512], start=True, stop=True)
    pe.matmul(k.psum[0:QH, 3, 0:V_ALL - 512], k.table[:], k.bucket_hot[:, 512:V_ALL], start=True,
              stop=True).then_inc(k.cols_flip, 1)
    pe.wait_ge(k.tok_in, 32)
    for kt in range(DT):
        pair = (kt + 2) % RING
        if kt >= 2:
            pe.wait_ge(k.h_new, max(kt - RING + 1, 1))
            pe.wait_ge(k.cols_ready, 4)
        pe.transpose(k.psum[:, 2 * pair, 0:META], k.rows_meta[0:META, kt * P:(kt + 1) * P], k.ident[0:META, 0:META])
        for b in range(NBLK):
            at = META + b * P if b < 2 else (b - 2) * P
            op = pe.transpose(k.psum[:, 2 * pair + b // 2, at:at + P], k.rows_x[:, b, kt * P:(kt + 1) * P], k.ident[:])
        op.then_inc(k.tok_flip, 1)
    pe.wait_ge(k.h_new, DT)
    for kind, step in k.steps:
        if kind == "dense":
            tensor_dense(k, pe, step)
        elif kind == "norm":
            if step.post_sum is not None:
                token_factors(k, pe, step)
        elif step.layer == 0:
            even_tensor(k, pe, step)
        else:
            odd_tensor(k, pe, step)
    for b in range(NBLK):
        if b >= 2:
            pe.wait_ge(k.out_left, b - 1)
            pe.wait_ge(k.out_right, b - 1)
        for kt in range(DT):
            if b % 2 == 0:
                pe.wait_ge(k.h_new, k.h_total - DT + b // 2 * DT + kt + 1)
            bank = 4 * (b % 2) + kt // 4
            op = pe.transpose(k.psum[:, bank, (kt % 4) * P:(kt % 4 + 1) * P],
                              k.h[:, kt, META + b * P:META + (b + 1) * P], k.ident[:])
            if kt % 4 == 3:
                op.then_inc(k.out_flip, 1)



def const_rows(k, a):
    loads = [
        (k.ident[:, :], a["masks"][:, C_ID:C_ID + P]),
        (k.rows_norm[0:12 * DT, :], a["norm_w"].rearrange("l n (k p) -> (l n k) p", p=P)),
        (k.rows_vec[0:48, :], a["even_conv_w"][0].rearrange("c (k p) -> (c k) p", p=P)),
        (k.rows_vec[48:52, :], a["gla_b_gate"][0:1, :].rearrange("a (k p) -> (a k) p", p=P)),
        (k.rows_vec[52:54, :], a["gla_norm_w"][0:1, :].rearrange("a (k p) -> (a k) p", p=P)),
        (k.rows_vec[54:55, :], a["dn_norm_w"][0:1, :]),
        (k.table[0:BUCKETS, :], a["rel_bias_table"]),
        (k.bucket_hot[:, :], a["bucket_hot"]),
        (k.heads[:, 0:QH], a["swa_sinks"][0:1, :].broadcast_to([P, QH])),
        (k.heads[:, QH:QH + DH], a["dn_a_log"][0:1, :].broadcast_to([P, DH])),
        (k.heads[:, QH + DH:QH + 2 * DH], a["dn_dt_bias"][0:1, :].broadcast_to([P, DH])),
    ]
    assert len(loads) == CONST_LOADS
    return loads


def bank_cols(core, pair, cols):
    if cols == TAIL:
        return core.psum[:, 2 * pair, 0:SEQ]
    return core.psum[:, 2 * pair:2 * pair + 2, 0:HALF]


def root(core, act, norm, n):
    k = core
    act.wait_ge(k.sum_ready, n + 1)
    act.activation(token_cols(k.rinv[:, :], norm.cols), bank_cols(k, norm.pair, norm.cols), ACT.Sqrt,
                   bias=k.eps[:, 0:1], scale=1.0 / D).then_inc(k.root_ready, 1)


def load_table(core, act, func):
    core.tables += 1
    if core.tables > 1:
        act.wait_ge(core.table_set, core.tables - 1)
    act.activation(core.eps[0:1, 3:4], core.eps[0:1, 0:1], func).then_inc(core.table_set, 1)


def scalar_norm(core, act, norm):
    k = core
    if norm.post_sum is not None:
        act.wait_ge(k.inverse_ready, 2 * norm.posts + 1)
        act.activation(k.by_token[0:norm.block, 0, 0:norm.blocks], k.by_token[0:norm.block, 1, 0:norm.blocks], ACT.Sqrt,
                       bias=k.eps[0:norm.block, 1:2] if norm.half else k.eps[0:norm.block, 0:1],
                       scale=(4.0 if norm.half else 1.0) / D).then_inc(k.root_ready, 1)
        act.wait_ge(k.spread_ready, 2 * norm.posts + 2)
        act.activation(token_cols(k.rinv[:, :], norm.cols), bank_cols(k, norm.copy_pair, norm.cols), ACT.Copy)\
            .then_inc(k.spread_copied, 1)
    else:
        load_table(k, act, ACT.Sqrt)
    if norm.pre_sum is None:
        return
    for kt in range(DT):
        act.wait_ge(k.h_new, norm.h0 + kt + 1)
        tile = k.h[:, kt, norm.t0:TOK]
        col = norm.pre_col + kt
        act.activation(k.x_hl[:, 0, kt, norm.t0:TOK], tile, ACT.Copy,
                       scale=k.norm_cols[:, col:col + 1]).then_inc(k.x_hi, 1)
        if kt >= 2:
            act.wait_ge(k.sq_added, norm.pre_added + kt - 1)
        buf = k.t_up if kt % 2 else k.t_gate
        act.activation(buf[:, norm.t0:TOK], tile, ACT.Square).then_inc(k.sq_made, 1)
        if kt == DT // 2:
            split_ahead(k, act, split_hi, norm.next, 0, 0)
    root(k, act, norm, norm.pre_sum)
    if norm.next.kind == "gu":
        load_table(k, act, ACT.Silu)


def scalar_dense(core, act, phase):
    k = core
    early = phase.kind in ("gu", "in")
    if not early:
        load_table(k, act, ACT.Sqrt)

    def step(i, u):
        if early and isinstance(i, int) and i == 0 and u < 2:
            if u == 0:
                split_ahead(k, act, split_hi, phase, 0, 1)
        else:
            split_ahead(k, act, split_hi, phase, i, u)
        slot = Slot(phase, i, u)
        if phase.kind == "gu":
            t = i * 2 + u // 2
            if u % 2 == 0:
                act.wait_ge(k.scaled, slot.local + (phase.evac0 + 1))
                act.activation(token_cols(k.t_gate[:, :], phase.cols), token_cols(k.t_gate[:, :], phase.cols),
                               ACT.Silu).then_inc(k.gate_silu, 1)
            else:
                act.wait_ge(k.act_full, t + (phase.a0 + 1))
                act.activation(token_cols(tile_at(k.acts[:, 0], t), phase.cols), token_cols(k.t_up[:, :], phase.cols),
                               ACT.Copy).then_inc(k.act_hi, 1)
        elif phase.kind == "down" and u % 2:
            pair = (phase.slot0 + u - 1) % RING
            result_tile(k, act, phase, slot, pair, i * 2 + u // 2, u // 2, k.f_down)
        elif phase.kind == "out":
            result_tile(k, act, phase, slot, slot.pair, slot.local, u % 2, k.f_mix)

    walk(k, phase, act, step, AHEAD, (even_scalar_between, odd_scalar_between))


def tile_at(buf, t):
    if isinstance(t, int):
        return buf[:, t, :]
    return buf[:, bass.ds(t, 1), :].rearrange("p a t -> p (a t)")


def result_tile(core, act, phase, slot, pair, m, odd, buf):
    k, norm = core, phase.after
    src = bank_cols(k, pair, phase.cols)
    act.wait_ge(k.slot_used, slot.count())
    if not (isinstance(m, int) and m < 2):
        act.wait_ge(k.sq_added, m + (norm.post_added - 1))
    squares = k.t_up if odd else k.t_gate
    act.activation(token_cols(squares[:, :], phase.cols), src, ACT.Square).then_inc(k.sq_made, 1)
    col = norm.post_col + m
    scale = k.norm_cols[:, col:col + 1] if isinstance(m, int) else k.norm_cols[:, bass.ds(col, 1)]
    act.activation(token_cols(tile_at(buf, m), phase.cols), src, ACT.Copy, scale=scale).then_inc(k.f_out, 1)


def scalar_program(core, act, a):
    k = core
    for dst, src in const_rows(k, a)[0:SCALAR_LOADS]:
        act.dma_start(dst, src).then_inc(k.vectors_in, 16)
    split_hi(k, act, Slot(k.phases[0], 0, 0), (DT, P))
    act.wait_ge(k.cols_flip, 1)
    act.activation(k.norm_cols[:, :], k.psum[:, 0, 0:12 * DT], ACT.Copy).then_inc(k.cols_ready, 1)
    act.activation(k.vec_cols[:, 0:VEC_ROWS], k.psum[:, 1, 0:VEC_ROWS], ACT.Copy).then_inc(k.cols_ready, 1)
    act.activation(k.bias_row[0:QH, 0:512], k.psum[0:QH, 2, 0:512], ACT.Copy).then_inc(k.cols_ready, 1)
    act.activation(k.bias_row[0:QH, 512:V_ALL], k.psum[0:QH, 3, 0:V_ALL - 512], ACT.Copy).then_inc(k.cols_ready, 1)
    act.wait_ge(k.consts_set, 5)
    for u in range(1, AHEAD):
        split_hi(k, act, Slot(k.phases[0], 0, u), (DT, P))
    act.wait_ge(k.bias_stored, 16)
    for kind, step in k.steps:
        if kind == "dense":
            scalar_dense(k, act, step)
        elif kind == "norm":
            scalar_norm(k, act, step)
        elif step.layer == 0:
            even_scalar(k, act, step)
        else:
            odd_scalar(k, act, step)
    for b in range(NBLK):
        act.wait_ge(k.out_flip, 2 * b + 1)
        act.activation(k.rows_out[:, b, 0:512], k.psum[:, 4 * (b % 2), :], ACT.Copy).then_inc(k.out_left, 1)



def vector_last(core, dve, norm, f):
    k = core
    dve.wait_ge(k.spread_copied, norm.posts + 1)

    def scale(kt):
        tile = f[:, kt, norm.t0:MIDDLE]
        dve.tensor_tensor(tile, tile, k.rinv[:, norm.t0:MIDDLE], ALU.mult).then_inc(k.f_scaled, 1)

    scale(0)
    for kt in range(DT):
        if kt + 1 < DT:
            scale(kt + 1)
        dve.wait_ge(k.f_scaled, norm.posts * (DT - POOL_SCALES) + kt + 1)
        h = k.h[:, kt, norm.t0:MIDDLE]
        dve.tensor_tensor(h, h, f[:, kt, norm.t0:MIDDLE], ALU.add).then_inc(k.h_new, 1)
    for kt in range(DT):
        dve.wait_ge(k.f_scaled_pool, norm.posts * POOL_SCALES + kt + 1)
        h = k.h[:, kt, MIDDLE:TOK]
        dve.tensor_tensor(h, h, f[:, kt, MIDDLE:TOK], ALU.add).then_inc(k.h_new, 1)


def vector_norm(core, dve, norm):
    k, t0 = core, norm.t0
    if norm.post_sum is not None:
        f = k.f_down if norm.half else k.f_mix
        n, blocks = norm.block, norm.blocks
        dve.wait_ge(k.sum_ready, norm.post_sum + 1)
        part = k.psum[0:n, 2 * norm.sum_pair, 0:2 * blocks]
        dve.tensor_reduce(k.by_token[0:n, 1, 0:blocks], part.rearrange("p (a b) -> p b a", a=2), AX.X, ALU.add)\
           .then_inc(k.inverse_ready, 1)
        dve.wait_ge(k.root_ready, norm.post_sum + 1)
        dve.reciprocal(k.by_token[0:n, 0, 0:blocks], k.by_token[0:n, 0, 0:blocks]).then_inc(k.inverse_ready, 1)
        dve.wait_ge(k.inverse_ready, 2 * norm.posts + 2)
        dve.tensor_tensor(k.t_gate[0:n, 0:blocks * n].rearrange("p (b q) -> p b q", q=n),
                          k.ident[0:n, 0:n].unsqueeze(1).broadcast_to([n, blocks, n]),
                          k.by_token[0:n, 0, 0:blocks].unsqueeze(2).broadcast_to([n, blocks, n]), ALU.mult)\
           .then_inc(k.spread_set, 1)
        if norm.last:
            vector_last(k, dve, norm, f)
            return
        dve.wait_ge(k.spread_ready, 2 * norm.posts + 1)
        shared = POOL_SCALES
        scaled0 = norm.posts * (DT - POOL_SCALES)

    def scale_f(kt):
        if kt >= DT - shared:
            return
        tile = token_cols(f[:, kt, :], norm.cols)
        dve.tensor_tensor(tile, tile, bank_cols(k, norm.pair, norm.cols), ALU.mult).then_inc(k.f_scaled, 1)

    def lo(kt):
        dve.wait_ge(k.x_hi, norm.x0 + kt + 1)
        col = norm.pre_col + kt
        dve.scalar_tensor_tensor(k.x_hl[:, 1, kt, t0:TOK], k.h[:, kt, t0:TOK], k.norm_cols[:, col:col + 1],
                                 k.x_hl[:, 0, kt, t0:TOK].bitcast(F32), ALU.mult, ALU.subtract).then_inc(k.x_lo, 1)

    def add(kt):
        if kt < DT - shared:
            dve.wait_ge(k.f_scaled, scaled0 + kt + 1)
        else:
            dve.wait_ge(k.f_scaled_pool, norm.posts * POOL_SCALES + kt - (DT - POOL_SCALES) + 1)
        dve.tensor_tensor(k.h[:, kt, t0:TOK], k.h[:, kt, t0:TOK], f[:, kt, t0:TOK], ALU.add).then_inc(k.h_new, 1)

    if norm.post_sum is not None:
        scale_f(0)
        add(0)
    for kt in range(DT):
        following = norm.post_sum is not None and kt + 1 < DT
        if following:
            scale_f(kt + 1)
        if norm.pre_sum is not None:
            lo(kt)
        if following:
            add(kt + 1)
    if norm.pre_sum is not None:
        split_ahead(k, dve, split_lo, norm.next, 0, 0)
        dve.wait_ge(k.root_ready, norm.pre_sum + 1)
        dve.reciprocal(k.rinv[:, t0:TOK], k.rinv[:, t0:TOK]).then_inc(k.rinv_ready, 1)


def vector_dense(core, dve, phase):
    k = core

    def step(i, u):
        slot = Slot(phase, i, u)
        src = bank_cols(k, slot.pair, phase.cols)
        rinv = token_cols(k.rinv[:, :], phase.cols)
        if phase.kind not in ("gu", "in"):
            split_ahead(k, dve, split_lo, phase, i, u)
            return
        if slot.peeled and slot.local == 0:
            dve.wait_ge(k.rinv_ready, phase.before.inverses + 1)
        dve.wait_ge(k.slot_used, slot.count())
        if phase.kind == "in":
            rows = P
            at = slot.local - phase.lead
            if slot.local == phase.partial:
                at = phase.slots - 1
                rows = RANK if phase.layer else EVEN_GATES
            if slot.peeled:
                tile = k.proj[phase.layer][0:rows, at, :]
                src = k.psum[0:rows, 2 * slot.pair:2 * slot.pair + 2, 0:HALF]
                rinv = token_cols(k.rinv[0:rows, :], phase.cols)
            dve.tensor_tensor(token_cols(tile, FULL), src, rinv, ALU.mult).then_inc(k.scaled, 1)
        elif u % 2 == 0:
            dve.tensor_tensor(token_cols(k.t_gate[:, :], phase.cols), src, rinv, ALU.mult).then_inc(k.scaled, 1)
        else:
            t = i * 2 + u // 2
            if not (slot.peeled and slot.local == 1 and phase.a0 == 0):
                dve.wait_ge(k.act_lo, t + phase.a0)
            up, gate = token_cols(k.t_up[:, :], phase.cols), token_cols(k.t_gate[:, :], phase.cols)
            dve.tensor_tensor(up, src, rinv, ALU.mult).then_inc(k.scaled, 1)
            dve.wait_ge(k.scaled, slot.local + (phase.evac0 + 1))
            dve.wait_ge(k.gate_silu, t + (phase.a0 + 1))
            dve.tensor_tensor(up, up, gate, ALU.mult).then_inc(k.act_full, 1)
        if slot.peeled and slot.local < 2:
            if slot.local == 0:
                split_ahead(k, dve, split_lo, phase, 0, 1)
        else:
            split_ahead(k, dve, split_lo, phase, i, u)
        if phase.kind == "gu" and u % 2:
            dve.wait_ge(k.act_hi, t + (phase.a0 + 1))
            hi = token_cols(tile_at(k.acts[:, 0], t), phase.cols).bitcast(F32)
            dve.tensor_tensor(token_cols(tile_at(k.acts[:, 1], t), phase.cols), up, hi, ALU.subtract)\
               .then_inc(k.act_lo, 1)

    walk(k, phase, dve, step, AHEAD, (even_vector_between, odd_vector_between))


def vector_program(core, dve):
    k = core
    dve.memset(k.ones[:, :], 1.0).then_inc(k.consts_set, 1)
    dve.memset(k.eps[:, 0:1], EPS).then_inc(k.consts_set, 1)
    dve.memset(k.eps[:, 1:2], 4 * EPS).then_inc(k.consts_set, 1)
    dve.memset(k.eps[:, 2:3], DN_DIM * EPS).then_inc(k.consts_set, 1)
    dve.memset(k.table[BUCKETS:BUCKETS + 1, :], MASKED).then_inc(k.consts_set, 1)
    split_lo(k, dve, Slot(k.phases[0], 0, 0), (DT, P))
    for kt in range(DT):
        pair = (kt + 2) % RING
        dve.wait_ge(k.tok_flip, kt + 1)
        dve.tensor_copy(k.h[:, kt, 0:META + 2 * P], k.psum[:, 2 * pair, 0:META + 2 * P])
        dve.tensor_copy(k.h[:, kt, META + 2 * P:TOK], k.psum[:, 2 * pair + 1, 0:2 * P]).then_inc(k.h_new, 1)
        if kt == DT // 2:
            split_lo(k, dve, Slot(k.phases[0], 0, 1), (DT, P))
    split_lo(k, dve, Slot(k.phases[0], 0, 2), (DT, P))
    for kind, step in k.steps:
        if kind == "dense":
            vector_dense(k, dve, step)
        elif kind == "norm":
            vector_norm(k, dve, step)
        elif step.layer == 0:
            even_vector(k, dve, step)
        else:
            odd_vector(k, dve, step)
    for b in range(NBLK):
        dve.wait_ge(k.out_flip, 2 * b + 2)
        dve.tensor_copy(k.rows_out[:, b, 512:D], k.psum[:, 4 * (b % 2) + 1, :]).then_inc(k.out_right, 1)



def add_squares(core, pool, n, cols, added, tiles):
    k = core
    t0 = META if cols == TAIL else 0
    for m in range(tiles):
        buf = (k.t_up if m % 2 else k.t_gate)[:, t0:TOK]
        if m == 0:
            if n:
                pool.wait_ge(k.sum_ready, n)
            pool.wait_ge(k.sq_made, DT * n + 1)
            pool.tensor_copy(k.sq_sum[:, t0:TOK], buf).then_inc(k.sq_added, 1)
        else:
            pool.wait_ge(k.sq_made, DT * n + m + 1)
            pool.wait_ge(k.sq_added, added + m)
            pool.tensor_tensor(k.sq_sum[:, t0:TOK], k.sq_sum[:, t0:TOK], buf, ALU.add).then_inc(k.sq_added, 1)


def scale_results(core, pool, norm):
    k = core
    pool.wait_ge(k.spread_copied, norm.posts + 1)
    f = k.f_down if norm.half else k.f_mix
    t0 = MIDDLE if norm.last else norm.t0
    for kt in range(0 if norm.last else DT - POOL_SCALES, DT):
        tile = f[:, kt, t0:TOK]
        pool.tensor_tensor(tile, tile, k.rinv[:, t0:TOK], ALU.mult).then_inc(k.f_scaled_pool, 1)


def gpsimd_program(core, pool, a):
    k = core
    for dst, src in const_rows(k, a)[SCALAR_LOADS:]:
        pool.dma_start(dst, src).then_inc(k.consts_in, 16)
    pool.wait_ge(k.cols_ready, 4)
    pool.dma_start(a["bias_scratch"], k.bias_row[0:QH, :]).then_inc(k.bias_stored, 16)
    for kind, step in k.steps:
        if kind == "norm":
            if step.post_sum is not None:
                add_squares(k, pool, step.post_sum, step.cols, step.post_added, DT - 1)
            if step.post_sum is not None:
                scale_results(k, pool, step)
            if step.pre_sum is not None:
                add_squares(k, pool, step.pre_sum, step.cols, step.pre_added, DT)
        elif kind == "mix" and step.layer == 0:
            even_gpsimd(k, pool, step, a)
        elif kind == "mix":
            odd_gpsimd(k, pool, step, a)
    pool.wait_ge(k.bias_stored, 16)



Q_TILE, K_TILE, V_TILE, DN_TILE, Z_TILE, GATE_TILE = 0, 4, 5, 6, 18, 22
BANDS = META + 2 * P
BLOCKS = [(0, META)] + [(META + b * P, P) for b in range(NBLK)]
UNITS = [(b, kv) for b in range(NBLK + 1) for kv in range(KVH)]
LAST_SLOT = GATE_TILE
SCORED_AT = {5: [0, 1]}
PROBS_AT = {5: [0, 1]}
FLIPPED_AT = {6: [0], 7: [1]}
OUTPUT_AT = {7: [0], 8: [1]}
for unit in range(2, len(UNITS)):
    SCORED_AT[2 * unit + 2] = [unit]
    PROBS_AT[2 * unit + 3] = [unit]
    FLIPPED_AT[2 * unit + 4] = [unit]
    OUTPUT_AT[2 * unit + 5] = [unit]
FLIPS_AT = 5
SILU_AT = {11: 0, 15: DH, 19: 2 * DH}
SUMS_AT = {13: 0, 17: DH}
SUMS_READ_AT = 17
SUMS_COL = 2 * P + GRP * META
BIAS_FLIPS = QH + 2
FLIP_BANKS = (2, 3, 6, 7)


class Even:

    def __init__(self, core):
        at, a, x = core.at, core.arena, core.x_at
        tile = 4 * TOK
        self.proj = at("even_proj", [P, EVEN_TILES + 1, TOK], a)
        self.o_swa = at("o_swa", [P, 4, TOK], a)
        self.conv_k = at("conv_k", [P, DH, TOK], a + DN_TILE * tile)
        self.conv_v = at("conv_v", [P, DH, TOK], a + (DN_TILE + DH) * tile)
        self.conv_q = at("conv_q", [P, DH, TOK], a + 23 * tile)
        self.o_dn = at("o_dn", [P, DH, TOK], a + (DN_TILE + DH) * tile)
        self.squares = at("conv_squares", [P, DH, TOK], a + Z_TILE * tile)
        rows = a + Z_TILE * tile
        self.bias_rows = at("bias_rows", [P, QH, BANDS], rows)
        self.near_rows = at("near_rows", [P, QH, META], rows + 8704)
        self.self_rows = at("self_rows", [META, QH, META], rows + 9216)
        free = a + 27 * tile
        self.bias = at("bias", [P, QH, BANDS], free)
        self.bias_near = at("bias_near", [P, QH, META], free + 8704)
        self.bias_self = at("bias_self", [META, QH, META], free + 9216)
        self.flip = at("flip", [P, P], free + 9728)
        self.scores = at("scores", [P, 2, GRP, BANDS], free + 10240)
        self.probs_t = at("probs_t", [P, 3, GRP * P], free + 18944)
        self.v_rows = at("v_rows", [P, NBLK + 1, P], free + 25088)
        self.stats = at("swa_stats", [P, 2, 6, GRP], free + 27648)
        self.masks = at("dn_masks", [P, 9, P], free + 27840)
        self.gates = at("dn_gates", [P, 12, NBLK + 1, DH], free + 27840 + 4608)

        big = 4 * (NBLK + 1) * DH * P
        self.wide = at("dn_wide", [P, 2, DH * P], a + 14 * tile)
        self.wide2 = at("dn_wide2", [P, 2, DH * P], a + 14 * tile + 4096)
        self.half_x = at("half_x", [P, NBLK + 1, DH, P], free)
        self.u = at("dn_u", [P, NBLK + 1, DH, P], free)
        self.attn = at("dn_attn", [P, NBLK + 1, DH, P], free + big)
        self.a_t = at("dn_a", [P, NBLK + 1, DH, P], x)
        self.k_dec = at("dn_k_dec", [P, NBLK + 1, DH, P], x)
        self.inv = at("dn_inv", [P, NBLK + 1, DH, P], x + big)
        self.w_t = at("dn_w", [P, NBLK + 1, DH, P], x + big)
        self.inv_t = at("dn_inv_t", [P, NBLK + 1, DH, P], x + 2 * big)
        self.wide3 = at("dn_wide3", [P, DH * P], x + 3 * big)
        self.rows_in = core.sem("e_rows_in")
        self.masks_in = core.sem("e_masks_in")
        self.v_flip = core.sem("e_v_flip")
        self.bias_flip = core.sem("e_bias_flip")
        self.v_rows_set = core.sem("e_v_rows_set")
        self.bias_set = core.sem("e_bias_set")
        self.scored = core.sem("e_scored")
        self.s_made = core.sem("e_s_made")
        self.exped = core.sem("e_exped")
        self.probs = core.sem("e_probs")
        self.p_flip = core.sem("e_p_flip")
        self.p_copied = core.sem("e_p_copied")
        self.o_made = core.sem("e_o_made")
        self.o_copied = core.sem("e_o_copied")
        self.conv_first = core.sem("e_conv_first")
        self.conv_tap = core.sem("e_conv_tap")
        self.conv_done = core.sem("e_conv_done")
        self.conv_sq = core.sem("e_conv_sq")
        self.gate_flip = core.sem("e_gate_flip")
        self.gates_dve = core.sem("e_gates_dve")
        self.gates_act = core.sem("e_gates_act")
        self.gate_sums = core.sem("e_gate_sums")
        self.spread_set = core.sem("e_spread_set")
        self.spread = core.sem("e_spread")
        self.gc_col = core.sem("e_gc_col")
        self.decay = core.sem("e_decay")
        self.diff = core.sem("e_diff")
        self.k_beta = core.sem("e_k_beta")
        self.kk = core.sem("e_kk")
        self.qk = core.sem("e_qk")
        self.a_set = core.sem("e_a_set")
        self.attn_set = core.sem("e_attn_set")
        self.q_decayed = core.sem("e_q_decayed")
        self.level_mask = core.sem("e_level_mask")
        self.x_flip = core.sem("e_x_flip")
        self.x_start = core.sem("e_x_start")
        self.x_mid = core.sem("e_x_mid")
        self.x_mid_set = core.sem("e_x_mid_set")
        self.x_step = core.sem("e_x_step")
        self.x_set = core.sem("e_x_set")
        self.tok_flip2 = core.sem("e_tok_flip2")
        self.tok_scaled = core.sem("e_tok_scaled")
        self.w_made = core.sem("e_w_made")
        self.w_set = core.sem("e_w_set")
        self.read_made = core.sem("e_read_made")
        self.v_new = core.sem("e_v_new")
        self.o_dn_made = core.sem("e_o_dn_made")
        self.state = core.sem("e_state")
        self.state_read = core.sem("e_state_read")
        self.o_dn_set = core.sem("e_o_dn_set")
        self.o_sq = core.sem("e_o_sq")
        self.o_sums = core.sem("e_o_sums")
        self.o_gates = core.sem("e_o_gates")
        self.z_silu = core.sem("e_z_silu")
        self.o_normed = core.sem("e_o_normed")
        self.o_full = core.sem("e_o_full")
        self.gates_raw = core.sem("e_gates_raw")
        self.gates_set = core.sem("e_gates_set")
        self.x_first = core.sem("e_x_first")
        self.o_spread = core.sem("e_o_spread")
        self.o_spread_set = core.sem("e_o_spread_set")
        self.dl_set = core.sem("e_dl_set")
        self.cols_decay = core.sem("e_cols_decay")
        self.state_made = core.sem("e_state_made")
        self.o_roots = core.sem("e_o_roots")
        self.swa_max = core.sem("e_swa_max")
        self.swa_den = core.sem("e_swa_den")
        self.gates_clear = core.sem("e_gates_clear")

    def conv(self, t):
        return (self.conv_q, self.conv_k, self.conv_v)[t // DH][:, t % DH, :]


def units_before(table, s):
    return sum(len(units) for at, units in table.items() if at < s)


def keys(b):
    if b == 0:
        return 0, 0
    if b == 1:
        return META, P
    return META + (b - 2) * P, 2 * P


def meta_scores(core, rows):
    return core.psum[0:rows, 7, 2 * P:2 * P + GRP * META].rearrange("p (h m) -> p h m", m=META)


def even_gpsimd(core, pool, mix, a):
    k, e = core, core.even
    pool.wait_ge(k.slot_used, mix.slots - EVEN_TILES - 1)
    pool.wait_ge(k.bias_stored, 16)
    scratch = a["bias_scratch"]
    tensor = scratch.tensor

    def skewed(first, rows, n):
        return bass.AP(tensor, first, [[1, rows], [V_ALL, QH], [1, n]])

    pool.dma_start(e.bias_rows[:, :, META:BANDS], skewed(V_BAND, P, 2 * P)).then_inc(e.rows_in, 16)
    pool.dma_start(e.bias_rows[:, :, 0:META], skewed(V_FAR, P, META)).then_inc(e.rows_in, 16)
    pool.dma_start(e.near_rows[:, :, :], skewed(V_NEAR, P, META)).then_inc(e.rows_in, 16)
    pool.dma_start(e.self_rows[:, :, :], skewed(V_SELF, META, META)).then_inc(e.rows_in, 16)
    pool.dma_start(e.flip[:, :], a["masks"][:, C_FLIP:C_FLIP + P]).then_inc(e.rows_in, 16)
    pool.dma_start(e.masks[:, 0:2, :], a["masks"][:, C_UP:C_UP + 2 * P].rearrange("p (n q) -> p n q", q=P))\
        .then_inc(e.masks_in, 16)
    pool.dma_start(e.masks[:, 2:9, :], a["masks"][:, C_LVL:C_LVL + LEVELS * P].rearrange("p (n q) -> p n q", q=P))\
        .then_inc(e.masks_in, 16)
    even_gpsimd_delta(k, e, pool)


def even_tensor_between(core, pe, mix, s):
    k, e = core, core.even
    ps, proj = k.psum, e.proj
    if s == FLIPS_AT:
        pe.wait_ge(k.scaled, mix.evac0 - EVEN_TILES - 1 + FLIPS_AT + 1)
        for c, (t0, n) in enumerate(BLOCKS):
            op = pe.transpose(ps[0:n, 4 + c // 4, (c % 4) * P:(c % 4 + 1) * P], proj[:, V_TILE, t0:t0 + n], k.ident[:])
        op.then_inc(e.v_flip, 1)
        pe.wait_ge(e.rows_in, 80)
        for j in range(BIAS_FLIPS):
            if j >= len(FLIP_BANKS):
                pe.wait_ge(e.bias_set, j - len(FLIP_BANKS) + 1)
            bank = FLIP_BANKS[j % len(FLIP_BANKS)]
            if j < QH:
                op = pe.matmul(ps[:, bank, 0:BANDS], e.flip[:], e.bias_rows[:, j, :], start=True, stop=True)
            elif j == QH:
                op = pe.matmul(ps[:, bank, 0:P], e.flip[:], e.near_rows[:].rearrange("p h m -> p (h m)"), start=True,
                               stop=True)
            else:
                op = pe.matmul(ps[0:META, bank, 0:P], e.flip[0:META, P - META:P],
                               e.self_rows[:].rearrange("p h m -> p (h m)"), start=True, stop=True)
            op.then_inc(e.bias_flip, 1)
        pe.wait_ge(e.bias_set, BIAS_FLIPS)
        pe.wait_ge(e.v_rows_set, 3)
    if s in SUMS_AT:
        first = SUMS_AT[s]
        pe.wait_ge(e.conv_sq, first + DH)
        pe.wait_ge(e.o_copied, OUTPUT_AT[s][0])
        pe.wait_ge(e.scored, units_before(SCORED_AT, s))
        for t in range(DH):
            for c, (t0, n) in enumerate(BLOCKS):
                at = SUMS_COL + c * 2 * DH + first + t
                op = pe.matmul(ps[0:n, 7, at:at + 1], e.squares[:, t, t0:t0 + n], k.ones[:, 0:1], start=True, stop=True)
        op.then_inc(e.gate_sums, 1)
    for i in OUTPUT_AT.get(s, []):
        b, kv = UNITS[i]
        n = BLOCKS[b][1]
        pe.wait_ge(e.p_copied, i + 1)
        pe.wait_ge(e.scored, units_before(SCORED_AT, s))
        if i:
            pe.wait_ge(e.o_copied, i)
        pieces = [META] + [P] * (keys(b)[1] // P)
        for odd in range(2):
            out = ps[HD * odd:HD * (odd + 1), 7, :].rearrange("p (g q) -> p g q", q=P)[:, 0:2, 0:n]
            for j, w in enumerate(pieces):
                block = 0 if j == 0 else (1 if b == 1 else b - 2 + j)
                moving = e.probs_t[0:w, j, :].rearrange("p (g o q) -> p g o q", o=2, q=P)[:, :, odd, 0:n]
                op = pe.matmul(out, e.v_rows[0:w, block, HD * kv:HD * (kv + 1)], moving, start=j == 0,
                               stop=j == len(pieces) - 1)
        op.then_inc(e.o_made, 1)
    for i in SCORED_AT.get(s, []):
        b, kv = UNITS[i]
        t0, n = BLOCKS[b]
        rows = slice(HD * kv, HD * (kv + 1))
        first, count = keys(b)
        if i:
            pe.wait_ge(e.scored, i)
        if i >= 2:
            outputs = units_before(OUTPUT_AT, s + 1)
            if outputs:
                pe.wait_ge(e.o_copied, outputs)
        if s > SUMS_READ_AT:
            pe.wait_ge(e.gates_raw, 1)
        for h in range(GRP):
            if count:
                at = (h % 2) * 2 * P
                pe.matmul(ps[0:n, 2 + h // 2, at:at + count], proj[rows, Q_TILE + h, t0:t0 + n],
                          proj[rows, K_TILE, first:first + count], start=True, stop=True)
            op = pe.matmul(meta_scores(k, n)[:, h, :], proj[rows, Q_TILE + h, t0:t0 + n], proj[rows, K_TILE, 0:META],
                           start=True, stop=True)
        op.then_inc(e.s_made, 1)
    for i in FLIPPED_AT.get(s, []):
        b, kv = UNITS[i]
        n = BLOCKS[b][1]
        pe.wait_ge(e.probs, i + 1)
        if i:
            pe.wait_ge(e.p_copied, i)
        for h in range(GRP):
            at = 0
            for j, w in enumerate([META] + [P] * (keys(b)[1] // P)):
                op = pe.transpose(ps[0:w, 4 + j, h * P:h * P + n], e.scores[0:n, i % 2, h, at:at + w],
                                  k.ident[0:n, 0:n])
                at += w
        op.then_inc(e.p_flip, 1)


def even_scalar_between(core, act, mix, s):
    k, e = core, core.even
    ps = k.psum
    if s == FLIPS_AT:
        act.wait_ge(e.v_flip, 1)
        act.activation(e.v_rows[0:META, 0, :], ps[0:META, 4, 0:P], ACT.Copy).then_inc(e.v_rows_set, 1)
        act.activation(e.v_rows[:, 1:4, :], ps[:, 4, P:4 * P].rearrange("p (c d) -> p c d", d=P), ACT.Copy)\
            .then_inc(e.v_rows_set, 1)
        act.activation(e.v_rows[:, 4, :], ps[:, 5, 0:P], ACT.Copy).then_inc(e.v_rows_set, 1)
    for i in OUTPUT_AT.get(s, []):
        b, kv = UNITS[i]
        t0, n = BLOCKS[b]
        act.wait_ge(e.o_made, i + 1)
        act.activation(e.o_swa[:, 2 * kv:2 * kv + 2, t0:t0 + n],
                       ps[:, 7, :].rearrange("p (g q) -> p g q", q=P)[:, 0:2, 0:n], ACT.Copy).then_inc(e.o_copied, 1)
    for i in FLIPPED_AT.get(s, []):
        b, kv = UNITS[i]
        n = BLOCKS[b][1]
        pieces = 1 + keys(b)[1] // P
        act.wait_ge(e.p_flip, i + 1)
        if i:
            act.wait_ge(e.o_made, i)
        op = act.activation(spread_cols(e.probs_t[0:META, 0, :], n), spread_cols(ps[0:META, 4, :], n), ACT.Copy)
        if pieces > 1:
            op = act.activation(e.probs_t[:, 1:pieces, :], ps[:, 5:4 + pieces, :], ACT.Copy)
        op.then_inc(e.p_copied, 1)
    t = s - DN_TILE
    if 0 <= t < 3 * DH:
        act.wait_ge(k.scaled, mix.evac0 - EVEN_TILES - 1 + s + 1)
        if t >= DH:
            act.wait_ge(e.conv_tap, (CONV - 1) * (t - DH + 1))
        col = (CONV - 1) * 3 * DH + t
        act.activation(e.conv(t), e.proj[:, DN_TILE + t, :], ACT.Copy, scale=k.vec_cols[:, col:col + 1])\
            .then_inc(e.conv_first, 1)
    for i in SCORED_AT.get(s, []):
        b, kv = UNITS[i]
        n = BLOCKS[b][1]
        st = e.stats[0:n, i % 2]
        act.wait_ge(e.swa_max, 3 * i + 3)
        for h in range(GRP):
            tile = e.scores[0:n, i % 2, h, 0:META + keys(b)[1]]
            act.activation(tile, tile, ACT.Exp, bias=st[:, 1, h:h + 1], accum_out=st[:, 2, h:h + 1])
        act.activation(st[:, 3, :], st[:, 3, :], ACT.Exp).then_inc(e.exped, 1)
    if s in SILU_AT:
        first = SILU_AT[s]
        act.wait_ge(e.conv_tap, (CONV - 1) * (first + DH))
        for t in range(first, first + DH):
            act.activation(e.conv(t), e.conv(t), ACT.Silu).then_inc(e.conv_done, 1)
        if first < 2 * DH:
            act.wait_ge(e.conv_done, first + DH)
            if first:
                act.wait_ge(e.gate_sums, 1)
            else:
                act.wait_ge(e.bias_set, BIAS_FLIPS)
            for t in range(DH):
                act.activation(e.squares[:, t, :], e.conv(first + t), ACT.Square).then_inc(e.conv_sq, 1)


def spread_cols(row, n):
    return row.rearrange("p (h q) -> p h q", q=P)[:, :, 0:n]


def even_vector_between(core, dve, mix, s):
    k, e = core, core.even
    ps = k.psum
    if s == FLIPS_AT:
        for j in range(BIAS_FLIPS):
            bank = FLIP_BANKS[j % len(FLIP_BANKS)]
            dve.wait_ge(e.bias_flip, j + 1)
            if j < QH:
                op = dve.tensor_copy(e.bias[:, j, :], ps[:, bank, 0:BANDS])
            elif j == QH:
                op = dve.tensor_copy(e.bias_near[:].rearrange("p h m -> p (h m)"), ps[:, bank, 0:P])
            else:
                op = dve.tensor_copy(e.bias_self[:].rearrange("p h m -> p (h m)"), ps[0:META, bank, 0:P])
            op.then_inc(e.bias_set, 1)
        dve.wait_ge(e.bias_set, BIAS_FLIPS)
        dve.memset(e.gates[:], 1.0).then_inc(e.gates_clear, 1)
    scale = HD ** -0.5
    for i in SCORED_AT.get(s, []):
        b, kv = UNITS[i]
        n = BLOCKS[b][1]
        heads = slice(GRP * kv, GRP * (kv + 1))
        count = keys(b)[1]
        width = META + count
        sc = e.scores[0:n, i % 2]
        st = e.stats[0:n, i % 2]
        dve.wait_ge(e.s_made, i + 1)
        if i >= 2:
            dve.wait_ge(e.p_flip, i - 1)
        meta_bias = (e.bias_self, e.bias_near, e.bias)[min(b, 2)][0:n, heads, 0:META]
        op = dve.scalar_tensor_tensor(sc[:, :, 0:META], meta_scores(k, n), scale, meta_bias, ALU.mult, ALU.add)
        if count:
            made = ps[0:n, 2:4, :].rearrange("p a (b c) -> p (a b) c", b=2)[:, :, 0:count]
            op = dve.scalar_tensor_tensor(sc[:, :, META:width], made, scale, e.bias[:, heads, BANDS - count:BANDS],
                                          ALU.mult, ALU.add)
        op.then_inc(e.scored, 1)
        dve.wait_ge(e.scored, i + 1)
        dve.tensor_reduce(st[:, 0, :], sc[:, :, 0:width], AX.X, ALU.max).then_inc(e.swa_max, 1)
        dve.wait_ge(e.swa_max, 3 * i + 1)
        dve.tensor_tensor(st[:, 0, :], st[:, 0, :], k.heads[0:n, heads], ALU.max).then_inc(e.swa_max, 1)
        dve.wait_ge(e.swa_max, 3 * i + 2)
        dve.tensor_scalar(st[:, 1, :], st[:, 0, :], -1.0, None, ALU.mult)
        dve.tensor_tensor(st[:, 3, :], k.heads[0:n, heads], st[:, 0, :], ALU.subtract).then_inc(e.swa_max, 1)
    t = s - DN_TILE - 1
    taps = [] if t < 0 or t >= 3 * DH else list(range(1, CONV))
    units = PROBS_AT.get(s, [])
    for i in units:
        b, kv = UNITS[i]
        n = BLOCKS[b][1]
        width = META + keys(b)[1]
        sc = e.scores[0:n, i % 2]
        st = e.stats[0:n, i % 2]
        dve.wait_ge(e.exped, i + 1)
        dve.tensor_tensor(st[:, 4, :], st[:, 2, :], st[:, 3, :], ALU.add).then_inc(e.swa_den, 1)
        dve.wait_ge(e.swa_den, 2 * i + 1)
        dve.reciprocal(st[:, 5, :], st[:, 4, :]).then_inc(e.swa_den, 1)
        dve.wait_ge(e.swa_den, 2 * i + 2)
        dve.tensor_tensor(sc[:, :, 0:width], sc[:, :, 0:width], st[:, 5, :].unsqueeze(2).broadcast_to([n, GRP, width]),
                          ALU.mult).then_inc(e.probs, 1)
    for back in taps:
        if back == 1:
            dve.wait_ge(e.conv_first, t + 1)
        else:
            dve.wait_ge(e.conv_tap, (CONV - 1) * t + back - 1)
        col = (CONV - 1 - back) * 3 * DH + t
        out = e.conv(t)[:, back:TOK]
        dve.scalar_tensor_tensor(out, e.proj[:, DN_TILE + t, 0:TOK - back], k.vec_cols[:, col:col + 1], out,
                                 ALU.mult, ALU.add).then_inc(e.conv_tap, 1)
    if s == SUMS_READ_AT:
        dve.wait_ge(e.gate_sums, 2)
        dve.wait_ge(e.gates_clear, 1)
        dve.wait_ge(e.o_copied, OUTPUT_AT[s][0] + 1)
        sums = ps[:, 7, SUMS_COL:SUMS_COL + 8 * (NBLK + 1)].rearrange("p (c q h) -> p q c h", q=2, h=DH)
        dve.tensor_copy(e.gates[0:META, G_SQ:G_SQ + 2, 0], sums[0:META, :, 0])
        dve.tensor_copy(e.gates[:, G_SQ:G_SQ + 2, 1:], sums[:, :, 1:]).then_inc(e.gates_raw, 1)


def even_rest(core, engine, mix, between):
    for s in range(LAST_SLOT + 1, max(OUTPUT_AT) + 1):
        between(core, engine, mix, s)


def even_tensor(core, pe, mix):
    even_rest(core, pe, mix, even_tensor_between)
    even_tensor_delta(core, core.even, pe, mix)


def even_scalar(core, act, mix):
    even_rest(core, act, mix, even_scalar_between)
    even_scalar_delta(core, core.even, act, mix)


def even_vector(core, dve, mix):
    even_rest(core, dve, mix, even_vector_between)
    even_vector_delta(core, core.even, dve, mix)


G_B, G_A, G_SQ, G_SK, G_BETA, G_LOG, G_RQ, G_RK, G_CUM, G_BEG, G_KD, G_DL = range(12)
M_UP, M_ADD, M_LVL = 0, 1, 2
SPREADS = ((M_UP, G_LOG), (None, G_RK), (None, G_RQ), (None, G_BETA))
LEVEL_ITEMS = [(lv, c) for lv in range(1, LEVELS) for c in range(NBLK + 1) if (1 << lv) < BLOCKS[c][1]]


def last_level(lv, c):
    return (2 << lv) >= BLOCKS[c][1]


def item_before(j):
    before = [i for i, (_, c) in enumerate(LEVEL_ITEMS[:j]) if c == LEVEL_ITEMS[j][1]]
    return before[-1] if before else None


def level_buffer(k, e, n):
    return (k.t_gate[:, 0:DH * P], k.t_up[:, 0:DH * P], e.wide[:, 0, :], e.wide[:, 1, :])[n % 4]


class Chain:

    def __init__(self, engine, sem):
        self.engine, self.sem, self.n = engine, sem, 0

    def then(self, op):
        op.then_inc(self.sem, 1)
        self.n += 1
        self.engine.wait_ge(self.sem, self.n)


def heads_view(buf, rows, n):
    flat = buf[0:rows]
    if len(flat.shape) == 2:
        flat = flat.rearrange("p (h q) -> p h q", q=P)
    return flat[:, :, 0:n]


def along(col, rows, n):
    return col.unsqueeze(2).broadcast_to([rows, DH, n])


def over_heads(mask, rows, n):
    return mask.unsqueeze(1).broadcast_to([rows, DH, n])


def even_gpsimd_delta(k, e, pool):
    pool.wait_ge(e.masks_in, 32)
    pool.wait_ge(e.gates_set, 1)
    for c, (t0, n) in enumerate(BLOCKS):
        for q, (mask, gate) in enumerate(SPREADS):
            j = 4 * c + q
            if j >= 2:
                pool.wait_ge(e.spread, j - 1)
            m = k.ident[0:n, 0:n] if mask is None else e.masks[0:n, mask, 0:n]
            pool.tensor_tensor(heads_view(e.wide[:, j % 2, :], n, n), over_heads(m, n, n),
                               along(e.gates[0:n, gate, c, :], n, n), ALU.mult).then_inc(e.spread_set, 1)
    for c, (t0, n) in enumerate(BLOCKS):
        pool.wait_ge(e.a_set, c + 1)
        if c >= 4:
            pool.wait_ge(e.x_first, c - 3)
        elif c >= 2:
            pool.wait_ge(e.spread, 4 * (NBLK + 1))
        pool.tensor_tensor(heads_view(level_buffer(k, e, c), n, n), heads_view(e.a_t[:, c], n, n),
                           over_heads(e.masks[0:n, M_LVL, 0:n], n, n), ALU.mult).then_inc(e.level_mask, 1)
    for j, (lv, c) in enumerate(LEVEL_ITEMS):
        n = BLOCKS[c][1]
        at = j + NBLK + 1
        if at < NBLK + 5:
            pool.wait_ge(e.x_first, at - 3)
        else:
            pool.wait_ge(e.x_mid, j - 3)
        pool.tensor_tensor(heads_view(level_buffer(k, e, at), n, n), heads_view(e.a_t[:, c], n, n),
                           over_heads(e.masks[0:n, M_LVL + lv, 0:n], n, n), ALU.mult).then_inc(e.level_mask, 1)
    for c, (t0, n) in enumerate(BLOCKS):
        pool.wait_ge(e.o_gates, c + 1)
        if c >= 2:
            pool.wait_ge(e.o_spread, c - 1)
        buf = (k.t_up if c % 2 else k.t_gate)[:, 0:DH * P]
        pool.tensor_tensor(heads_view(buf, n, n), over_heads(k.ident[0:n, 0:n], n, n),
                           along(e.gates[0:n, G_SK, c, :], n, n), ALU.mult).then_inc(e.o_spread_set, 1)


def even_tensor_delta(k, e, pe, mix):
    ps = k.psum
    pe.wait_ge(k.scaled, mix.evac0)
    pe.wait_ge(e.p_copied, len(UNITS))
    for c, (t0, n) in enumerate(BLOCKS):
        op = pe.transpose(ps[0:n, 4, c * 8:(c + 1) * 8], e.proj[0:2 * DH, GATE_TILE, t0:t0 + n],
                          k.ident[0:2 * DH, 0:2 * DH])
    op.then_inc(e.gate_flip, 1)
    pe.wait_ge(e.o_copied, len(UNITS))
    for c, (t0, n) in enumerate(BLOCKS):
        for q in range(4):
            pe.wait_ge(e.spread_set, 4 * c + q + 1)
            if q == 0 and c:
                pe.wait_ge(e.decay, 2 * c)
                pe.wait_ge(e.k_beta, c)
            pe.matmul(heads_view(ps[:, q, :], P, n), k.ones[0:n, :], heads_view(e.wide[:, (4 * c + q) % 2, :], n, n),
                      start=True, stop=True).then_inc(e.spread, 1)
            if q == 0:
                pe.matmul(ps[0:n, 6, 0:DH], e.masks[0:n, M_UP, 0:n], e.gates[0:n, G_LOG, c, :], start=True,
                          stop=True).then_inc(e.gc_col, 1)
        if c:
            pe.wait_ge(e.attn_set, c)
        pe.wait_ge(e.k_beta, c + 1)
        for h in range(DH):
            op = pe.matmul(ps[0:n, 4, h * P:h * P + n], e.conv_k[:, h, t0:t0 + n], e.wide3[:, h * P:h * P + n],
                           start=True, stop=True)
        op.then_inc(e.kk, 1)
        for h in range(DH):
            op = pe.matmul(ps[0:n, 5, h * P:h * P + n], e.conv_k[:, h, t0:t0 + n], e.conv_q[:, h, t0:t0 + n],
                           start=True, stop=True)
        op.then_inc(e.qk, 1)
    pe.wait_ge(e.attn_set, NBLK + 1)
    for c, (t0, n) in enumerate(BLOCKS):
        pe.wait_ge(e.x_first, c + 1)
        if c >= 2:
            pe.wait_ge(e.x_start, c - 1)
        for h in range(DH):
            op = pe.transpose(ps[0:n, c % 2, h * P:h * P + n], e.inv_t[0:n, c, h, 0:n], k.ident[0:n, 0:n])
        op.then_inc(e.x_flip, 1)
    pe.wait_ge(e.x_start, NBLK + 1)

    def middle(j):
        lv, c = LEVEL_ITEMS[j]
        n = BLOCKS[c][1]
        pe.wait_ge(e.level_mask, NBLK + 1 + j + 1)
        before = item_before(j)
        if before is not None:
            pe.wait_ge(e.x_set, before + 1)
        if j >= 2:
            pe.wait_ge(e.x_mid_set, j - 1)
        buf = level_buffer(k, e, NBLK + 1 + j)
        for h in range(DH):
            op = pe.matmul(ps[0:n, j % 2, h * P:h * P + n], buf[0:n, h * P:h * P + n], e.inv[0:n, c, h, 0:n],
                           start=True, stop=True)
        op.then_inc(e.x_mid, 1)

    middle(0)
    for j, (lv, c) in enumerate(LEVEL_ITEMS):
        n = BLOCKS[c][1]
        if j + 1 < len(LEVEL_ITEMS):
            middle(j + 1)
        pe.wait_ge(e.x_mid_set, j + 1)
        if j >= 2:
            pe.wait_ge(e.x_set, j - 1)
        for h in range(DH):
            if not last_level(lv, c):
                pe.matmul(ps[0:n, 2 + j % 2, h * P:h * P + n], e.inv_t[0:n, c, h, 0:n], e.half_x[0:n, c, h, 0:n],
                          start=True, stop=True)
            op = pe.matmul(ps[0:n, 4 + j % 2, h * P:h * P + n], e.half_x[0:n, c, h, 0:n], e.inv_t[0:n, c, h, 0:n],
                           start=True, stop=True)
        op.then_inc(e.x_step, 1)
    pe.wait_ge(e.x_set, len(LEVEL_ITEMS))
    def by_token(c):
        t0, n = BLOCKS[c]
        if c >= 2:
            pe.wait_ge(e.tok_scaled, 3 * (c - 1))
        for h in range(DH):
            op = pe.transpose(ps[0:n, c % 2, h * P:(h + 1) * P], e.conv_k[:, h, t0:t0 + n], k.ident[:])
        op.then_inc(e.tok_flip2, 1)
        for h in range(DH):
            op = pe.transpose(ps[0:n, 2 + c % 2, h * P:(h + 1) * P], e.conv_v[:, h, t0:t0 + n], k.ident[:])
        op.then_inc(e.tok_flip2, 1)

    by_token(0)
    for c, (t0, n) in enumerate(BLOCKS):
        if c < NBLK:
            by_token(c + 1)
        pe.wait_ge(e.tok_scaled, 3 * c + 3)
        if c >= 2:
            pe.wait_ge(e.w_set, 2 * (c - 1))
        for h in range(DH):
            op = pe.matmul(ps[:, 4 + c % 2, h * P:h * P + n], e.wide[0:n, c % 2, h * P:(h + 1) * P],
                           e.inv_t[0:n, c, h, 0:n], start=True, stop=True)
        op.then_inc(e.w_made, 1)
        for h in range(DH):
            op = pe.matmul(ps[0:n, 6 + c % 2, h * P:(h + 1) * P], e.inv_t[0:n, c, h, 0:n],
                           e.wide2[0:n, c % 2, h * P:(h + 1) * P], start=True, stop=True)
        op.then_inc(e.w_made, 1)
    pe.wait_ge(e.w_set, 2 * (NBLK + 1))

    def out_sums(c):
        n = BLOCKS[c][1]
        if c >= 2:
            pe.wait_ge(e.o_roots, c - 1)
        pe.wait_ge(e.o_sq, c + 1)
        for h in range(DH):
            op = pe.matmul(ps[0:n, 6 + c % 2, h:h + 1], e.wide[:, c % 2, h * P:h * P + n], k.ones[:, 0:1],
                           start=True, stop=True)
        op.then_inc(e.o_sums, 1)

    def out_factors(c):
        n = BLOCKS[c][1]
        pe.wait_ge(e.o_spread_set, c + 1)
        if c >= 2:
            pe.wait_ge(e.o_normed, c - 1)
        buf = (k.t_up if c % 2 else k.t_gate)[:, 0:DH * P]
        pe.matmul(heads_view(ps[:, 5 - 4 * (c % 2), :], P, n), k.ones[0:n, :], heads_view(buf, n, n), start=True,
                  stop=True).then_inc(e.o_spread, 1)

    for c, (t0, n) in enumerate(BLOCKS):
        if c:
            pe.wait_ge(e.state, c)
            for h in range(DH):
                op = pe.matmul(ps[0:n, 0, h * P:(h + 1) * P], e.w_t[:, c, h, 0:n], e.wide3[:, h * P:(h + 1) * P],
                               start=True, stop=True)
            op.then_inc(e.read_made, 1)
            if c >= 2:
                pe.wait_ge(e.o_dn_set, c - 1)
            for h in range(DH):
                op = pe.matmul(ps[:, 2 + c % 2, h * P:h * P + n], e.wide3[:, h * P:(h + 1) * P],
                               e.conv_q[:, h, t0:t0 + n], start=h == 0, stop=False)
            op.then_inc(e.state_read, 1)
            pe.wait_ge(e.v_new, c)
        if c < NBLK:
            for h in range(DH):
                op = pe.matmul(ps[:, 4, h * P:(h + 1) * P], e.k_dec[0:n, c, h, :], e.u[0:n, c, h, :], start=True,
                               stop=True)
            op.then_inc(e.state_made, 1)
        for h in range(DH):
            op = pe.matmul(ps[:, 2 + c % 2, h * P:h * P + n], e.u[0:n, c, h, :], e.attn[0:n, c, h, 0:n],
                           start=c == 0 and h == 0, stop=h == DH - 1)
        op.then_inc(e.o_dn_made, 1)
        if c:
            out_sums(c - 1)
        if c >= 2:
            out_factors(c - 2)
    out_sums(NBLK)
    out_factors(NBLK - 1)
    out_factors(NBLK)


def even_banks_read(k, pe):
    e = k.even
    pe.wait_ge(e.o_roots, NBLK + 1)
    pe.wait_ge(e.o_dn_set, NBLK + 1)
    pe.wait_ge(e.o_normed, NBLK)


def even_scalar_delta(k, e, act, mix):
    ps = k.psum
    g = e.gates
    act.wait_ge(e.gates_raw, 4)
    act.activation(g[:, G_B], g[:, G_B], ACT.Exp, scale=-1.0).then_inc(e.gates_act, 1)
    act.activation(g[:, G_A], g[:, G_A], ACT.Exp).then_inc(e.gates_act, 1)
    act.activation(k.heads[:, QH:QH + DH], k.heads[:, QH:QH + DH], ACT.Exp).then_inc(e.gates_act, 1)
    act.wait_ge(e.gates_act, 3)
    act.activation(g[:, G_A], g[:, G_A], ACT.Ln, bias=k.ones[:, 0:1]).then_inc(e.gates_act, 1)
    act.activation(g[:, G_RQ], g[:, G_SQ], ACT.Sqrt, bias=k.eps[:, 2:3], scale=float(DN_DIM)).then_inc(e.gates_act, 1)
    act.activation(g[:, G_RK], g[:, G_SK], ACT.Sqrt, bias=k.eps[:, 0:1]).then_inc(e.gates_act, 1)
    for c, (t0, n) in enumerate(BLOCKS):
        act.wait_ge(e.spread, 4 * c + 1)
        if c:
            act.wait_ge(e.q_decayed, c)
            act.wait_ge(e.dl_set, c)
        act.activation(heads_view(e.wide2[:, 0, :], P, n), heads_view(ps[:, 0, :], P, n), ACT.Exp).then_inc(e.decay, 1)
        act.wait_ge(e.diff, 3 * c + 1)
        act.activation(g[0:n, G_BEG, c], g[0:n, G_CUM, c], ACT.Exp)
        act.activation(g[0:n, G_KD, c], g[0:n, G_KD, c], ACT.Exp).then_inc(e.cols_decay, 1)
        act.wait_ge(e.diff, 3 * c + 3)
        gamma = heads_view(e.wide2[:, 1, :], n, n)
        act.activation(gamma, gamma, ACT.Exp).then_inc(e.decay, 1)
    for c, (t0, n) in enumerate(BLOCKS):
        act.wait_ge(e.x_flip, c + 1)
        act.activation(heads_view(e.inv[:, c], n, n), heads_view(ps[:, c % 2, :], n, n), ACT.Copy)\
            .then_inc(e.x_start, 1)
    for j, (lv, c) in enumerate(LEVEL_ITEMS):
        n = BLOCKS[c][1]
        act.wait_ge(e.x_mid, j + 1)
        before = item_before(j)
        if before is not None:
            act.wait_ge(e.x_step, before + 1)
        act.activation(heads_view(e.half_x[:, c], n, n), heads_view(ps[:, j % 2, :], n, n), ACT.Copy)\
            .then_inc(e.x_mid_set, 1)
    act.wait_ge(e.x_set, len(LEVEL_ITEMS))
    for c, (t0, n) in enumerate(BLOCKS):
        act.wait_ge(e.w_made, 2 * c + 1)
        act.activation(heads_view(e.w_t[:, c], P, n), heads_view(ps[:, 4 + c % 2, :], P, n), ACT.Copy)\
            .then_inc(e.w_set, 1)
        act.wait_ge(e.w_made, 2 * c + 2)
        act.activation(heads_view(e.u[:, c], n, P), heads_view(ps[:, 6 + c % 2, :], n, P), ACT.Copy)\
            .then_inc(e.w_set, 1)
    for h in range(DH):
        act.activation(e.proj[:, Z_TILE + h, :], e.proj[:, Z_TILE + h, :], ACT.Silu).then_inc(e.z_silu, 1)
    load_table(k, act, ACT.Sqrt)

    def hi(kt, tile):
        act.activation(k.x_hl[:, 0, kt, :], tile, ACT.Copy).then_inc(k.x_hi, 1)

    def out_root(c):
        n = BLOCKS[c][1]
        act.wait_ge(e.o_sums, c + 1)
        act.activation(g[0:n, G_SQ, c], ps[0:n, 6 + c % 2, 0:DH], ACT.Sqrt, bias=k.eps[0:n, 0:1],
                       scale=1.0 / DN_DIM).then_inc(e.o_roots, 1)

    for c, (t0, n) in enumerate(BLOCKS):
        if c == NBLK:
            act.wait_ge(e.state_made, NBLK)
            for kt in range(DT // 2):
                hi(kt, e.o_swa[:, kt, :])
        act.wait_ge(e.o_dn_made, c + 1)
        if c >= 2:
            act.wait_ge(e.o_sums, c - 1)
        src = heads_view(ps[:, 2 + c % 2, :], P, n)
        act.activation(heads_view(e.wide[:, c % 2, :], P, n), src, ACT.Square).then_inc(e.o_sq, 1)
        act.activation(e.o_dn[:, :, t0:t0 + n], src, ACT.Copy).then_inc(e.o_dn_set, 1)
        if c:
            out_root(c - 1)
    out_root(NBLK)
    for h in range(DH):
        act.wait_ge(e.o_full, h + 1)
        hi(DT // 2 + h, e.o_dn[:, h, :])


def even_vector_delta(k, e, dve, mix):
    ps, g = k.psum, e.gates
    chain = Chain(dve, e.gates_dve)
    dve.wait_ge(e.gate_flip, 1)
    raw = ps[:, 4, 0:8 * (NBLK + 1)].rearrange("p (c q h) -> p q c h", q=2, h=DH)
    dve.tensor_copy(g[0:META, 0:2, 0], raw[0:META, :, 0])
    chain.then(dve.tensor_copy(g[:, 0:2, 1:], raw[:, :, 1:]))
    dt = k.heads[:, QH + DH:QH + 2 * DH].unsqueeze(1).broadcast_to([P, NBLK + 1, DH])
    a_log = k.heads[:, QH:QH + DH].unsqueeze(1).broadcast_to([P, NBLK + 1, DH])
    x, neg = g[:, G_LOG], g[:, G_BEG]
    chain.then(dve.tensor_tensor(x, g[:, G_A], dt, ALU.add))
    dve.sem_inc(e.gates_raw, 2)
    chain.then(dve.tensor_scalar(neg, x, -1.0, None, ALU.mult))
    dve.tensor_tensor(g[:, G_A], x, neg, ALU.min).then_inc(e.gates_raw, 1)
    dve.wait_ge(e.gates_act, 1)
    chain.then(dve.tensor_scalar(g[:, G_BETA], g[:, G_B], 1.0, None, ALU.add))
    chain.then(dve.reciprocal(g[:, G_BETA], g[:, G_BETA]))
    dve.wait_ge(e.gates_act, 4)
    chain.then(dve.scalar_tensor_tensor(x, x, 0.0, g[:, G_A], ALU.max, ALU.add))
    chain.then(dve.scalar_tensor_tensor(x, x, -1.0, a_log, ALU.mult, ALU.mult))
    dve.wait_ge(e.gates_act, 6)
    dve.reciprocal(g[:, G_RQ:G_RQ + 2], g[:, G_RQ:G_RQ + 2]).then_inc(e.gates_set, 1)
    dve.wait_ge(e.masks_in, 32)
    for c, (t0, n) in enumerate(BLOCKS):
        diff = heads_view(e.wide2[:, 1, :], n, n)
        cum = heads_view(ps[:, 0, :], n, n)
        toks = slice(t0, t0 + n)
        dve.wait_ge(e.gc_col, c + 1)
        chain.then(dve.tensor_copy(g[0:n, G_CUM, c], ps[0:n, 6, 0:DH]))
        dve.wait_ge(e.decay, 2 * c + 1)
        dve.tensor_tensor(g[0:n, G_KD, c], cum[:, :, n - 1], g[0:n, G_CUM, c], ALU.subtract).then_inc(e.diff, 1)
        if c:
            dve.wait_ge(e.attn_set, c)
        dve.tensor_tensor(diff, cum, along(g[0:n, G_CUM, c], n, n), ALU.subtract).then_inc(e.diff, 1)
        dve.wait_ge(e.diff, 3 * c + 2)
        dve.scalar_tensor_tensor(diff, diff, 0.0, over_heads(e.masks[0:n, M_ADD, 0:n], n, n), ALU.min, ALU.add)\
            .then_inc(e.diff, 1)
        dve.wait_ge(e.spread, 4 * c + 2)
        keys_t = e.conv_k[:, :, toks]
        chain.then(dve.tensor_tensor(keys_t, keys_t, heads_view(ps[:, 1, :], P, n), ALU.mult))
        dve.wait_ge(e.spread, 4 * c + 3)
        queries_t = e.conv_q[:, :, toks]
        chain.then(dve.tensor_tensor(queries_t, queries_t, heads_view(ps[:, 2, :], P, n), ALU.mult))
        dve.wait_ge(e.spread, 4 * c + 4)
        if c:
            dve.wait_ge(e.kk, c)
        dve.tensor_tensor(heads_view(e.wide3[:, :], P, n), keys_t, heads_view(ps[:, 3, :], P, n), ALU.mult)\
            .then_inc(e.k_beta, 1)
        dve.wait_ge(e.decay, 2 * c + 2)
        dve.tensor_copy(g[:, G_DL, c], heads_view(e.wide2[:, 0, :], P, n)[:, :, n - 1]).then_inc(e.dl_set, 1)
        dve.wait_ge(e.cols_decay, c + 1)
        dve.tensor_tensor(g[0:n, G_BEG, c], g[0:n, G_BEG, c], g[0:n, G_BETA, c], ALU.mult)
        dve.wait_ge(e.kk, c + 1)
        dve.tensor_tensor(heads_view(e.a_t[:, c], n, n), heads_view(ps[:, 4, :], n, n), diff, ALU.mult)\
            .then_inc(e.a_set, 1)
        dve.wait_ge(e.qk, c + 1)
        dve.tensor_tensor(heads_view(e.attn[:, c], n, n), heads_view(ps[:, 5, :], n, n), diff, ALU.mult)\
            .then_inc(e.attn_set, 1)
        dve.tensor_tensor(queries_t, queries_t, heads_view(e.wide2[:, 0, :], P, n), ALU.mult).then_inc(e.q_decayed, 1)
    for c, (t0, n) in enumerate(BLOCKS):
        dve.wait_ge(e.level_mask, c + 1)
        dve.tensor_tensor(heads_view(e.inv_t[:, c], n, n), over_heads(k.ident[0:n, 0:n], n, n),
                          heads_view(level_buffer(k, e, c), n, n), ALU.subtract).then_inc(e.x_first, 1)
    for j, (lv, c) in enumerate(LEVEL_ITEMS):
        n = BLOCKS[c][1]
        dve.wait_ge(e.x_step, j + 1)
        inv, inv_t = heads_view(e.inv[:, c], n, n), heads_view(e.inv_t[:, c], n, n)
        if not last_level(lv, c):
            dve.tensor_tensor(inv, inv, heads_view(ps[:, 2 + j % 2, :], n, n), ALU.subtract)
        dve.tensor_tensor(inv_t, inv_t, heads_view(ps[:, 4 + j % 2, :], n, n), ALU.subtract).then_inc(e.x_set, 1)
    dve.wait_ge(e.level_mask, NBLK + 1 + len(LEVEL_ITEMS))
    for c, (t0, n) in enumerate(BLOCKS):
        dve.wait_ge(e.tok_flip2, 2 * c + 1)
        if c >= 2:
            dve.wait_ge(e.w_made, 2 * (c - 1))
        keys_c, values_c = heads_view(ps[:, c % 2, :], n, P), heads_view(ps[:, 2 + c % 2, :], n, P)
        dve.tensor_tensor(heads_view(e.wide[:, c % 2, :], n, P), keys_c, along(g[0:n, G_BEG, c], n, P), ALU.mult)\
            .then_inc(e.tok_scaled, 1)
        dve.tensor_tensor(heads_view(e.k_dec[:, c], n, P), keys_c, along(g[0:n, G_KD, c], n, P), ALU.mult)\
            .then_inc(e.tok_scaled, 1)
        dve.wait_ge(e.tok_flip2, 2 * c + 2)
        dve.tensor_tensor(heads_view(e.wide2[:, c % 2, :], n, P), values_c, along(g[0:n, G_BETA, c], n, P), ALU.mult)\
            .then_inc(e.tok_scaled, 1)

    def lo(kt, tile):
        dve.wait_ge(k.x_hi, mix.x0 + kt + 1)
        dve.tensor_tensor(k.x_hl[:, 1, kt, :], tile, k.x_hl[:, 0, kt, :].bitcast(F32), ALU.subtract).then_inc(k.x_lo, 1)

    def out_inverse(c):
        n = BLOCKS[c][1]
        dve.wait_ge(e.o_roots, c + 1)
        dve.reciprocal(g[0:n, G_SK, c], g[0:n, G_SQ, c]).then_inc(e.o_gates, 1)

    def out_normed(c):
        t0, n = BLOCKS[c]
        dve.wait_ge(e.o_spread, c + 1)
        dve.wait_ge(e.o_dn_set, c + 1)
        out = e.o_dn[:, :, t0:t0 + n]
        dve.tensor_tensor(out, out, heads_view(ps[:, 5 - 4 * (c % 2), :], P, n), ALU.mult).then_inc(e.o_normed, 1)

    for c, (t0, n) in enumerate(BLOCKS):
        u = heads_view(e.u[:, c], n, P)
        if c:
            dve.wait_ge(e.read_made, c)
            dve.tensor_tensor(u, u, heads_view(ps[:, 0, :], n, P), ALU.subtract).then_inc(e.v_new, 1)
        if c == 0:
            dve.wait_ge(e.state_made, c + 1)
            dve.tensor_copy(e.wide3[:, :], ps[:, 4, :]).then_inc(e.state, 1)
        elif c < NBLK:
            dve.wait_ge(e.state_made, c + 1)
            dve.wait_ge(e.state, c)
            dve.wait_ge(e.state_read, c)
            for h in range(DH):
                s = e.wide3[:, h * P:(h + 1) * P]
                op = dve.scalar_tensor_tensor(s, s, g[:, G_DL, c, h:h + 1], ps[:, 4, h * P:(h + 1) * P], ALU.mult,
                                              ALU.add)
            op.then_inc(e.state, 1)
        if c == NBLK:
            for kt in range(DT // 2):
                lo(kt, e.o_swa[:, kt, :])
        if c:
            out_inverse(c - 1)
        if c >= 2:
            out_normed(c - 2)
    out_inverse(NBLK)
    out_normed(NBLK - 1)
    out_normed(NBLK)
    dve.wait_ge(e.o_normed, NBLK + 1)
    dve.wait_ge(e.z_silu, DH)
    weight = k.vec_cols[:, VEC_ROWS - 1:VEC_ROWS]

    def gated(h):
        dve.scalar_tensor_tensor(e.o_dn[:, h, :], e.o_dn[:, h, :], weight, e.proj[:, Z_TILE + h, :], ALU.mult,
                                 ALU.mult).then_inc(e.o_full, 1)

    gated(0)
    for h in range(DH):
        if h + 1 < DH:
            gated(h + 1)
        lo(DT // 2 + h, e.o_dn[:, h, :])


GQ, GK, GV, GG, GATE_LOW = 0, 4, 8, 16, 24
VD = 2 * P
NORM_GATE = 16.0
CHUNKS = [(0, 0, 0, META)] + [(1 + s // 2, CH * (s % 2), META + s * CH, CH) for s in range(SEQ // CH)]


class Odd:

    def __init__(self, core):
        at, a = core.at, core.arena
        tile = 4 * TOK
        self.proj = at("odd_proj", [P, ODD_TILES + 1, TOK], a)
        free = a + (ODD_TILES + 1) * tile
        self.ex = at("gla_ex", [P, 6, TOK], free)
        self.k_grow = at("gla_k_grow", [P, GH, TOK], free + 6 * tile)
        self.v_rows = at("gla_v_rows", [P, NBLK + 1, GH * VD], free)
        self.diag = at("gla_diag", [P, 2, GH * P], free)
        self.meta_k_rows = at("gla_meta_k_rows", [META, GH, P], a + GATE_LOW * tile)
        self.attn = at("gla_attn", [P, NBLK, GH, P], free + 10 * tile)
        self.gate_up = at("gla_gate_up", [RANK, GH * P], free + 10 * tile)
        self.state = at("gla_state", [P, 2, GH, VD], free + 10 * tile + 8192)
        self.mask = at("gla_mask", [P, P], free + 10 * tile + 8192)
        self.keep = at("gla_keep", [P, TOK], free + 10 * tile + 16384)
        self.cols = at("gla_cols", [P, 2 * NBLK * GH + GH * len(CHUNKS)], free + 11 * tile + 16384)
        self.decay = self.cols[:, 2 * NBLK * GH:].rearrange("p (h s) -> p h s", h=GH)
        self.roots = self.cols[:, 0:NBLK * GH]
        self.inverse = self.cols[:, NBLK * GH:2 * NBLK * GH].rearrange("p (c h) -> p c h", h=GH)
        self.s_in = core.sem("o_in")
        self.s_gate_lin = core.sem("o_gate_lin")
        self.s_gate_x = core.sem("o_gate_x")
        self.s_gate_neg = core.sem("o_gate_neg")
        self.s_gate_exp = core.sem("o_gate_exp")
        self.s_gate_log = core.sem("o_gate_log")
        self.s_gate_min = core.sem("o_gate_min")
        self.s_cum = core.sem("o_cum")
        self.s_kd_arg = core.sem("o_kd_arg")
        self.s_grown = core.sem("o_grown")
        self.s_q_dec = core.sem("o_q_dec")
        self.s_k_grow = core.sem("o_k_grow")
        self.s_k_dec = core.sem("o_k_dec")
        self.s_v_flip = core.sem("o_v_flip")
        self.s_v_set = core.sem("o_v_set")
        self.s_k_flip = core.sem("o_k_flip")
        self.s_k_set = core.sem("o_k_set")
        self.s_attn_made = core.sem("o_attn_made")
        self.s_attn_set = core.sem("o_attn_set")
        self.s_kv_made = core.sem("o_kv_made")
        self.s_state = core.sem("o_state")
        self.s_o_made = core.sem("o_o_made")
        self.s_o_sq = core.sem("o_o_sq")
        self.s_o_set = core.sem("o_o_set")
        self.s_o_sums = core.sem("o_o_sums")
        self.s_o_roots = core.sem("o_o_roots")
        self.s_o_inverse = core.sem("o_o_inverse")
        self.s_diag_set = core.sem("o_diag_set")
        self.s_diag_used = core.sem("o_diag_used")
        self.s_o_normed = core.sem("o_o_normed")
        self.s_g_silu = core.sem("o_g_silu")
        self.s_o_full = core.sem("o_o_full")

    def k_rows(self, c):
        if c == 0:
            return self.meta_k_rows[:, :, :]
        t0, n = BLOCKS[c]
        return self.proj[:, GK:GK + GH, t0:t0 + n]


GATE_AT = {GATES_OUT - 1: [0, 1, 2], GATES_OUT: [3]}
NEG_AT = {5: [0, 1], 9: [2, 3]}
LOG_AT = {6: [0, 1], 10: [2, 3]}
MIN_AT = {6: [0, 1], 10: [2, 3]}
CUM_AT = {6: [0], 7: [1], 10: [2], 11: [3]}
GROW_AT = {7: [0], 8: [1], 11: [2], 12: [3]}
DECAY_AT = {8: [0], 9: [1], 12: [2], 13: [3]}
KEYS_AT = {KEYS_FROM: [0, 1], KEYS_FROM + 1: [2, 3], KEYS_FROM + 2: [4]}
VALUES_AT = {17: [0, 1], 18: [2], 19: [3], 20: [4]}
ODD_LAST = ODD_TILES
KV_AT = {18: [0], 19: [1], 20: [2], 21: [3], 22: [4], 23: [5], 24: [6, 7]}
OUT_AT = {19: [1], 20: [2], 21: [3], 22: [4], 23: [5], 24: [6], 25: [7, 8]}
SILU_G_AT = {18 + j: [j] for j in range(2 * GH - 1)}
SILU_G_AT[ODD_LAST] = [2 * GH - 2, 2 * GH - 1]
EARLY_SUMS = len(CHUNKS) - 3


def odd_gpsimd(core, pool, mix, a):
    k, o = core, core.odd
    pool.wait_ge(k.slot_used, mix.slots - ODD_TILES - 1)
    pool.dma_start(o.gate_up[:, :], a["gla_w_gate_up"][0]).then_inc(o.s_in, 16)
    pool.dma_start(o.keep[:, :], a["scan_keep"]).then_inc(o.s_in, 16)
    pool.dma_start(o.mask[:, :], a["masks"][:, C_GLA:C_GLA + P]).then_inc(o.s_in, 16)
    for c in range(NBLK):
        pool.wait_ge(o.s_o_inverse, 1 if c < NBLK - 1 else 2)
        if c >= 2:
            pool.wait_ge(o.s_diag_used, c - 1)
        pool.tensor_tensor(heads_view(o.diag[:, c % 2, :], P, P), over_heads(k.ident[:, :], P, P),
                           along(o.inverse[:, c], P, P), ALU.mult).then_inc(o.s_diag_set, 1)


def odd_tensor_between(core, pe, mix, s):
    k, o = core, core.odd
    ps, proj = k.psum, o.proj
    for h in GATE_AT.get(s, []):
        if h == 0:
            pe.wait_ge(k.scaled, mix.evac0 - ODD_TILES - 1 + s + 1)
            pe.wait_ge(o.s_in, 48)
        if h >= 3:
            pe.wait_ge(o.s_gate_x, h - 2)
        for b, (t0, n) in enumerate(halves(FULL)):
            op = pe.matmul(ps[:, 2 * (h % 3) + b, 0:n], o.gate_up[:, h * P:(h + 1) * P],
                           proj[0:RANK, GATE_LOW, t0:t0 + n], start=True, stop=True)
        op.then_inc(o.s_gate_lin, 1)
    for c in KEYS_AT.get(s, []):
        t0, n = BLOCKS[c]
        if c == 0:
            pe.wait_ge(o.s_k_dec, GH)
            pe.wait_ge(o.s_gate_x, GH)
        if c >= 2:
            pe.wait_ge(o.s_k_set, c - 1)
        for h in range(GH):
            op = pe.transpose(ps[0:n, c % 2, h * P:(h + 1) * P], proj[:, GK + h, t0:t0 + n], k.ident[:])
        op.then_inc(o.s_k_flip, 1)
        if c == 0:
            continue
        if c > 2:
            pe.wait_ge(o.s_attn_set, c - 2)
        for h in range(GH):
            op = pe.matmul(ps[:, 2 + c % 2, h * P:(h + 1) * P], o.k_grow[:, h, t0:t0 + n], proj[:, GQ + h, t0:t0 + n],
                           start=True, stop=True)
        op.then_inc(o.s_attn_made, 1)
    for c in VALUES_AT.get(s, []):
        t0, n = BLOCKS[c]
        if c:
            pe.wait_ge(o.s_v_set, c)
        else:
            pe.wait_ge(o.s_attn_set, NBLK)
        for j in range(2 * GH):
            op = pe.transpose(ps[0:n, 2 + j // 4, (j % 4) * P:(j % 4 + 1) * P], proj[:, GV + j, t0:t0 + n], k.ident[:])
        op.then_inc(o.s_v_flip, 1)
    for n_chunk in sorted(set(KV_AT.get(s, []) + OUT_AT.get(s, []))):
        c, r0, t0, n = CHUNKS[n_chunk]
        rows = slice(r0, r0 + n)
        pe.wait_ge(o.s_state, n_chunk)
        if n_chunk in KV_AT.get(s, []):
            pe.wait_ge(o.s_v_set, c + 1)
            pe.wait_ge(o.s_k_set, NBLK + 1)
            for h in range(GH):
                out = ps[:, h // 2, (h % 2) * VD:(h % 2 + 1) * VD]
                op = pe.matmul(out, o.k_rows(c)[rows, h, :], o.v_rows[rows, c, h * VD:(h + 1) * VD], start=True,
                               stop=True)
            op.then_inc(o.s_kv_made, 1)
        if n_chunk in OUT_AT.get(s, []):
            if n_chunk > 1:
                pe.wait_ge(o.s_o_set, n_chunk - 1)
            for j in range(2 * GH):
                h = j // 2
                out = ps[:, 4, j * CH:(j + 1) * CH]
                pe.matmul(out, o.state[:, n_chunk % 2, h, (j % 2) * P:(j % 2 + 1) * P], proj[:, GQ + h, t0:t0 + n],
                          start=True, stop=False)
                op = pe.matmul(out, o.v_rows[rows, c, j * P:(j + 1) * P], o.attn[rows, c - 1, h, r0:r0 + n],
                               start=False, stop=True)
            op.then_inc(o.s_o_made, 1)
            if n_chunk > 1:
                chunk_sums(k, o, pe, mix, n_chunk - 1)


def chunk_sums(k, o, pe, mix, n_chunk):
    c, r0, t0, n = CHUNKS[n_chunk]
    if n_chunk == EARLY_SUMS + 1:
        pe.wait_ge(k.scaled, mix.evac0)
    pe.wait_ge(o.s_o_sq, n_chunk)
    squares = k.t_up if n_chunk % 2 else k.t_gate
    for h in range(GH):
        at = (c - 1) * GH + h
        for j in range(2):
            first = (2 * h + j) * CH
            op = pe.matmul(k.psum[r0:r0 + n, 5 if c < NBLK else 6, at:at + 1], squares[:, first:first + CH],
                           k.ones[:, 0:1], start=j == 0, stop=j == 1)
    op.then_inc(o.s_o_sums, 1)


def odd_tensor(core, pe, mix):
    k, o = core, core.odd
    odd_tensor_between(k, pe, mix, ODD_LAST + 1)
    chunk_sums(k, o, pe, mix, len(CHUNKS) - 1)
    for c in range(NBLK):
        pe.wait_ge(o.s_diag_set, c + 1)
        if c >= 2:
            pe.wait_ge(o.s_o_normed, c - 1)
        pe.matmul(k.psum[:, 2 + c % 2, :], k.ones[:], o.diag[:, c % 2, :], start=True, stop=True)\
          .then_inc(o.s_diag_used, 1)


def chunk_ends(tile):
    return tile[:, META:TOK].rearrange("p (s t) -> p s t", t=CH)[:, :, CH - 1:CH]


def odd_scalar_between(core, act, mix, s):
    k, o = core, core.odd
    ps, proj = k.psum, o.proj
    for h in GATE_AT.get(s, []):
        act.wait_ge(o.s_gate_lin, h + 1)
        act.activation(token_cols(o.ex[:, h, :], FULL), bank_cols(k, h % 3, FULL), ACT.Identity,
                       bias=k.vec_cols[:, 48 + h:49 + h]).then_inc(o.s_gate_x, 1)
    for h in LOG_AT.get(s, []):
        u = o.ex[:, 4 + h % 2, :]
        act.wait_ge(o.s_gate_neg, h + 1)
        act.activation(u, u, ACT.Exp).then_inc(o.s_gate_exp, 1)
    for h in LOG_AT.get(s, []):
        u = o.ex[:, 4 + h % 2, :]
        act.wait_ge(o.s_gate_exp, h + 1)
        act.activation(u, u, ACT.Ln, bias=k.ones[:, 0:1]).then_inc(o.s_gate_log, 1)
    for h in GROW_AT.get(s, []):
        cum, scale = o.ex[:, h, :], 1.0 / NORM_GATE
        act.wait_ge(o.s_cum, h + 1)
        if h >= 2:
            act.wait_ge(o.s_q_dec, h - 1)
        act.activation((k.t_up if h % 2 else k.t_gate)[:, :], cum, ACT.Exp, scale=scale)
        act.activation(o.k_grow[:, h, :], cum, ACT.Exp, scale=-scale)
        act.activation(o.decay[:, h, 0:1], cum[:, META - 1:META], ACT.Exp, scale=scale)
        act.activation(o.decay[:, h, 1:].unsqueeze(2), chunk_ends(cum), ACT.Exp, scale=scale)
        act.wait_ge(o.s_kd_arg, h + 1)
        u = o.ex[:, 4 + h % 2, :]
        act.activation(u, u, ACT.Exp, scale=scale).then_inc(o.s_grown, 1)
    for c in KEYS_AT.get(s, []):
        n = BLOCKS[c][1]
        act.wait_ge(o.s_k_flip, c + 1)
        act.activation(o.k_rows(c), ps[0:n, c % 2, :].rearrange("p (h q) -> p h q", q=P), ACT.Copy)\
            .then_inc(o.s_k_set, 1)
    for c in VALUES_AT.get(s, []):
        n = BLOCKS[c][1]
        act.wait_ge(o.s_v_flip, c + 1)
        act.activation(o.v_rows[0:n, c, :].rearrange("p (b q) -> p b q", b=2), ps[0:n, 2:4, :], ACT.Copy)\
            .then_inc(o.s_v_set, 1)
    for n_chunk in OUT_AT.get(s, []):
        c, r0, t0, n = CHUNKS[n_chunk]
        act.wait_ge(o.s_o_made, n_chunk)
        if n_chunk > 2:
            act.wait_ge(o.s_o_sums, n_chunk - 2)
        src = ps[:, 4, :].rearrange("p (j t) -> p j t", t=CH)
        squares = (k.t_up if n_chunk % 2 else k.t_gate)[:, 0:2 * GH * CH].rearrange("p (j t) -> p j t", t=CH)
        act.activation(squares, src, ACT.Square).then_inc(o.s_o_sq, 1)
        act.activation(proj[:, GV:GV + 2 * GH, t0:t0 + n], src, ACT.Copy).then_inc(o.s_o_set, 1)
        if n_chunk == EARLY_SUMS + 1:
            early = (NBLK - 1) * GH
            act.wait_ge(o.s_o_sums, EARLY_SUMS)
            act.activation(o.roots[:, 0:early], ps[:, 5, 0:early], ACT.Sqrt, bias=k.eps[:, 0:1], scale=1.0 / VD)\
                .then_inc(o.s_o_roots, 1)
    for j in SILU_G_AT.get(s, []):
        act.wait_ge(k.scaled, mix.evac0 - ODD_TILES - 1 + GG + j + 2)
        g = proj[:, GG + j, META:TOK]
        act.activation(g, g, ACT.Silu).then_inc(o.s_g_silu, 1)


def odd_scalar(core, act, mix):
    k, o = core, core.odd
    proj = o.proj
    load_table(k, act, ACT.Sqrt)
    odd_scalar_between(k, act, mix, ODD_LAST + 1)
    early = (NBLK - 1) * GH
    act.wait_ge(o.s_o_sums, 2 * NBLK)
    act.activation(o.roots[:, early:], k.psum[:, 6, early:early + GH], ACT.Sqrt, bias=k.eps[:, 0:1], scale=1.0 / VD)\
        .then_inc(o.s_o_roots, 1)
    for kt in range(DT):
        act.wait_ge(o.s_o_full, kt + 1)
        act.activation(k.x_hl[:, 0, kt, META:TOK], proj[:, GV + kt, META:TOK], ACT.Copy).then_inc(k.x_hi, 1)


def odd_vector_between(core, dve, mix, s):
    k, o = core, core.odd
    ps, proj = k.psum, o.proj
    for h in MIN_AT.get(s, []):
        x, u = o.ex[:, h, :], o.ex[:, 4 + h % 2, :]
        dve.wait_ge(o.s_gate_log, h + 1)
        dve.scalar_tensor_tensor(x, x, 0.0, u, ALU.min, ALU.subtract).then_inc(o.s_gate_min, 1)
    for h in CUM_AT.get(s, []):
        x, u = o.ex[:, h, :], o.ex[:, 4 + h % 2, :]
        dve.wait_ge(o.s_in, 48)
        dve.wait_ge(o.s_gate_min, h + 1)
        dve.tensor_tensor_scan(x, o.keep[:, :], x, 0.0, ALU.mult, ALU.add).then_inc(o.s_cum, 1)
        dve.wait_ge(o.s_cum, h + 1)
        dve.tensor_tensor(u[:, 0:META], x[:, META - 1:META].broadcast_to([P, META]), x[:, 0:META], ALU.subtract)
        rest = u[:, META:TOK].rearrange("p (s t) -> p s t", t=CH)
        cum = x[:, META:TOK].rearrange("p (s t) -> p s t", t=CH)
        dve.tensor_tensor(rest, chunk_ends(x).broadcast_to([P, SEQ // CH, CH]), cum, ALU.subtract)\
            .then_inc(o.s_kd_arg, 1)
    for h in DECAY_AT.get(s, []):
        dve.wait_ge(o.s_grown, h + 1)
        q, key = proj[:, GQ + h, :], proj[:, GK + h, :]
        dve.scalar_tensor_tensor(q, q, float(P) ** -0.5, (k.t_up if h % 2 else k.t_gate)[:, :], ALU.mult, ALU.mult)\
            .then_inc(o.s_q_dec, 1)
        grow = o.k_grow[:, h, :]
        dve.tensor_tensor(grow, grow, key, ALU.mult).then_inc(o.s_k_grow, 1)
        dve.wait_ge(o.s_k_grow, h + 1)
        dve.tensor_tensor(key, key, o.ex[:, 4 + h % 2, :], ALU.mult).then_inc(o.s_k_dec, 1)
    for h in NEG_AT.get(s, []):
        x, u = o.ex[:, h, :], o.ex[:, 4 + h % 2, :]
        dve.wait_ge(o.s_gate_x, h + 1)
        if h >= 2:
            dve.wait_ge(o.s_k_dec, h - 1)
        dve.scalar_tensor_tensor(u, x, -1.0, x, ALU.mult, ALU.min).then_inc(o.s_gate_neg, 1)
    for c in KEYS_AT.get(s, []):
        if c:
            dve.wait_ge(o.s_attn_made, c)
            dve.tensor_tensor(o.attn[:, c - 1], heads_view(ps[:, 2 + c % 2, :], P, P), over_heads(o.mask[:, :], P, P),
                              ALU.mult).then_inc(o.s_attn_set, 1)
    for n_chunk in KV_AT.get(s, []):
        dve.wait_ge(o.s_kv_made, n_chunk + 1)
        to = o.state[:, (n_chunk + 1) % 2]
        if n_chunk == 0:
            dve.wait_ge(o.s_attn_set, NBLK)
            dve.tensor_copy(to.rearrange("p (b h) v -> p b (h v)", b=2), ps[:, 0:2, :]).then_inc(o.s_state, 1)
            continue
        if n_chunk >= 2:
            dve.wait_ge(o.s_o_made, n_chunk - 1)
        dve.wait_ge(o.s_state, n_chunk)
        for h in range(GH):
            op = dve.scalar_tensor_tensor(to[:, h], o.state[:, n_chunk % 2, h], o.decay[:, h, n_chunk:n_chunk + 1],
                                          ps[:, h // 2, (h % 2) * VD:(h % 2 + 1) * VD], ALU.mult, ALU.add)
        op.then_inc(o.s_state, 1)


def odd_vector(core, dve, mix):
    k, o = core, core.odd
    ps, proj = k.psum, o.proj
    early = (NBLK - 1) * GH
    dve.wait_ge(o.s_o_roots, 1)
    dve.reciprocal(o.inverse[:, 0:NBLK - 1], o.roots[:, 0:early].rearrange("p (c h) -> p c h", h=GH))\
       .then_inc(o.s_o_inverse, 1)
    for c in range(NBLK):
        if c == NBLK - 1:
            dve.wait_ge(o.s_o_roots, 2)
            dve.reciprocal(o.inverse[:, c], o.roots[:, early:]).then_inc(o.s_o_inverse, 1)
        dve.wait_ge(o.s_o_set, 2 * c + 2)
        dve.wait_ge(o.s_diag_used, c + 1)
        t0 = META + c * P
        out = proj[:, GV:GV + 2 * GH, t0:t0 + P].rearrange("p (h j) t -> p h j t", j=2)
        factor = heads_view(ps[:, 2 + c % 2, :], P, P).unsqueeze(2).broadcast_to([P, GH, 2, P])
        dve.tensor_tensor(out, out, factor, ALU.mult).then_inc(o.s_o_normed, 1)
    dve.wait_ge(o.s_o_normed, NBLK)
    dve.wait_ge(o.s_g_silu, 2 * GH)

    def gated(j):
        out = proj[:, GV + j, META:TOK]
        dve.scalar_tensor_tensor(out, out, k.vec_cols[:, 52 + j % 2:53 + j % 2], proj[:, GG + j, META:TOK], ALU.mult,
                                 ALU.mult).then_inc(o.s_o_full, 1)

    gated(0)
    for kt in range(DT):
        if kt + 1 < DT:
            gated(kt + 1)
        dve.wait_ge(k.x_hi, mix.x0 + kt + 1)
        dve.tensor_tensor(k.x_hl[:, 1, kt, META:TOK], proj[:, GV + kt, META:TOK],
                          k.x_hl[:, 0, kt, META:TOK].bitcast(F32), ALU.subtract).then_inc(k.x_lo, 1)


INPUTS = ["x", "meta_tokens", "norm_w", "ffn_w_gate", "ffn_w_up", "ffn_w_down", "rel_bias_table", "even_w_in",
          "even_conv_w", "swa_sinks", "dn_a_log", "dn_dt_bias", "dn_norm_w", "even_w_out", "odd_w_in",
          "gla_w_gate_up", "gla_b_gate", "gla_norm_w", "odd_w_out"]


def trunk(nc, a, stop=None):
    steps = linked(plan(stop))
    with ExitStack() as ctx:
        core = Core(nc, ctx, steps)
        block = ctx.enter_context(nc.Block())

        @block.sync
        def _(sp):
            sync_program(core, sp, a)

        @block.tensor
        def _(pe):
            tensor_program(core, pe)

        @block.scalar
        def _(act):
            scalar_program(core, act, a)

        @block.vector
        def _(dve):
            vector_program(core, dve)

        @block.gpsimd
        def _(pool):
            gpsimd_program(core, pool, a)


def kernel(**inputs):
    import concourse.bacc as bacc
    from concourse.bass_utils import run_bass_kernel_spmd

    nc = bacc.Bacc("TRN2", target_bir_lowering=False, num_devices=1)
    masks, hot, scan = shape_constants()
    arrays, args = {}, {}
    for name in INPUTS:
        arrays[name] = np.ascontiguousarray(inputs[name])
    arrays.update(masks=masks, bucket_hot=hot, scan_keep=scan)
    for name, array in arrays.items():
        args[name] = nc.dram_tensor(name, array.shape, mybir.dt.from_np(array.dtype), kind="ExternalInput").ap()
    args["bias_scratch"] = nc.dram_tensor("bias_scratch", (QH, V_ALL), F32, kind="Internal").ap()
    args["out"] = nc.dram_tensor("out", (1, SEQ, D), F32, kind="ExternalOutput").ap()
    trunk(nc, args)
    r = run_bass_kernel_spmd(nc, [arrays], core_ids=[0])
    return r.results[0]["out"]
```
